# Optimizing a Trainium2 kernel written in Bass

```python
import jax, jax.numpy as jnp
from jax import lax
import numpy as np

D_MODEL = 1024
BATCH = 1
SEQ = 128
DEPTH = 2
DEC_BATCH = 1
DEC_SEQ = 512
PAST_LEN = 128

GRID_W = 64
CHUNK = 128
N_EVEN = (DEPTH + 1) // 2
N_ODD = DEPTH // 2
N_SUB = 3
D_FF = 2816
EPS = 1e-6
ROPE_THETA = 10000.0
A_GROUPS = 4
A_DIM = 128
A_WIDTH = A_GROUPS * A_DIM
B_HEADS = 8
B_KV = 2
HEAD_DIM = 64
B_WIDTH = B_HEADS * HEAD_DIM
IN_EVEN = 2 * A_WIDTH + B_WIDTH + 2 * B_KV * HEAD_DIM
MIX_EVEN = A_WIDTH + B_WIDTH
EVEN_SPLITS = (A_WIDTH, 2 * A_WIDTH, 2 * A_WIDTH + B_WIDTH, 2 * A_WIDTH + B_WIDTH + B_KV * HEAD_DIM)
C_HEADS = 4
C_DK = 128
C_DV = 128
C_WIDTH = C_HEADS * C_DV
N_DIR = 2
N_GATES = N_DIR * 2 * C_HEADS
D_GROUPS = 4
D_DIM = 128
D_WIDTH = D_GROUPS * D_DIM
IN_ODD = 2 * C_HEADS * C_DK + 2 * C_WIDTH + N_GATES + D_WIDTH
MIX_ODD = C_WIDTH + D_WIDTH
ODD_SPLITS = (C_HEADS * C_DK, 2 * C_HEADS * C_DK, 2 * C_HEADS * C_DK + C_WIDTH,
              2 * C_HEADS * C_DK + 2 * C_WIDTH, 2 * C_HEADS * C_DK + 2 * C_WIDTH + N_GATES)

kernel_name = "hybrid_flow_trunk_ctx_prefix_step"

def _rmsnorm(x, gain):
    xf = x.astype(jnp.float32)
    y = xf * lax.rsqrt(jnp.mean(xf * xf, axis=-1, keepdims=True) + EPS)
    return (y * gain.astype(jnp.float32)).astype(x.dtype)

def _swiglu(h, w_in, w_out):
    g, u = jnp.split(h @ w_in, 2, axis=-1)
    return (jax.nn.silu(g) * u) @ w_out

def _grid_rope(n_tokens):
    rows = n_tokens // GRID_W
    r, cidx = jnp.meshgrid(jnp.arange(rows), jnp.arange(GRID_W), indexing="ij")
    r = r.reshape(-1).astype(jnp.float32)
    cidx = cidx.reshape(-1).astype(jnp.float32)
    n_freq = HEAD_DIM // 4
    inv = ROPE_THETA ** (-jnp.arange(n_freq, dtype=jnp.float32) / n_freq)
    ang = jnp.concatenate([r[:, None] * inv, cidx[:, None] * inv], axis=-1)
    ang = jnp.concatenate([ang, ang], axis=-1)
    return jnp.cos(ang), jnp.sin(ang)

def _apply_rope(x, cos, sin):
    xf = x.astype(jnp.float32)
    x1, x2 = jnp.split(xf, 2, axis=-1)
    rot = jnp.concatenate([-x2, x1], axis=-1)
    return (xf * cos[None, :, None, :] + rot * sin[None, :, None, :]).astype(x.dtype)

def _block_attention(q, k, v):
    bsz, t, h, hd = q.shape
    grp = h // B_KV
    nb = t // CHUNK
    qb = q.reshape(bsz, nb, CHUNK, B_KV, grp, hd).transpose(1, 0, 2, 3, 4, 5)
    scale = hd ** -0.5

    def one_block(qblk):
        s = jnp.einsum('bqkgd,bskd->bkgqs', qblk, k, preferred_element_type=jnp.float32) * scale
        p = jax.nn.softmax(s, axis=-1).astype(v.dtype)
        return jnp.einsum('bkgqs,bskd->bqkgd', p, v)

    out = lax.map(one_block, qb)
    return out.transpose(1, 0, 2, 3, 4, 5).reshape(bsz, t, h * hd)

def _chunk_mlp(u, vv, sgu_gain, w_s, b_s):
    bsz, t, _ = u.shape
    nc = t // CHUNK
    vg = _rmsnorm(vv.reshape(bsz, t, A_GROUPS, A_DIM), sgu_gain)
    vg = vg.reshape(bsz, nc, CHUNK, A_GROUPS, A_DIM)
    s = jnp.einsum('gpq,bnqgc->bnpgc', w_s, vg) + b_s.T[None, None, :, :, None]
    return u * s.reshape(bsz, t, A_WIDTH)

def _fourier(d):
    bsz, t, _ = d.shape
    dg = d.reshape(bsz, t, D_GROUPS, D_DIM).astype(jnp.float32)
    f = jnp.fft.fft2(dg, axes=(1, 3), norm="ortho").real
    return f.reshape(bsz, t, D_WIDTH).astype(d.dtype)

def _mlstm_chunkwise(q, k, v, i_pre, log_f, C0, n0, m0):
    bsz, t, h, _ = q.shape
    nc = t // CHUNK

    def chunks(a):
        return jnp.moveaxis(a.reshape((bsz, nc, CHUNK) + a.shape[2:]), 1, 0)

    causal = jnp.tril(jnp.ones((CHUNK, CHUNK), dtype=bool))

    def step(carry, xs):
        C, n, m = carry
        qc, kc, vc, ic, fc = xs
        b = jnp.cumsum(fc, axis=1).transpose(0, 2, 1)
        li = ic.transpose(0, 2, 1)
        log_d = jnp.where(causal, b[..., :, None] - b[..., None, :] + li[..., None, :], -jnp.inf)
        log_inter = b + m[..., None]
        m_t = jnp.maximum(log_inter, jnp.max(log_d, axis=-1))
        w_intra = jnp.exp(log_d - m_t[..., None])
        w_prev = jnp.exp(log_inter - m_t)
        a = w_intra * jnp.einsum('bthd,bshd->bhts', qc, kc)
        num = (jnp.einsum('bhts,bshe->bthe', a, vc)
               + w_prev.transpose(0, 2, 1)[..., None] * jnp.einsum('bhed,bthd->bthe', C, qc))
        den = a.sum(-1) + w_prev * jnp.einsum('bhd,bthd->bht', n, qc)
        denom = jnp.maximum(jnp.abs(den), jnp.exp(-m_t)).transpose(0, 2, 1)[..., None]
        hc = num / denom
        b_last = b[..., -1]
        log_s = b_last[..., None] - b + li
        m_new = jnp.maximum(b_last + m, jnp.max(log_s, axis=-1))
        w_s = jnp.exp(log_s - m_new[..., None])
        w_p = jnp.exp(b_last + m - m_new)
        C_new = w_p[..., None, None] * C + jnp.einsum('bhs,bshe,bshd->bhed', w_s, vc, kc)
        n_new = w_p[..., None] * n + jnp.einsum('bhs,bshd->bhd', w_s, kc)
        return (C_new, n_new, m_new), hc

    (C, n, m), hs = lax.scan(step, (C0, n0, m0),
                             (chunks(q), chunks(k), chunks(v), chunks(i_pre), chunks(log_f)))
    hs = jnp.moveaxis(hs, 0, 1).reshape(bsz, t, h, v.shape[-1])
    return hs, (C, n, m)

def _even_mixer(h, w_in, w_out, w_s, b_s, sgu_gain, q_gain, k_gain, rope, ctx_kv):
    bsz, t, _ = h.shape
    a_u, a_v, q, k, v = jnp.split(h @ w_in, EVEN_SPLITS, axis=-1)
    out_a = _chunk_mlp(jax.nn.gelu(a_u), jax.nn.gelu(a_v), sgu_gain, w_s, b_s)
    q = _rmsnorm(q.reshape(bsz, t, B_HEADS, HEAD_DIM), q_gain)
    k = _rmsnorm(k.reshape(bsz, t, B_KV, HEAD_DIM), k_gain)
    v = v.reshape(bsz, t, B_KV, HEAD_DIM)
    if ctx_kv is None:
        keys, vals = k, v
        new_ctx = (k, v)
    else:
        cos, sin = rope
        q = _apply_rope(q, cos, sin)
        keys = jnp.concatenate([ctx_kv[0].astype(k.dtype), _apply_rope(k, cos, sin)], axis=1)
        vals = jnp.concatenate([ctx_kv[1].astype(v.dtype), v], axis=1)
        new_ctx = None
    out_b = _block_attention(q, keys, vals)
    return jnp.concatenate([out_a, out_b], axis=-1) @ w_out, new_ctx

def _odd_mixer(h, w_in, b_gate, w_out, ctx_state):
    bsz, t, _ = h.shape
    q, k, v, o, g, d = jnp.split(h @ w_in, ODD_SPLITS, axis=-1)
    q = q.reshape(bsz, t, C_HEADS, C_DK).astype(jnp.float32)
    k = k.reshape(bsz, t, C_HEADS, C_DK).astype(jnp.float32) * (C_DK ** -0.5)
    v = v.reshape(bsz, t, C_HEADS, C_DV).astype(jnp.float32)
    g = g.astype(jnp.float32).reshape(bsz, t, N_DIR, 2, C_HEADS) + b_gate.astype(jnp.float32)
    i_pre = g[:, :, :, 0]
    log_f = jax.nn.log_sigmoid(g[:, :, :, 1])
    if ctx_state is None:
        C0 = jnp.zeros((bsz, N_DIR, C_HEADS, C_DV, C_DK), jnp.float32)
        n0 = jnp.zeros((bsz, N_DIR, C_HEADS, C_DK), jnp.float32)
        m0 = jnp.zeros((bsz, N_DIR, C_HEADS), jnp.float32)
    else:
        C0, n0, m0 = (s.astype(jnp.float32) for s in ctx_state)
    h_f, (Cf, nf, mf) = _mlstm_chunkwise(q, k, v, i_pre[:, :, 0], log_f[:, :, 0], C0[:, 0], n0[:, 0], m0[:, 0])
    rev = lambda a: a[:, ::-1]
    h_b, (Cb, nb, mb) = _mlstm_chunkwise(rev(q), rev(k), rev(v), rev(i_pre[:, :, 1]), rev(log_f[:, :, 1]),
                                         C0[:, 1], n0[:, 1], m0[:, 1])
    h_b = rev(h_b)
    out_c = (jax.nn.sigmoid(o.astype(jnp.float32)) * (h_f + h_b).reshape(bsz, t, C_WIDTH)).astype(h.dtype)
    out_d = _fourier(d)
    out = jnp.concatenate([out_c, out_d], axis=-1) @ w_out
    new_state = (jnp.stack([Cf, Cb], axis=1), jnp.stack([nf, nb], axis=1), jnp.stack([mf, mb], axis=1))
    return out, new_state

def setup_inputs(seed: int = 0) -> dict:
    key = jax.random.key(seed)
    ks = jax.random.split(key, 24)
    nrm = lambda kk, shape, s=1.0: jax.random.normal(kk, shape, jnp.float32) * s
    gate_offset = jnp.array([0.0, 3.0], jnp.float32)[:, None]
    return {
        "x_prompt": nrm(ks[0], (BATCH, SEQ, D_MODEL)),
        "x_sample": nrm(ks[1], (DEC_BATCH, DEC_SEQ, D_MODEL)),
        "c": nrm(ks[2], (DEC_BATCH, D_MODEL)),
        "cache_k": nrm(ks[3], (DEC_BATCH, N_EVEN, PAST_LEN, B_KV, HEAD_DIM)),
        "cache_v": nrm(ks[4], (DEC_BATCH, N_EVEN, PAST_LEN, B_KV, HEAD_DIM)),
        "state_C": nrm(ks[5], (DEC_BATCH, N_ODD, N_DIR, C_HEADS, C_DV, C_DK)),
        "state_n": nrm(ks[6], (DEC_BATCH, N_ODD, N_DIR, C_HEADS, C_DK)),
        "state_m": nrm(ks[7], (DEC_BATCH, N_ODD, N_DIR, C_HEADS), 0.1),
        "c_ctx": nrm(ks[8], (D_MODEL,)),
        "norm_gain": 1.0 + nrm(ks[9], (DEPTH, N_SUB, D_MODEL), 0.02),
        "w_mod": nrm(ks[10], (DEPTH, D_MODEL, 3 * N_SUB * D_MODEL), 0.5 * D_MODEL ** -0.5),
        "b_mod": nrm(ks[11], (DEPTH, 3 * N_SUB * D_MODEL), 0.02),
        "ffn_w_in": nrm(ks[12], (DEPTH, 2, D_MODEL, 2 * D_FF), D_MODEL ** -0.5),
        "ffn_w_out": nrm(ks[13], (DEPTH, 2, D_FF, D_MODEL), D_FF ** -0.5),
        "w_in_even": nrm(ks[14], (N_EVEN, D_MODEL, IN_EVEN), D_MODEL ** -0.5),
        "w_out_even": nrm(ks[15], (N_EVEN, MIX_EVEN, D_MODEL), MIX_EVEN ** -0.5),
        "spatial_w": nrm(ks[16], (N_EVEN, A_GROUPS, CHUNK, CHUNK), CHUNK ** -0.5),
        "spatial_b": 1.0 + nrm(ks[17], (N_EVEN, A_GROUPS, CHUNK), 0.02),
        "sgu_gain": 1.0 + nrm(ks[18], (N_EVEN, A_GROUPS, A_DIM), 0.02),
        "q_gain": 1.0 + nrm(ks[19], (N_EVEN, HEAD_DIM), 0.02),
        "k_gain": 1.0 + nrm(ks[20], (N_EVEN, HEAD_DIM), 0.02),
        "w_in_odd": nrm(ks[21], (N_ODD, D_MODEL, IN_ODD), D_MODEL ** -0.5),
        "b_gate_odd": gate_offset + nrm(ks[22], (N_ODD, N_DIR, 2, C_HEADS), 0.1),
        "w_out_odd": nrm(ks[23], (N_ODD, MIX_ODD, D_MODEL), MIX_ODD ** -0.5),
    }

def reference(x_prompt, x_sample, c, cache_k, cache_v, state_C, state_n, state_m, c_ctx,
              norm_gain, w_mod, b_mod, ffn_w_in, ffn_w_out,
              w_in_even, w_out_even, spatial_w, spatial_b, sgu_gain, q_gain, k_gain,
              w_in_odd, b_gate_odd, w_out_odd):

    def layer(l, x, mod, rope, ctx):
        g = norm_gain[l]

        def modulated(j, y):
            return _rmsnorm(y, g[j]) * (1 + mod[:, :, 3 * j + 1]) + mod[:, :, 3 * j]

        x = x + 0.5 * mod[:, :, 2] * _swiglu(modulated(0, x), ffn_w_in[l, 0], ffn_w_out[l, 0])
        h = modulated(1, x)
        e = l // 2
        if l % 2 == 0:
            out, new_ctx = _even_mixer(h, w_in_even[e], w_out_even[e], spatial_w[e], spatial_b[e],
                                       sgu_gain[e], q_gain[e], k_gain[e], rope, ctx)
        else:
            out, new_ctx = _odd_mixer(h, w_in_odd[e], b_gate_odd[e], w_out_odd[e], ctx)
        x = x + mod[:, :, 5] * out
        x = x + 0.5 * mod[:, :, 8] * _swiglu(modulated(2, x), ffn_w_in[l, 1], ffn_w_out[l, 1])
        return x, new_ctx

    x = x_prompt
    ks_, vs_, Cs_, ns_, ms_ = [], [], [], [], []
    for l in range(DEPTH):
        mod = (jax.nn.silu(c_ctx) @ w_mod[l] + b_mod[l]).reshape(1, 1, 3 * N_SUB, D_MODEL)
        x, st = layer(l, x, mod, None, None)
        if l % 2 == 0:
            ks_.append(st[0])
            vs_.append(st[1])
        else:
            Cs_.append(st[0])
            ns_.append(st[1])
            ms_.append(st[2])
    y_prompt = x
    new_cache_k = jnp.stack(ks_, axis=1)
    new_cache_v = jnp.stack(vs_, axis=1)
    new_state_C = jnp.stack(Cs_, axis=1)
    new_state_n = jnp.stack(ns_, axis=1)
    new_state_m = jnp.stack(ms_, axis=1)

    xs = x_sample
    rope = _grid_rope(xs.shape[1])
    for l in range(DEPTH):
        mod = (jax.nn.silu(c) @ w_mod[l] + b_mod[l]).reshape(xs.shape[0], 1, 3 * N_SUB, D_MODEL)
        e = l // 2
        if l % 2 == 0:
            ctx = (cache_k[:, e], cache_v[:, e])
        else:
            ctx = (state_C[:, e], state_n[:, e], state_m[:, e])
        xs, _ = layer(l, xs, mod, rope, ctx)
    y_sample = xs

    return (y_prompt, y_sample, new_cache_k, new_cache_v, new_state_C, new_state_n, new_state_m)


_drawn_inputs = setup_inputs


def setup_inputs(seed=0):
    import zlib

    import numpy as np

    out = dict(_drawn_inputs(seed))
    spreads = {}
    factors = {'cache_k': 2.673,
     'state_m': 2.911,
     'spatial_b': 4.989,
     'sgu_gain': 4.485,
     'q_gain': 8.0,
     'k_gain': 2.921}
    for name, (base, spread) in spreads.items():
        noise = np.random.default_rng([zlib.crc32(name.encode()), seed]).standard_normal(out[name].shape)
        drawn = base * np.exp(spread * noise) if base else spread * noise
        out[name] = __import__('jax').numpy.asarray(drawn.astype(out[name].dtype))
    for name, factor in factors.items():
        out[name] = (out[name] * factor).astype(out[name].dtype)
    return out
```

```python
import concourse.bass as bass
from concourse import mybir
from contextlib import ExitStack
import numpy as np

F32 = mybir.dt.float32
F32R = mybir.dt.float32r
ALU = mybir.AluOpType
ACT = mybir.ActivationFunctionType
AX = mybir.AxisListType

P = 128
D = 1024
KT = D // P
T_CTX = 128
T_LAT = 512
T = T_CTX + T_LAT
TT = T // P
HALF = T // 2
DEPTH = 2
C_HEADS, C_DK, C_DV = 4, 128, 128
C_WIDTH = C_HEADS * C_DV
D_GROUPS, D_DIM = 4, 128
A_GROUPS, A_DIM = 4, 128
A_WIDTH = A_GROUPS * A_DIM
B_HEADS, B_KV, HEAD_DIM = 8, 2, 64
B_WIDTH = B_HEADS * HEAD_DIM
GRID_W, ROPE_THETA = 64, 10000.0
N_SUB = 3
D_FF = 2816
FT = D_FF // P
CHUNK_TILES = (12, 10)
FFN_UNITS = FT + 2 * KT
MIX_EVEN_UNITS = 12
MIX_ODD_UNITS = 14
EPS = 1e-6
N_MOD = 3 * N_SUB * D
MOD_COLS = 512
MOD_TILES = MOD_COLS // P
MOD_PE_BLOCKS = 4
MOD_BLOCKS = DEPTH * N_MOD // MOD_COLS - MOD_PE_BLOCKS
MC = DEPTH * N_MOD // P

FFN_AT = (0, FFN_UNITS + MIX_EVEN_UNITS, 2 * FFN_UNITS + MIX_EVEN_UNITS,
          3 * FFN_UNITS + MIX_EVEN_UNITS + MIX_ODD_UNITS)
EVEN_AT = FFN_UNITS
ODD_AT = 3 * FFN_UNITS + MIX_EVEN_UNITS


def trunk(nc, a, out, mixers=True):
    with ExitStack() as ctx:
        sems = {}

        def sem(name):
            sems[name] = ctx.enter_context(nc.semaphore(name))
            return sems[name]

        arena = [-(-nc.sbuf_base // 64) * 64]

        def place(name, shape, dtype=F32, at=None):
            size = int(np.prod(shape[1:])) * 4
            if at is None:
                at, arena[0] = arena[0], arena[0] + -(-size // 32) * 32
                assert arena[0] <= nc.sbuf_usable_end, (name, arena[0])
            t = nc.alloc_sbuf_tensor_at(name, shape, dtype, offset=at)
            place.at[name] = at
            return t
        place.at = {}

        x = place("x", [P, KT, T])
        h_hi = place("h_hi", [P, KT, T], F32R)
        h_lo = place("h_lo", [P, KT, T], F32R)
        hid_hi = place("hid_hi", [P, CHUNK_TILES[0], T], F32R)
        hid_lo = place("hid_lo", [P, CHUNK_TILES[0], T], F32R)
        w_raw = place("w_raw", [P, 2 * 16 * P])
        w_hi = place("w_hi", [P, 2, 16, P], F32R)
        w_lo = place("w_lo", [P, 2, 16, P], F32R)
        mod_raw = place("mod_raw", [P, KT, MOD_COLS])
        mod_acc = place("mod_acc", [P, 2, MOD_COLS])
        mod = place("mod", [P, 2, MC])
        mod_add = place("mod_add", [P, MC])
        mod_mul = place("mod_mul", [P, MC])
        mod_tmp = place("mod_tmp", [P, 2, MOD_TILES])
        silu_c = place("silu_c", [P, KT, 2])
        rows_t = place("rows_t", [P, 72])
        ident = place("ident", [P, P])
        ones = place("ones", [P, P])
        eps = place("eps", [P, 1])
        work_a = place("work_a", [P, 2, T])
        work_b = place("work_b", [P, 2, T])
        ss = place("ss", [P, T])

        x_rows = place("x_rows", [P, TT, D], at=place.at["h_hi"])
        y_rows = place("y_rows", [P, TT, D], at=place.at["h_hi"])
        mod_first = [place(f"mod_first{r}", [P, KT, MOD_COLS], at=place.at["hid_hi"] + r * KT * MOD_COLS * 4)
                     for r in range(3)] + [mod_raw]
        small_rows = place("small_rows", [P, 3, P], at=place.at["w_hi"])

        bank2 = [ctx.enter_context(nc.psum_tensor(f"banks{2 * i}_{2 * i + 1}", [P, 2, 512], F32)) for i in range(4)]
        bank = [bank2[i // 2][:, i % 2, :] for i in range(8)]
        MODB, SUMS = 4, (6, 7)

        consts_in = sem("consts_in")
        rows_in = sem("rows_in")
        rows_turned = sem("rows_turned")
        rows_kept = sem("rows_kept")
        silu_ready = sem("silu_ready")
        ones_set = sem("ones_set")
        x_in = sem("x_in")
        x_turned = sem("x_turned")
        x_kept_act = sem("x_kept_act")
        x_kept_dve = sem("x_kept_dve")
        mod_first_in = [sem(f"mod_first_in{r}") for r in range(MOD_PE_BLOCKS)]
        mod_first_sum = sem("mod_first_sum")
        mod_in = sem("mod_in")
        mod_summed = sem("mod_summed")
        mod_turned = sem("mod_turned")
        raw_in = sem("raw_in")
        hi_ready = sem("hi_ready")
        lo_ready = sem("lo_ready")
        w_used = sem("w_used")
        g_ready = sem("g_ready")
        silu_done = sem("silu_done")
        prod_done = sem("prod_done")
        hid_hi_done = sem("hid_hi_done")
        hid_lo_done = sem("hid_lo_done")
        out_ready = sem("out_ready")
        x_updated = sem("x_updated")
        squared = sem("squared")
        square_added = sem("square_added")
        sums_ready = sem("sums_ready")
        rms_ready = sem("rms_ready")
        xn_ready = sem("xn_ready")
        h_ready = sem("h_ready")
        h_hi_ready = sem("h_hi_ready")
        h_lo_ready = sem("h_lo_ready")
        dve_chain = sem("dve_chain")
        y_turned = sem("y_turned")
        y_kept_act = sem("y_kept_act")
        y_kept_dve = sem("y_kept_dve")
        stored = sem("stored")

        HD, NH, NKV = HEAD_DIM, B_HEADS, B_KV
        KEY_TILES = TT + 1
        q_tok = place("q_tok", [P, TT, NH * HD], at=place.at["hid_hi"] + KT * T * 4)
        v_gate = place("v_gate", [P, TT, A_WIDTH], at=place.at["hid_lo"] + KT * T * 4)
        u_gate = place("u_gate", [P, A_GROUPS, T], at=place.at["work_a"])
        o = place.at["mod_raw"]
        k_tok = place("k_tok", [P, KEY_TILES, NKV, 2, HD], at=o)
        v_tok = place("v_tok", [P, KEY_TILES, NKV * HD], at=o + 6144)
        spatial_t = place("spatial_t", [P, A_GROUPS, P], at=o + 9216)
        spatial_bias = place("spatial_bias", [P, A_GROUPS, P], at=o + 11264)
        rope = place("rope", [P, 2, T_LAT // P, HD], at=o + 13312)
        qk_gain = place("qk_gain", [P, 2, HD], at=o + 15360)
        assert 15872 <= KT * MOD_COLS * 4
        spatial_raw = place("spatial_raw", [P, A_GROUPS, P], at=place.at["hid_hi"])
        q_feat = place("q_feat", [P, NH // 2, T], at=place.at["h_hi"])
        k_feat = place("k_feat", [P, NKV, KEY_TILES * P], at=place.at["h_hi"] + 10240)
        prob = place("prob", [P, 2, T], at=place.at["h_lo"])
        prob_t = place("prob_t", [P, 2, T], at=place.at["h_lo"] + 5120)
        rot = place("rot", [P, T])
        stat = place("stat", [P, TT * (NH + NKV) + TT * A_GROUPS])
        soft = place("soft", [P, 3, 4])

        tok_in = sem("tok_in")
        tok_ready = sem("tok_ready")
        tok_kept_dve = sem("tok_kept_dve")
        tok_kept_act = sem("tok_kept_act")
        u_gate_ready = sem("u_gate_ready")
        u_gate_kept = sem("u_gate_kept")
        stat_ready = sem("stat_ready")
        root_ready = sem("root_ready")
        qk_done = sem("qk_done")
        turned = sem("turned")
        turn_kept_act = sem("turn_kept_act")
        turn_kept_dve = sem("turn_kept_dve")
        spatial_ready = sem("spatial_ready")
        spatial_gated = sem("spatial_gated")
        spatial_hi = sem("spatial_hi")
        mix_done = sem("mix_done")
        scores_ready = sem("scores_ready")
        max_ready = sem("max_ready")
        exp_done = sem("exp_done")
        prob_ready = sem("prob_ready")
        prob_turned = sem("prob_turned")
        prob_kept = sem("prob_kept")
        att_ready = sem("att_ready")
        att_hi = sem("att_hi")
        cache_stored = sem("cache_stored")

        EU = EVEN_AT
        N_TOK_UNITS = 5
        N_ATT = TT * NH

        def att_keys(i):
            return (0, 1) if i // NH == 0 else (1, KEY_TILES)
        def turned_out(copy, n, *more):
            if n < 4:
                dst = k_feat[:, :, 2 * (n - 1) * P:2 * n * P].rearrange("p g (t k) -> p t g k", t=2)
                src = bank[n % 4][:, :].rearrange("p (t g k) -> p t g k", t=2, g=2)
            else:
                dst = q_feat[:, :, (n - 4) * P:(n - 3) * P]
                src = bank[n % 4][:, :].rearrange("p (j t) -> p j t", j=4)
            return copy(dst, src, *more)


        def fill_ready(eng, base, r):
            u, t = divmod(r, TT)
            if t == TT - 1:
                eng.wait_ge(w_used, base + u + 1)
            else:
                eng.wait_ge(tok_ready, (TT - 1) * (tok_units_before(base) + u) + t + 1)

        def tok_units_before(base):
            return 0 if base == EU else N_TOK_UNITS

        def u_tile_ready(eng, m):
            if m == 0:
                eng.wait_ge(u_gate_ready, 1)
            else:
                eng.wait_ge(w_used, EU + N_TOK_UNITS + m)


        OU = ODD_AT
        CH, DK = C_HEADS, C_DK
        GR = 2 * 32
        q_f = place("q_f", [P, CH, T], at=place.at["q_tok"])
        k_f = place("k_f", [P, CH, T], at=place.at["v_gate"])
        v_t = place("v_t", [P, TT, CH * C_DV], at=place.at["mod_raw"])
        o_f = place("o_f", [P, CH, T], at=place.at["mod_raw"] + 10240)
        d_f = place("d_f", [P, D_GROUPS, T], at=place.at["work_a"])
        hh, hl = place.at["hid_hi"], place.at["hid_lo"]
        state = place("state", [P, 2, CH, 2 * P], at=hh)
        gate_bias = place("gate_bias", [P, 16], at=hh + 8192)
        m_start = place("m_start", [P, GR], at=hh + 8256)
        m_end = place("m_end", [P, 2, CH], at=hh + 8512)
        m_given = place("m_given", [P, 2, CH], at=hh + 8544)
        n_end = place("n_end", [P, 2, CH], at=hh + 8576)
        masks = place("masks", [P, 4, P], at=hl)
        gate_raw = place("gate_raw", [P, KT, 16], at=hl + 2048)
        gate_hi = place("gate_hi", [P, KT, 16], F32R, at=hl + 2560)
        gate_lo = place("gate_lo", [P, KT, 16], F32R, at=hl + 3072)
        gates = place("gates", [P, TT, 16], at=hl + 3584)
        gate_abs = place("gate_abs", [P, TT, 2, CH], at=hl + 3904)
        log_f = place("log_f", [P, GR], at=hl + 4096)
        ab = place("ab", [P, 2, GR], at=hl + 4352)
        a_rows = place("a_rows", [GR, P], at=hl + 4864)
        b_rows = place("b_rows", [GR, P], at=hl + 5376)
        c_rows = place("c_rows", [GR, P], at=hl + 5888)
        m_rows = place("m_rows", [GR, 2, P], at=hl + 6400)
        a_max = place("a_max", [GR, P], at=hl + 7424)
        n_col = place("n_col", [P, 2, CH], at=hl + 7936)
        dft_t = place("dft_t", [P, 2, T_LAT // P, T_LAT], at=place.at["h_lo"])
        dft_c = place("dft_c", [P, 3, P], at=place.at["h_lo"] + 16384)
        uv = place("uv", [P, TT, D_GROUPS, 2 * P], at=place.at["h_hi"])
        a0 = place.at["h_hi"]
        k_t = place("k_t", [P, TT, CH * DK], at=a0)
        w_in_ = place("w_intra", [P, 2, CH, P], at=a0 + 10240)
        w_pr = place("w_prev", [P, 2, CH, P], at=a0 + 14336)
        a0 = place.at["h_lo"]
        e_m = place("e_m", [P, 2, CH * P], at=a0)
        a_t = place("a_t", [P, 2, CH * P], at=a0 + 4096)
        q_w = place("q_w", [P, 2, CH, P], at=a0 + 8192)
        v_w = place("v_w", [P, 2, CH, 2 * P], at=a0 + 12288)
        c_end = [place("c_end0", [P, CH, P], at=place.at["h_hi"] + 18432),
                 place("c_end1", [P, CH, P], at=hl + 8192)]
        h_sum = place("h_sum", [P, CH, T], at=place.at["work_a"])
        den = place("den", [P, CH * P], at=place.at["rot"])

        odd_in = sem("odd_in")
        gate_w_in = sem("gate_w_in")
        gate_w_hi = sem("gate_w_hi")
        gate_pe = sem("gate_pe")
        gate_dve = sem("gate_dve")
        gate_act = sem("gate_act")
        tile_ready = sem("tile_ready")
        tile_kept_act = sem("tile_kept_act")
        tile_kept_dve = sem("tile_kept_dve")
        dft_in = sem("dft_in")
        uv_ready = sem("uv_ready")
        uv_kept_act = sem("uv_kept_act")
        uv_kept_dve = sem("uv_kept_dve")
        four_ready = sem("four_ready")
        four_hi = sem("four_hi")
        four_lo = sem("four_lo")
        k_turned = sem("k_turned")
        k_kept = sem("k_kept")
        state_kept = sem("state_kept")
        end_kept = sem("end_kept")
        bcast_ready = sem("bcast_ready")
        x_ready = sem("x_ready")
        exps_done = sem("exps_done")
        qk_ready = sem("qk_ready")
        a_ready = sem("a_ready")
        v_ready = sem("v_ready")
        nd_ready = sem("nd_ready")
        st_ready = sem("st_ready")
        h_done = sem("h_done")
        st_taken = sem("st_taken")
        gate_dve_abs = sem("gate_dve_abs")
        h_final = sem("h_final")
        c_hi = sem("c_hi")
        c_lo = sem("c_lo")
        state_stored = sem("state_stored")

        GROUPS = [(0, 0), (0, 1)]
        for i in range(TT - 1):
            GROUPS += [(1 + i, 0), (TT - 1 - i, 1)]
        NG = len(GROUPS)
        SEEN = [sum(g[0] == t for g in GROUPS[:n]) for n, (t, _) in enumerate(GROUPS)]
        STATE_GROUPS = [n for n in range(NG) if n < NG - 2]

        def row_of(t, d, h=0):
            return d * 32 + t * CH + h

        def col_view(tile, d, t):
            return tile[:, row_of(t, d):row_of(t, d) + CH]

        def odd_tile_ready(eng, f):
            unit = (0, 2, 6, 8)[f // 4] + f % 4 // 2
            if f % 2 == 0:
                eng.wait_ge(tile_ready, f // 2 + 1)
            else:
                eng.wait_ge(w_used, OU + unit + 1)

        block = ctx.enter_context(nc.Block())

        class Count:

            def __init__(self, eng, s):
                self.eng, self.s, self.base, self.n = eng, s, 0, 0

            def inc(self, ins):
                self.n += 1
                return ins.then_inc(self.s, 1)

            def wait(self, back=0):
                self.eng.wait_ge(self.s, self.base + (self.n - back))

        A_IN, B_IN = CHUNK_TILES
        A_OUT = A_IN + KT
        assert FFN_UNITS == A_OUT + B_IN + KT
        B_OUT = A_OUT + B_IN

        def halves():
            return [(0, slice(0, HALF)), (1, slice(HALF, T))]

        norm_at = (0, 2, 3, 5) if mixers else (0, 1, 2, 3)
        norm_kind = (0, 1, 2, 3, 4, 5) if mixers else (0, 2, 3, 5)
        FFN_AT = tuple(f * FFN_UNITS + (f > 0) * mixers * MIX_EVEN_UNITS + (f > 2) * mixers * MIX_ODD_UNITS for f in range(4))

        def out_base(f):
            return 2 * KT * f + mixers * KT * ((f > 0) + (f > 2))

        PARTS = ((0, slice(0, T_CTX)), (1, slice(T_CTX, T)))
        PIECES = ((0, 0, slice(0, T_CTX), slice(0, T_CTX)),
                  (0, 1, slice(T_CTX, HALF), slice(T_CTX, HALF)),
                  (1, 1, slice(HALF, T), slice(0, HALF)))

        def mod_col(v, layer, kind, kt):
            return mod[:, v, bass.ds((layer * 3 * N_SUB + kind) * KT + kt, 1)]

        def raw_view(kind, slot):
            if kind == "mix":
                return w_raw[:, :].rearrange("p (s n c) -> p s n c", s=2, c=P)[:, slot]
            if kind == "one":
                return w_raw[:, :].rearrange("p (s n c) -> p s n c", s=2, c=2 * P)[:, slot, :, 0:P]
            n = {"in": 16, "outA": CHUNK_TILES[0], "outB": CHUNK_TILES[1]}[kind]
            return w_raw[:, :].rearrange("p (n c) -> p n c", c=2 * P)[:, 0:n, slot * P:(slot + 1) * P]

        def split_view(w, kind, slot):
            if kind == "one":
                return w[:, slot].rearrange("p (k c) q -> p k c q", c=2)[:, :, 0, :]
            return w[:, slot, 0:{"in": 16, "mix": 16, "outA": CHUNK_TILES[0], "outB": CHUNK_TILES[1]}[kind], :]

        @block.sync
        def _(sp):
            w_in = a["ffn_w_in"].rearrange("l h (k p) n -> l h p k n", p=P)
            w_out = a["ffn_w_out"].rearrange("l h (k p) n -> l h p k n", p=P)
            w_mod = a["w_mod"].rearrange("l (k p) n -> l p k n", p=P)

            def load_pair(f, kind, pair, which):
                if not (isinstance(pair, int) and pair == 0):
                    sp.wait_ge(lo_ready, 2 * pair)
                l, h = divmod(f, 2)
                if kind == "in":
                    dst = w_raw[:, :].rearrange("p (k g c) -> p k g c", k=KT, g=2)
                    for g in range(2):
                        sp.dma_start(dst[:, :, g, :], w_in[l, h][:, :, bass.ts(which + g * (FT // 2), 2 * P)])\
                            .then_inc(raw_in, 16)
                else:
                    k0, n = (0, A_IN) if kind == "outA" else (A_IN, B_IN)
                    dst = w_raw[:, :].rearrange("p (k c) -> p k c", c=2 * P)
                    for i in range(2):
                        ks = slice(i * n // 2, (i + 1) * n // 2)
                        src = w_out[l, h][:, k0 + ks.start:k0 + ks.stop, bass.ts(which, 2 * P)]
                        sp.dma_start(dst[:, ks, :], src).then_inc(raw_in, 16)

            def load_mod(b):
                if isinstance(b, int) and b == 0:
                    sp.wait_ge(mod_first_sum, 1)
                else:
                    sp.wait_ge(mod_summed, b)
                lay = load_mod.layer
                cols = b + (MOD_PE_BLOCKS - lay * (N_MOD // MOD_COLS))
                sp.dma_start(mod_raw[:, :, :], w_mod[lay][:, :, bass.ts(cols, MOD_COLS)]).then_inc(mod_in, 16)

            def ffn(f):
                U = FFN_AT[f] // 2
                blk = ffn.block

                def run(first, last, kind, origin):
                    turns = (last - first) // 2
                    load_mod.layer = (blk[0] + MOD_PE_BLOCKS) // (N_MOD // MOD_COLS)
                    with sp.Fori(0, turns) as t:
                        load_pair(f, kind, U + first // 2 + t, t + (first - origin[0]) // 2 + origin[1])
                        if f < 2:
                            load_mod(t + blk[0])
                    if f < 2:
                        blk[0] += turns
                run(2, A_IN, "in", (0, 0))
                load_pair(f, "outA", U + A_IN // 2, 0)
                run(A_IN + 2, A_OUT, "outA", (A_IN, 0))
                load_pair(f, "in", U + A_OUT // 2, A_IN // 2)
                run(A_OUT + 2, B_OUT, "in", (A_OUT, A_IN // 2))
                load_pair(f, "outB", U + B_OUT // 2, 0)
                run(B_OUT + 2, FFN_UNITS, "outB", (B_OUT, 0))
            ffn.block = [2]

            def load_mix(unit, w, kts, cols):
                if unit % 2 == 0:
                    sp.wait_ge(lo_ready, unit)
                dst = w_raw[:, unit % 2 * 16 * P:(unit % 2 + 1) * 16 * P].rearrange("p (k c) -> p k c", c=2 * P)
                sp.dma_start(dst[:, 0:kts, 0:cols.stop - cols.start], w[:, :, cols]).then_inc(raw_in, 16)

            def even_sp():
                w = a["w_in_even"][0].rearrange("(k p) n -> p k n", p=P)
                wo = a["w_out_even"][0].rearrange("(k p) n -> p k n", p=P)
                AV, Q, K = A_WIDTH, 2 * A_WIDTH, 2 * A_WIDTH + B_WIDTH
                starts = [(K, 256), (Q, 256), (Q + 256, 256), (AV, 256), (AV + 256, 256), (0, 256), (256, P), (384, P)]
                sp.wait_ge(mod_summed, 17)
                sp.dma_start(k_tok[:, 1, :, 0, :], a["cache_k"][0, 0]).then_inc(tok_in, 16)
                sp.dma_start(v_tok[:, 1, :], a["cache_v"][0, 0].rearrange("t h d -> t (h d)")).then_inc(tok_in, 16)
                sp.dma_start(rope[:, :, :, :], a["rope"].rearrange("s (t p) d -> p s t d", p=P)).then_inc(tok_in, 16)
                for i, g in enumerate(("q_gain", "k_gain")):
                    sp.dma_start(qk_gain[:, i, :], a[g][0].partition_broadcast(P)).then_inc(tok_in, 16)
                sp.dma_start(spatial_bias[:, :, :].rearrange("p g q -> p (g q)"),
                             a["spatial_b"][0].rearrange("g q -> (g q)").partition_broadcast(P)).then_inc(tok_in, 16)
                for i, (c0, n) in enumerate(starts):
                    if i == 2:
                        sp.wait_ge(w_used, EU)
                        sp.dma_start(spatial_raw[:, :, :], a["spatial_w"][0].rearrange("g p q -> p g q"))\
                            .then_inc(tok_in, 16)
                    load_mix(EU + i, w, KT, slice(c0, c0 + n))
                for i in range(4):
                    load_mix(EU + 8 + i, wo, KT, slice(256 * i, 256 * (i + 1)))
                sp.wait_ge(qk_done, 1)
                sp.dma_start(out["new_cache_k"][0, 0], k_tok[:, 0, :, 0, :]).then_inc(cache_stored, 16)
                sp.dma_start(out["new_cache_v"][0, 0].rearrange("t h d -> t (h d)"), v_tok[:, 0, :]).then_inc(cache_stored, 16)
                sp.wait_ge(cache_stored, 32)

            def odd_sp():
                w = a["w_in_odd"][0].rearrange("(k p) n -> p k n", p=P)
                wo = a["w_out_odd"][0].rearrange("(k p) n -> p k n", p=P)
                K, V, O = CH * DK, 2 * CH * DK, 2 * CH * DK + C_WIDTH
                G = O + C_WIDTH
                DD = G + 16
                for i, c0 in enumerate((0, 256, K, K + 256, V, V + 256, O, O + 256, DD, DD + 256)):
                    load_mix(OU + i, w, KT, slice(c0, c0 + 256))
                    if i == 1:
                        sp.wait_ge(w_used, OU)
                        sp.dma_start(gate_raw[:, :, :], w[:, :, G:G + 16]).then_inc(gate_w_in, 16)
                        sp.dma_start(gate_bias[:, :], a["b_gate_odd"][0].rearrange("d k h -> (d k h)")
                                     .partition_broadcast(P)).then_inc(odd_in, 16)
                        sp.dma_start(m_given[:, :, :].rearrange("p d h -> p (d h)"),
                                     a["state_m"][0, 0].rearrange("d h -> (d h)").partition_broadcast(P)).then_inc(odd_in, 16)
                        sp.dma_start(masks[:, :, :], a["masks"].rearrange("m s t -> s m t")).then_inc(odd_in, 16)
                        with nc.allow_non_contiguous_dma(reason="1024 values of state n, one per partition"):
                            sp.dma_start(n_col[:, :, :], a["state_n"][0, 0].rearrange("d h k -> k d h")).then_inc(odd_in, 16)
                        sp.dma_start(state[:, :, :, 0:P], a["state_C"][0, 0].rearrange("d h e k -> e d h k"))\
                            .then_inc(odd_in, 16)
                sp.wait_ge(w_used, OU + 10)
                sp.dma_start(dft_c[:, :, :], a["dft_c"].rearrange("s p n -> p s n")).then_inc(dft_in, 16)
                sp.dma_start(dft_t[:, :, :, :], a["dft_t"].rearrange("s (t p) n -> p s t n", p=P)).then_inc(dft_in, 16)
                for i in range(4):
                    load_mix(OU + 10 + i, wo, KT, slice(256 * i, 256 * (i + 1)))
                for d in range(2):
                    sp.wait_ge(end_kept, d + 1)
                    sp.dma_start(out["new_state_C"][0, 0, d].rearrange("h e k -> e h k"), c_end[d][:, :, :])\
                        .then_inc(state_stored, 16)
                with nc.allow_non_contiguous_dma(reason="1024 values of state n, one per partition"):
                    sp.dma_start(out["new_state_n"][0, 0].rearrange("d h k -> k d h"), n_end[:, :, :]).then_inc(state_stored, 16)
                sp.dma_start(out["new_state_m"][0, 0].rearrange("(o d) h -> o (d h)", o=1),
                             m_end[0:1, :, :].rearrange("p d h -> p (d h)")).then_inc(state_stored, 16)
                sp.wait_ge(state_stored, 16 * 4)

            sp.dma_start(ident[:, :], a["identity"]).then_inc(consts_in, 16)
            b_rows = a["b_mod"].rearrange("l (r p) -> l r p", p=P)
            for l in range(DEPTH):
                sp.dma_start(small_rows[0:3 * N_SUB * KT, l, :], b_rows[l]).then_inc(rows_in, 16)
            sp.dma_start(small_rows[0:KT, 2, :], a["c_ctx"].rearrange("(r p) -> r p", p=P)).then_inc(rows_in, 16)
            sp.dma_start(small_rows[KT:2 * KT, 2, :], a["c"].rearrange("b (r p) -> (b r) p", p=P)).then_inc(rows_in, 16)
            sp.dma_start(small_rows[2 * KT:8 * KT, 2, :], a["norm_gain"].rearrange("l s (r p) -> (l s r) p", p=P))\
                .then_inc(rows_in, 16)
            sp.dma_start(small_rows[64:68, 2, :], a["sgu_gain"].rearrange("e g p -> (e g) p")).then_inc(rows_in, 16)
            sp.dma_start(small_rows[68:72, 2, :], a["identity"][0:4, :]).then_inc(rows_in, 16)
            for r in range(2):
                sp.dma_start(mod_first[r][:, :, :], w_mod[0][:, :, r * MOD_COLS:(r + 1) * MOD_COLS])\
                    .then_inc(mod_first_in[r], 16)
            sp.dma_start(x_rows[:, 0, :], a["x_prompt"][0]).then_inc(x_in, 16)
            sp.dma_start(x_rows[:, 1:TT, :], a["x_sample"][0].rearrange("(t p) d -> p t d", p=P)).then_inc(x_in, 16)
            for r in range(2, MOD_PE_BLOCKS):
                sp.dma_start(mod_first[r][:, :, :], w_mod[0][:, :, r * MOD_COLS:(r + 1) * MOD_COLS])\
                    .then_inc(mod_first_in[r], 16)
            load_pair(0, "in", 0, 0)
            load_mod.layer = 0
            load_mod(0)
            load_mod(1)
            ffn(0)
            if mixers:
                even_sp()
            load_pair(1, "in", FFN_AT[1] // 2, 0)
            ffn(1)
            load_pair(2, "in", FFN_AT[2] // 2, 0)
            ffn(2)
            if mixers:
                odd_sp()
            load_pair(3, "in", FFN_AT[3] // 2, 0)
            ffn(3)
            for t in range(TT):
                sp.wait_ge(y_kept_act, t + 1)
                sp.wait_ge(y_kept_dve, t + 1)
                dst = out["y_prompt"][0] if t == 0 else out["y_sample"][0][(t - 1) * P:t * P, :]
                sp.dma_start(dst, y_rows[:, t, :]).then_inc(stored, 16)
            sp.wait_ge(stored, 16 * TT)

        @block.tensor
        def _(pe):
            def split_product(outs, w3, v3, first, last):
                for i, (w, v) in enumerate(((0, 0), (0, 1), (1, 0))):
                    for o, cols in outs:
                        ins = pe.matmul(o, w3[w], v3[v][cols], start=first and i == 0, stop=last and i == 2)
                return ins

            def in_unit(f, s, slot, i, fresh=False):
                n = 22 * f + i
                pe.wait_ge(lo_ready, FFN_AT[f] + s + 1)
                if isinstance(i, int) and i == A_IN:
                    pe.wait_ge(x_updated, out_base(f) + KT)
                elif not (isinstance(i, int) and i == 0):
                    pe.wait_ge(silu_done, n)
                for g in range(2):
                    if g == 1 and not (isinstance(i, int) and i in (0, A_IN)):
                        pe.wait_ge(prod_done, n)
                    for kt in range(KT):
                        if fresh and g == 0:
                            pe.wait_ge(h_lo_ready, 8 * norm_at[f] + kt + 1)
                        t = 2 * kt + g
                        ins = split_product(
                            [(bank[2 * g + hf][:, 0:HALF], (slice(None), kt, cols)) for hf, cols in halves()],
                            (w_hi[:, slot, t, :], w_lo[:, slot, t, :]), (h_hi, h_lo), kt == 0, kt == KT - 1)
                    ins.then_inc(g_ready if g == 0 else w_used, 1)

            def out_unit(f, s, slot, kd, chunk):
                pe.wait_ge(lo_ready, FFN_AT[f] + s + 1)
                first = isinstance(kd, int) and kd == 0
                if first:
                    pe.wait_ge(silu_done, 22 * f + (A_IN, FT)[chunk])
                elif isinstance(kd, int) and kd == 1:
                    pe.wait_ge(prod_done, 22 * f + (A_IN, FT)[chunk])
                else:
                    pe.wait_ge(x_updated, out_base(f) + 8 * chunk + kd - 1)
                n = CHUNK_TILES[chunk]
                for k in range(n):
                    if first:
                        pe.wait_ge(hid_lo_done, 22 * f + (0, A_IN)[chunk] + k + 1)
                    ins = split_product(
                        [(bank[2 * slot + hf][:, 0:HALF], (slice(None), k, cols)) for hf, cols in halves()],
                        (w_hi[:, slot, k, :], w_lo[:, slot, k, :]), (hid_hi, hid_lo), k == 0, k == n - 1)
                ins.then_inc(w_used, 1)

            def turn_mod(b):
                pe.wait_ge(mod_summed, b + 1)
                for m in range(MOD_TILES):
                    for v in range(2):
                        ins = pe.matmul(bank[MODB][:, 2 * m + v:2 * m + v + 1], mod_acc[:, v, m * P:(m + 1) * P],
                                        ones[:, 0:1], start=True, stop=True)
                ins.then_inc(mod_turned, 1)

            def sum_squares(n):
                pe.wait_ge(square_added, KT * (n + 1))
                for hf, cols in halves():
                    ins = pe.matmul(bank[SUMS[hf]][:, 0:HALF], ones[:, :], ss[:, cols], start=True, stop=True)
                ins.then_inc(sums_ready, 1)

            def ffn(f):
                blk = ffn.block

                def run(first, last, body):
                    turns = (last - first) // 2
                    with pe.Fori(0, turns) as t:
                        if f < 2:
                            turn_mod(t + (blk[0] - 1))
                        for slot in range(2):
                            body(first + 2 * t + slot, slot)
                    if f < 2:
                        blk[0] += turns
                for s in range(2):
                    in_unit(f, s, s, s, fresh=s == 0)
                    if f == 0 and s == 0:
                        turn_mod(0)
                run(2, A_IN, lambda s, slot: in_unit(f, s, slot, s))
                for s in range(A_IN, A_IN + 2):
                    out_unit(f, s, s % 2, s - A_IN, 0)
                run(A_IN + 2, A_OUT, lambda s, slot: out_unit(f, s, slot, s - A_IN, 0))
                for s in range(A_OUT, A_OUT + 2):
                    in_unit(f, s, s % 2, s - A_OUT + A_IN)
                run(A_OUT + 2, B_OUT, lambda s, slot: in_unit(f, s, slot, s - (A_OUT - A_IN)))
                for s in range(B_OUT, B_OUT + 2):
                    out_unit(f, s, s % 2, s - B_OUT, 1)
                run(B_OUT + 2, FFN_UNITS, lambda s, slot: out_unit(f, s, slot, s - B_OUT, 1))
            ffn.block = [2]

            def out_pair(unit, ready_x, first):
                slot = unit % 2
                pe.wait_ge(lo_ready, unit + 1)
                for i in range(2):
                    if ready_x + i >= first + 2:
                        pe.wait_ge(x_updated, ready_x + i - 1)
                    for k in range(KT):
                        ins = split_product(
                            [(bank[2 * i + hf][:, 0:HALF], (slice(None), k, cols)) for hf, cols in halves()],
                            (w_hi[:, slot, 2 * k + i, :], w_lo[:, slot, 2 * k + i, :]), (hid_hi, hid_lo), k == 0, k == KT - 1)
                    ins.then_inc(out_ready if i == 0 else w_used, 1)

            def token_unit(unit, fill0, fresh, taken):
                slot = unit % 2
                pe.wait_ge(lo_ready, unit + 1)
                wh, wl = (w[:, slot].rearrange("p (k c) q -> p k (c q)", c=2) for w in (w_hi, w_lo))
                for t in range(TT):
                    taken(fill0 + t)
                    cols = slice(t * P, (t + 1) * P)
                    dst = bank[(fill0 + t) % 4][:, 0:2 * P]
                    for kt in range(KT):
                        if fresh is not None and t == 0:
                            pe.wait_ge(h_lo_ready, KT * fresh + kt + 1)
                        pe.matmul(dst, h_hi[:, kt, cols], wh[:, kt, :], start=kt == 0, stop=False)
                        pe.matmul(dst, h_hi[:, kt, cols], wl[:, kt, :], start=False, stop=False)
                        ins = pe.matmul(dst, h_lo[:, kt, cols], wh[:, kt, :], start=False, stop=kt == KT - 1)
                    ins.then_inc(tok_ready if t < TT - 1 else w_used, 1)

            def feature_tile(unit, i, banks, last_sem):
                slot = unit % 2
                if i == 0:
                    pe.wait_ge(lo_ready, unit + 1)
                for kt in range(KT):
                    ins = split_product(
                        [(bank[banks + hf][:, 0:HALF], (slice(None), kt, cols)) for hf, cols in halves()],
                        (w_hi[:, slot, 2 * kt + i, :], w_lo[:, slot, 2 * kt + i, :]), (h_hi, h_lo), kt == 0, kt == KT - 1)
                ins.then_inc(last_sem, 1)

            def even_pe():
                bank_flat = [bank2[i][:, :, :].rearrange("p a b -> p (a b)") for i in range(4)]

                def taken(r):
                    if r - 4 >= 15:
                        pe.wait_ge(tok_kept_act, r - 4 - 15 + 1)
                    elif r >= 4:
                        pe.wait_ge(tok_kept_dve, r - 4 + 1)
                for u in range(N_TOK_UNITS):
                    token_unit(EU + u, TT * u, 1 if u == 0 else None, taken)
                for m, (u, i) in enumerate(((5, 0), (5, 1), (6, 0), (7, 0))):
                    if m >= 2:
                        pe.wait_ge(u_gate_kept, m - 1)
                    feature_tile(EU + u, i, 4 + 2 * (m % 2), u_gate_ready if m == 0 else w_used)

                def turn(n, blocks):
                    if n >= 4:
                        pe.wait_ge(turn_kept_act if n % 2 == 0 else turn_kept_dve, (n - 4) // 2 + 1)
                    for j, src in enumerate(blocks):
                        ins = pe.transpose(bank[n % 4][:, j * P:(j + 1) * P], src, ident[:, :])
                    ins.then_inc(turned, 1)
                pe.wait_ge(tok_in, 16 * 7)
                pe.wait_ge(tok_kept_act, 10)
                turn(0, [spatial_raw[:, g, :] for g in range(A_GROUPS)])
                pe.wait_ge(qk_done, 1)
                for n in range(3):
                    turn(1 + n, [k_tok[:, 2 * n + j // 2, j % 2, :, :].rearrange("p a d -> p (a d)") for j in range(4)])
                pe.wait_ge(qk_done, 2)
                for t in range(TT):
                    turn(4 + t, [q_tok[:, t, j * P:(j + 1) * P] for j in range(NH // 2)])

                pe.wait_ge(qk_done, 3)
                pe.wait_ge(turn_kept_act, 5)
                pe.wait_ge(turn_kept_dve, 4)
                pe.wait_ge(u_gate_kept, 4)
                for g in range(A_GROUPS):
                    for t in range(TT):
                        ins = pe.matmul(bank[2 * g + t // 4][:, t % 4 * P:(t % 4 + 1) * P],
                                        v_gate[:, t, g * P:(g + 1) * P], spatial_t[:, g, :], start=True, stop=True)
                    ins.then_inc(spatial_ready, 1)

                def scores(i):
                    t, h = divmod(i, NH)
                    k0, k1 = att_keys(i)
                    if i < 2:
                        pe.wait_ge(spatial_gated, i + 1)
                    else:
                        pe.wait_ge(exp_done, i - 1)
                    rows = slice(h % 2 * HD, (h % 2 + 1) * HD)
                    q = q_feat[rows, h // 2, t * P:(t + 1) * P]
                    n = (k1 - k0) * P
                    parts = [slice(0, n)] if n <= 512 else [slice(0, n // 2), slice(n // 2, n)]
                    for j, c in enumerate(parts):
                        ins = pe.matmul(bank[2 * (i % 2) + j][:, 0:c.stop - c.start], q,
                                        k_feat[rows, h // (NH // NKV), k0 * P + c.start:k0 * P + c.stop],
                                        start=True, stop=True)
                    ins.then_inc(scores_ready, 1)

                def turn_probs(i):
                    k0, k1 = att_keys(i)
                    pe.wait_ge(prob_ready, i + 1)
                    if i == 0:
                        pe.wait_ge(spatial_gated, 3)
                    else:
                        pe.wait_ge(prob_kept, i)
                    for j in range(k1 - k0):
                        ins = pe.transpose(bank[4 + j // 4][:, j % 4 * P:(j % 4 + 1) * P],
                                           prob[:, i % 2, j * P:(j + 1) * P], ident[:, :])
                    ins.then_inc(prob_turned, 1)

                def values(i):
                    t, h = divmod(i, NH)
                    k0, k1 = att_keys(i)
                    pe.wait_ge(prob_kept, i + 1)
                    if h == 0:
                        if t == 0:
                            pe.wait_ge(spatial_gated, 4)
                        elif t >= 2:
                            pe.wait_ge(mix_done, A_GROUPS + t - 1)
                    g = h // (NH // NKV)
                    for j in range(k1 - k0):
                        ins = pe.matmul(bank[6 + t % 2][h % 2 * HD:(h % 2 + 1) * HD, h // 2 * P:(h // 2 + 1) * P],
                                        v_tok[:, k0 + j, g * HD:(g + 1) * HD], prob_t[:, i % 2, j * P:(j + 1) * P],
                                        start=j == 0, stop=j == k1 - k0 - 1)
                    if h == NH - 1:
                        ins.then_inc(att_ready, 1)

                for i in range(N_ATT + 2):
                    if i < N_ATT:
                        scores(i)
                    if i >= 2:
                        values(i - 2)
                    if 1 <= i <= N_ATT:
                        turn_probs(i - 1)

                pe.wait_ge(mix_done, A_GROUPS + TT)
                for i in range(4):
                    out_pair(EU + 8 + i, out_base(1) - KT + 2 * i, out_base(1) - KT)

            def odd_pe():
                def feature_pair(unit, f0, fresh=False):
                    for i in range(2):
                        f = f0 + i
                        if f >= 2:
                            kind, n = (f - 2) // 4, (f - 2) % 4
                            pe.wait_ge(tile_kept_act if kind in (0, 2) else tile_kept_dve, (kind // 2) * 4 + n + 1)
                        if fresh and i == 0:
                            pe.wait_ge(lo_ready, unit + 1)
                            for kt in range(KT):
                                pe.wait_ge(h_lo_ready, KT * 4 + kt + 1)
                        feature_tile(unit, i, 4 + 2 * (f % 2), tile_ready if i == 0 else w_used)

                def taken(r):
                    if r < 4:
                        pe.wait_ge(gate_dve, 1 if r < 3 else 3)
                    else:
                        pe.wait_ge(tok_kept_dve, 15 + r - 4 + 1)

                feature_pair(OU, 0, fresh=True)
                feature_pair(OU + 1, 2)
                pe.wait_ge(gate_dve, 1)
                for t in range(TT):
                    cols = slice(t * P, (t + 1) * P)
                    for kt in range(KT):
                        for i, (hx, gx) in enumerate(((h_hi, gate_hi), (h_hi, gate_lo), (h_lo, gate_hi))):
                            ins = pe.matmul(bank[0][:, 16 * t:16 * t + 16], hx[:, kt, cols], gx[:, kt, :],
                                            start=kt == 0 and i == 0, stop=kt == KT - 1 and i == 2)
                ins.then_inc(gate_pe, 1)
                feature_pair(OU + 2, 4)
                feature_pair(OU + 3, 6)
                pe.wait_ge(gate_dve, 2)
                for d in range(2):
                    pe.matmul(bank[3][:, 32 * d:32 * (d + 1)], masks[:, 2 + d, :], log_f[:, 32 * d:32 * (d + 1)],
                              start=True, stop=True)
                pe.matmul(bank[3][:, GR:2 * GR], ones[:, :], log_f[:, :], start=True, stop=True).then_inc(gate_pe, 1)
                for u in range(2):
                    token_unit(OU + 4 + u, TT * u, None, taken)
                pe.wait_ge(tok_kept_dve, 25)
                for i in range(2):
                    ins = pe.transpose(bank[0][0:GR, i * P:(i + 1) * P], ab[:, i, :], ident[:, :])
                ins.then_inc(gate_pe, 1)
                feature_pair(OU + 6, 8)
                pe.wait_ge(gate_dve, 4)
                pe.matmul(bank[1][:, 0:GR], a_max[:, :], ident[0:GR, 0:GR], start=True, stop=True).then_inc(gate_pe, 1)
                feature_pair(OU + 7, 10)
                pe.wait_ge(gate_dve, 5)
                pe.transpose(bank[2][0:GR, 0:P], m_start[:, :], ident[:, :]).then_inc(gate_pe, 1)
                feature_pair(OU + 8, 12)
                feature_pair(OU + 9, 14)

                pe.wait_ge(dft_in, 32)
                pe.wait_ge(gate_dve, 6)
                pe.wait_ge(tile_kept_dve, 8)
                for n in range(2 * TT):
                    t, g0 = n // 2, n % 2 * 2
                    if n >= 4:
                        pe.wait_ge(uv_kept_act if n % 2 == 0 else uv_kept_dve, (n - 4) // 2 + 1)
                    for j in range(2):
                        ins = pe.matmul(bank[n % 4][:, 2 * P * j:2 * P * (j + 1)], d_f[:, g0 + j, t * P:(t + 1) * P],
                                        dft_c[:, 0:2, :].rearrange("p s n -> p (s n)"), start=True, stop=True)
                    ins.then_inc(uv_ready, 1)
                pe.wait_ge(uv_kept_act, TT)
                pe.wait_ge(uv_kept_dve, TT)
                for g in range(D_GROUPS):
                    b = 4 + 2 * (g % 2)
                    if g >= 2:
                        pe.wait_ge(four_lo, g - 1)
                    for t in range(1, TT):
                        for s in range(2):
                            pe.matmul(bank[b][:, :], uv[:, t, g, s * P:(s + 1) * P], dft_t[:, s, t - 1, :],
                                      start=t == 1 and s == 0, stop=t == TT - 1 and s == 1)
                    for s in range(2):
                        ins = pe.matmul(bank[b + 1][:, 0:P], uv[:, 0, g, s * P:(s + 1) * P], dft_c[:, 2 * s, :],
                                        start=s == 0, stop=s == 1)
                    ins.then_inc(four_ready, 1)

                for n in range(TT + 2):
                    if n >= 4:
                        pe.wait_ge(k_kept, n - 3)
                    for h in range(CH):
                        src = k_f[:, h, n * P:(n + 1) * P] if n < TT else state[:, n - TT, h, 0:P]
                        if n == TT and h == 0:
                            pe.wait_ge(odd_in, 16 * 5)
                        ins = pe.transpose(bank[n % 4][:, h * P:(h + 1) * P], src, ident[:, :])
                    ins.then_inc(k_turned, 1)

                def bcast(n):
                    t, d = GROUPS[n]
                    if n == 0:
                        pe.wait_ge(k_kept, TT + 2)
                        pe.wait_ge(four_lo, D_GROUPS)
                    else:
                        pe.wait_ge(exps_done, n)
                    for i in range(2):
                        for h in range(CH):
                            r = row_of(t, d, h)
                            ins = pe.matmul(bank[i][:, h * P:(h + 1) * P], ident[0:GR, r:r + 1].to_broadcast([GR, P]),
                                            m_rows[:, i, :], start=True, stop=True)
                    ins.then_inc(bcast_ready, 1)
                    if n >= 1:
                        pe.wait_ge(a_ready, n)
                    for h in range(CH):
                        cols = slice(t * P, (t + 1) * P)
                        ins = pe.matmul(bank[4][:, h * P:(h + 1) * P], k_f[:, h, cols], q_f[:, h, cols],
                                        start=True, stop=True)
                    ins.then_inc(qk_ready, 1)

                def group(n):
                    t, d = GROUPS[n]
                    c = n % 2
                    given = t > 0
                    pe.wait_ge(a_ready, n + 1)
                    if n >= 1:
                        pe.wait_ge(h_done, n)
                    if given:
                        if n >= 4:
                            pe.wait_ge(st_taken, n - 1)
                        else:
                            pe.wait_ge(state_kept, 1)
                    for h in range(CH):
                        hp = slice(h * P, (h + 1) * P)
                        pe.matmul(bank[2][:, hp], v_t[:, t, hp], a_t[:, c, hp], start=True, stop=not given)
                        if given:
                            pe.matmul(bank[2][:, hp], state[:, d, h, 0:P], q_w[:, c, h, :], start=False, stop=True)
                    for h in range(CH):
                        hp = slice(h * P, (h + 1) * P)
                        ins = pe.matmul(bank[3][:, hp], ones[:, :], a_t[:, c, hp], start=True, stop=not given)
                        if given:
                            ins = pe.matmul(bank[3][:, hp], state[:, d, h, P:2 * P], q_w[:, c, h, :], start=False, stop=True)
                    ins.then_inc(nd_ready, 1)
                    if n not in STATE_GROUPS:
                        return
                    pe.wait_ge(v_ready, n + 1)
                    if n >= 1:
                        pe.wait_ge(st_taken, n)
                    for h in range(CH):
                        k_h = k_t[:, t, h * P:(h + 1) * P]
                        if given:
                            ins = pe.matmul(bank[6 + h // 2][:, h % 2 * 2 * P:(h % 2 + 1) * 2 * P], k_h, v_w[:, c, h, :],
                                            start=True, stop=True)
                        else:
                            pe.matmul(bank[6][:, h * P:(h + 1) * P], v_w[:, c, h, 0:P], k_h, start=True, stop=True)
                            ins = pe.matmul(bank[7][:, h:h + 1], k_h, v_w[:, c, h, P:P + 1], start=True, stop=True)
                    ins.then_inc(st_ready, 1)

                bcast(0)
                for n in range(NG):
                    if n + 1 < NG:
                        bcast(n + 1)
                    group(n)
                pe.wait_ge(c_lo, CH)
                for i in range(4):
                    out_pair(OU + 10 + i, out_base(3) - KT + 2 * i, out_base(3) - KT)

            pe.wait_ge(consts_in, 16)
            pe.wait_ge(rows_in, 16 * 7)
            for r in range(3):
                ins = pe.transpose(bank[5][:, r * P:r * P + 72], small_rows[0:72, r, :], ident[0:72, 0:72])
            ins.then_inc(rows_turned, 1)
            pe.wait_ge(x_in, 32)
            for n in range(2 * TT):
                t, half = divmod(n, 2)
                if n >= 4:
                    pe.wait_ge(x_kept_act if n % 2 == 0 else x_kept_dve, (n - 4) // 2 + 1)
                for q in range(4):
                    kt = 4 * half + q
                    ins = pe.transpose(bank[n % 4][:, q * P:(q + 1) * P], x_rows[:, t, kt * P:(kt + 1) * P], ident[:, :])
                ins.then_inc(x_turned, 1)
            pe.wait_ge(silu_ready, 1)
            for r in range(MOD_PE_BLOCKS):
                pe.wait_ge(mod_first_in[r], 16)
                for m in range(MOD_TILES):
                    o = 2 * (MOD_TILES * r + m)
                    for kt in range(KT):
                        ins = pe.matmul(bank[MODB][:, o:o + 2], mod_first[r][:, kt, m * P:(m + 1) * P],
                                        silu_c[:, kt, :], start=kt == 0, stop=kt == KT - 1)
            ins.then_inc(mod_first_sum, 1)
            sum_squares(0)
            ffn(0)
            sum_squares(1)
            if mixers:
                even_pe()
                sum_squares(2)
            ffn(1)
            turn_mod(MOD_BLOCKS - 1)
            sum_squares(norm_at[2])
            ffn(2)
            sum_squares(norm_at[2] + 1)
            if mixers:
                odd_pe()
                sum_squares(5)
            ffn(3)
            pe.wait_ge(x_updated, out_base(3) + 16)
            for n in range(2 * TT):
                t, half = divmod(n, 2)
                if n >= 4:
                    pe.wait_ge(y_kept_act if n % 2 == 0 else y_kept_dve, (n - 4) // 2 + 1)
                for q in range(4):
                    kt = 4 * half + q
                    ins = pe.transpose(bank[n % 4 + 4][:, q * P:(q + 1) * P], x[:, kt, t * P:(t + 1) * P], ident[:, :])
                ins.then_inc(y_turned, 1)

        @block.scalar
        def _(act):
            def split_hi(u, slot, pair, kind):
                act.wait_ge(raw_in, 32 * (pair + 1))
                if not (isinstance(u, int) and u < 2):
                    act.wait_ge(w_used, u - 1)
                act.activation(split_view(w_hi, kind, slot), raw_view(kind, slot), ACT.Copy).then_inc(hi_ready, 1)

            def silu(f, i, c):
                act.wait_ge(g_ready, 22 * f + i + 1)
                for hf, cols in halves():
                    ins = act.activation(work_a[:, c, cols], bank[hf][:, 0:HALF], ACT.Silu)
                ins.then_inc(silu_done, 1)

            def hidden_hi(f, i, c, k):
                act.wait_ge(prod_done, 22 * f + i + 1)
                act.activation(hid_hi[:, k, :], work_b[:, c, :], ACT.Copy).then_inc(hid_hi_done, 1)

            def square(n, d, c):
                if not (isinstance(d, int) and d < 2):
                    act.wait_ge(square_added, KT * n + d - 1)
                act.activation(work_a[:, c, :], x[:, d, :], ACT.Square).then_inc(squared, 1)

            def norm(n):
                l, j = divmod(norm_kind[n], N_SUB)
                act.wait_ge(sums_ready, n + 1)
                for hf, cols in halves():
                    ins = act.activation(ss[:, cols], bank[SUMS[hf]][:, 0:HALF], ACT.Sqrt, scale=1.0 / D, bias=eps[:, 0:1])
                ins.then_inc(rms_ready, 1)
                for kt in range(KT):
                    c = kt % 2
                    act.wait_ge(xn_ready, KT * n + kt + 1)
                    if kt >= 2:
                        act.wait_ge(h_lo_ready, KT * n + kt - 1)
                    for v, cols in PARTS:
                        ins = act.activation(work_a[:, c, cols], work_b[:, c, cols], ACT.Identity,
                                             bias=mod_col(v, l, 3 * j, kt), scale=mod_col(v, l, 3 * j + 1, kt))
                    ins.then_inc(h_ready, 1)
                    act.wait_ge(h_ready, KT * n + kt + 1)
                    act.activation(h_hi[:, kt, :], work_a[:, c, :], ACT.Copy).then_inc(h_hi_ready, 1)

            def ffn(f, after):
                U = FFN_AT[f]

                def run(first, last, body):
                    with act.Fori(0, (last - first) // 2) as t:
                        for slot in range(2):
                            body(first + 2 * t + slot, slot, U // 2 + first // 2 + t)

                def in_step(shift):
                    def body(s, slot, pair):
                        split_hi(U + s, slot, pair, "in")
                        hidden_hi(f, s - 2 + shift[0], slot, s - 2 - shift[1])
                        silu(f, s - 1 + shift[0], 1 - slot)
                    return body

                def out_step(kind, origin, final):
                    def body(s, slot, pair):
                        split_hi(U + s, slot, pair, kind)
                        if final:
                            d = s - 2 - origin
                            act.wait_ge(x_updated, out_base(f) + 8 + d + 1)
                            square_in_loop(d, slot)
                    return body

                def square_in_loop(d, c):
                    if after[0] is not None:
                        act.wait_ge(squares_free, square_wait(after[0], d))
                        act.activation(work_a[:, c, :], x[:, d, :], ACT.Square).then_inc(squared, 1)

                silu(f, 0, 0)
                run(2, A_IN, in_step((0, 0)))
                split_hi(U + A_IN, 0, (U + A_IN) // 2, "outA")
                hidden_hi(f, A_IN - 2, 0, A_IN - 2)
                silu(f, A_IN - 1, 1)
                split_hi(U + A_IN + 1, 1, (U + A_IN) // 2, "outA")
                hidden_hi(f, A_IN - 1, 1, A_IN - 1)
                run(A_IN + 2, A_OUT, out_step("outA", A_IN, False))
                split_hi(U + A_OUT, 0, (U + A_OUT) // 2, "in")
                split_hi(U + A_OUT + 1, 1, (U + A_OUT) // 2, "in")
                silu(f, A_IN, 0)
                run(A_OUT + 2, B_OUT, in_step((A_IN - A_OUT, A_OUT)))
                split_hi(U + B_OUT, 0, (U + B_OUT) // 2, "outB")
                hidden_hi(f, FT - 2, 0, B_IN - 2)
                silu(f, FT - 1, 1)
                split_hi(U + B_OUT + 1, 1, (U + B_OUT) // 2, "outB")
                hidden_hi(f, FT - 1, 1, B_IN - 1)
                run(B_OUT + 2, FFN_UNITS, out_step("outB", B_OUT, True))
                for d in range(KT - 2, KT):
                    if d == KT - 2 and after[1] is not None:
                        split_hi(U + FFN_UNITS, 0, (U + FFN_UNITS) // 2, after[1])
                    act.wait_ge(x_updated, out_base(f) + 8 + d + 1)
                    square_in_loop(d, d % 2)
                if after[0] is not None:
                    norm(after[0])
                    split_hi(U + FFN_UNITS + 1, 1, (U + FFN_UNITS) // 2, after[1])

            squares_free = square_added

            def square_wait(n, d):
                return KT * n + d - 1

            def mix_squares(n, base, unit, last_kind):
                for d in range(KT):
                    if d % 2 == 0 and d >= 2:
                        split_hi(unit + d // 2 + 1, (unit + d // 2 + 1) % 2, (unit + d // 2 + 1) // 2,
                                 "mix" if d < 6 else last_kind)
                    act.wait_ge(x_updated, base + d + 1)
                    square(n, d, d % 2)

            def even_act():
                def keep_v(r):
                    fill_ready(act, EU, r)
                    u, t = divmod(r - 15, TT)
                    act.activation(v_gate[:, t, 2 * P * u:2 * P * (u + 1)], bank[r % 4][:, 0:2 * P], ACT.Gelu_apprx_tanh)\
                        .then_inc(tok_kept_act, 1)

                def keep_u(m):
                    u_tile_ready(act, m)
                    for hf, cols in halves():
                        ins = act.activation(u_gate[:, m, cols], bank[4 + 2 * (m % 2) + hf][:, 0:HALF], ACT.Gelu_apprx_tanh)
                    ins.then_inc(u_gate_kept, 1)

                def roots(n, cols, scale):
                    act.wait_ge(stat_ready, n)
                    act.activation(stat[:, cols], stat[:, cols], ACT.Sqrt, scale=scale, bias=eps[:, 0:1]).then_inc(root_ready, 1)

                def split(i):
                    split_hi(EU + i, (EU + i) % 2, (EU + i) // 2, "mix" if i not in (6, 7) else "one")
                n_qk = TT * (NH + NKV)
                for i in (2, 3, 4):
                    split(i)
                for r in range(15, 20):
                    keep_v(r)
                roots(1, slice(0, n_qk), 1.0 / HD)
                split(5)
                for r in range(20, 25):
                    keep_v(r)
                split(6)
                keep_u(0)
                keep_u(1)
                split(7)
                keep_u(2)
                roots(2, slice(n_qk, n_qk + TT * A_GROUPS), 1.0 / A_DIM)
                split(8)
                keep_u(3)
                split(9)
                act.wait_ge(turned, 1)
                act.activation(spatial_t[:, :, :], bank[0][:, :].rearrange("p (g q) -> p g q", g=A_GROUPS), ACT.Copy)\
                    .then_inc(turn_kept_act, 1)
                for n in range(2, 9, 2):
                    act.wait_ge(turned, n + 1)
                    turned_out(act.activation, n, ACT.Copy).then_inc(turn_kept_act, 1)
                for g in range(A_GROUPS):
                    act.wait_ge(spatial_gated, g + 1)
                    act.activation(hid_hi[:, g, :], u_gate[:, g, :], ACT.Copy).then_inc(spatial_hi, 1)

                for i in range(N_ATT + 2):
                    if i < N_ATT:
                        k0, k1 = att_keys(i)
                        n = (k1 - k0) * P
                        act.wait_ge(max_ready, i + 1)
                        if i >= 2:
                            act.wait_ge(prob_turned, i - 1)
                        src = bank2[i % 2][:, 0, 0:P] if n == P else bank2[i % 2][:, :, 0:n // 2]
                        dst = prob[:, i % 2, 0:n] if n == P else prob[:, i % 2, :].rearrange("p (a b) -> p a b", a=2)
                        act.activation(dst, src, ACT.Exp, scale=HD ** -0.5, bias=soft[:, 1, i % 4:i % 4 + 1],
                                       accum_out=soft[:, 2, i % 4:i % 4 + 1]).then_inc(exp_done, 1)
                    if 1 <= i <= N_ATT:
                        k0, k1 = att_keys(i - 1)
                        n = (k1 - k0) * P
                        act.wait_ge(prob_turned, i)
                        act.activation(prob_t[:, (i - 1) % 2, 0:n], bank2[2][:, :, :].rearrange("p a b -> p (a b)")[:, 0:n],
                                       ACT.Copy).then_inc(prob_kept, 1)
                    if i >= 2 and (i - 2) % NH == NH - 1:
                        t = (i - 2) // NH
                        act.wait_ge(att_ready, t + 1)
                        act.activation(hid_hi[:, 4:8, t * P:(t + 1) * P],
                                       bank[6 + t % 2][:, :].rearrange("p (k t) -> p k t", k=4), ACT.Copy).then_inc(att_hi, 1)
                mix_squares(2, out_base(1) - KT, EU + 8, "in")
                norm(2)
                split_hi(EU + MIX_EVEN_UNITS + 1, 1, (EU + MIX_EVEN_UNITS) // 2, "in")

            def odd_act():
                def keep(f):
                    odd_tile_ready(act, f)
                    dst, func = (q_f, ACT.Copy) if f < 4 else (o_f, ACT.Sigmoid)
                    for hf, cols in halves():
                        ins = act.activation(dst[:, f % 4, cols], bank[4 + 2 * (f % 2) + hf][:, 0:HALF], func)
                    ins.then_inc(tile_kept_act, 1)

                def split(i):
                    split_hi(OU + i, (OU + i) % 2, (OU + i) // 2, "mix")
                act.wait_ge(gate_w_in, 16)
                act.activation(gate_hi[:, :, :], gate_raw[:, :, :], ACT.Copy).then_inc(gate_w_hi, 1)
                keep(0)
                keep(1)
                split(2)
                keep(2)
                keep(3)
                split(3)
                act.wait_ge(gate_dve_abs, 1)
                act.activation(gate_abs[:, :, :, :], gate_abs[:, :, :, :], ACT.Exp, scale=-1.0).then_inc(gate_act, 1)
                act.wait_ge(gate_act, 1)
                act.activation(gate_abs[:, :, :, :], gate_abs[:, :, :, :], ACT.Ln, bias=ones[:, 0:1]).then_inc(gate_act, 1)
                for i in range(4, 8):
                    split(i)
                keep(8)
                keep(9)
                split(8)
                keep(10)
                keep(11)
                split(9)
                split(10)
                for n in range(0, 2 * TT, 2):
                    if n == 2 * TT - 2:
                        split(11)
                    act.wait_ge(uv_ready, n + 1)
                    act.activation(uv[:, n // 2, 0:2, :], bank[n % 4][:, :].rearrange("p (g c) -> p g c", g=2), ACT.Copy)\
                        .then_inc(uv_kept_act, 1)
                for g in range(D_GROUPS):
                    act.wait_ge(four_ready, g + 1)
                    b = 4 + 2 * (g % 2)
                    act.activation(hid_hi[:, 4 + g, T_CTX:T], bank[b][:, :], ACT.Copy, scale=(T_LAT * D_DIM) ** -0.5)
                    act.activation(hid_hi[:, 4 + g, 0:T_CTX], bank[b + 1][:, 0:P], ACT.Copy, scale=(T_CTX * D_DIM) ** -0.5)\
                        .then_inc(four_hi, 1)
                for n in range(NG):
                    t, d = GROUPS[n]
                    c = n % 2
                    act.wait_ge(x_ready, n + 1)
                    if n >= 2:
                        act.wait_ge(a_ready, n - 1)
                        act.wait_ge(h_done, n - 1)
                        if n - 2 in STATE_GROUPS:
                            act.wait_ge(st_taken, n - 1)
                    act.activation(w_in_[:, c, :, :], w_in_[:, c, :, :], ACT.Exp, scale=-1.0)
                    for h in range(CH):
                        r = row_of(t, d, h)
                        act.activation(w_pr[:, c, h, :], bank[0][:, h * P:(h + 1) * P], ACT.Exp, scale=-1.0,
                                       bias=m_start[:, r:r + 1])
                    act.activation(e_m[:, c, :], bank[1][:, :], ACT.Exp, scale=-1.0).then_inc(exps_done, 1)
                act.wait_ge(state_stored, 16 * 4)
                for h in range(CH):
                    act.wait_ge(h_final, h + 1)
                    act.activation(hid_hi[:, h, :], h_sum[:, h, :], ACT.Copy).then_inc(c_hi, 1)
                mix_squares(5, out_base(3) - KT, OU + 10, "in")
                norm(5)
                split_hi(OU + MIX_ODD_UNITS + 1, 1, (OU + MIX_ODD_UNITS) // 2, "in")

            act.wait_ge(rows_kept, 1)
            act.activation(silu_c[:, :, :].rearrange("p k v -> p v k"),
                           rows_t[:, 0:2 * KT].rearrange("p (v k) -> p v k", v=2), ACT.Silu).then_inc(silu_ready, 1)
            for n in range(0, 2 * TT, 2):
                act.wait_ge(x_turned, n + 1)
                act.activation(x[:, 0:4, n // 2 * P:(n // 2 + 1) * P],
                               bank[n % 4][:, :].rearrange("p (k t) -> p k t", k=4), ACT.Copy).then_inc(x_kept_act, 1)
            act.wait_ge(x_kept_dve, TT)
            act.wait_ge(x_kept_act, TT)
            for d in range(KT):
                square(0, d, d % 2)
            split_hi(0, 0, 0, "in")
            norm(0)
            split_hi(1, 1, 0, "in")
            ffn(0, (1, "mix" if mixers else "in"))
            if mixers:
                even_act()
            ffn(1, (norm_at[2], "in"))
            ffn(2, (norm_at[2] + 1, "mix" if mixers else "in"))
            if mixers:
                odd_act()
            ffn(3, (None, None))
            for n in range(0, 2 * TT, 2):
                act.wait_ge(y_turned, n + 1)
                act.activation(y_rows[:, n // 2, 0:4 * P], bank[n % 4 + 4][:, :], ACT.Copy).then_inc(y_kept_act, 1)

        @block.vector
        def _(dve):
            chain = Count(dve, dve_chain)

            def split_lo(u, slot, kind):
                dve.wait_ge(hi_ready, u + 1)
                dve.tensor_tensor(split_view(w_lo, kind, slot), raw_view(kind, slot),
                                  split_view(w_hi, kind, slot).bitcast(F32), ALU.subtract).then_inc(lo_ready, 1)

            def product(f, s, i, c):
                dve.wait_ge(silu_done, 22 * f + i + 1)
                dve.wait_ge(w_used, FFN_AT[f] + s + 1)
                for hf, cols in halves():
                    ins = dve.tensor_tensor(work_b[:, c, cols], work_a[:, c, cols], bank[2 + hf][:, 0:HALF], ALU.mult)
                ins.then_inc(prod_done, 1)

            def hidden_lo(f, i, c, k):
                dve.wait_ge(hid_hi_done, 22 * f + i + 1)
                dve.wait_ge(prod_done, 22 * f + i + 1)
                dve.tensor_tensor(hid_lo[:, k, :], work_b[:, c, :], hid_hi[:, k, :].bitcast(F32), ALU.subtract)\
                    .then_inc(hid_lo_done, 1)

            def update_x(unit, layer, j, d, c):
                if unit is not None:
                    dve.wait_ge(w_used, unit + 1)
                for hf, v, cols, in_bank in PIECES:
                    xs = x[:, d, cols]
                    ins = dve.scalar_tensor_tensor(out=xs, in0=bank[2 * c + hf][:, in_bank],
                                                   scalar=mod_col(v, layer, 3 * j + 2, d), in1=xs,
                                                   op0=ALU.mult, op1=ALU.add)
                ins.then_inc(x_updated, 1)

            def sum_mod(b, kts):
                if kts[0] == 0:
                    dve.wait_ge(mod_in, 16 * (b + 1))
                for kt in kts:
                    for v in range(2):
                        sc = silu_c[:, kt, v:v + 1]
                        if kt == 0:
                            chain.inc(dve.tensor_scalar(mod_acc[:, v, :], mod_raw[:, kt, :], sc, None, ALU.mult))
                        else:
                            chain.wait(back=1)
                            ins = dve.scalar_tensor_tensor(out=mod_acc[:, v, :], in0=mod_raw[:, kt, :], scalar=sc,
                                                           in1=mod_acc[:, v, :], op0=ALU.mult, op1=ALU.add)
                            if kt == KT - 1 and v == 1:
                                ins.then_inc(mod_summed, 1)
                            else:
                                chain.inc(ins)

            def keep_mod(sums, cols, n):
                for v in range(2):
                    chain.inc(dve.tensor_tensor(keep_mod.tmp(v, n), sums[:, :, v], mod_add[:, cols], ALU.add))
                chain.wait()
                for v in range(2):
                    chain.inc(dve.tensor_tensor(mod[:, v, cols], keep_mod.tmp(v, n), mod_mul[:, cols], ALU.mult))
                chain.wait()
            keep_mod.tmp = lambda v, n: mod_tmp[:, v, 0:n] if n <= MOD_TILES else work_b[:, v, 0:n]

            def keep_block(b):
                dve.wait_ge(mod_turned, b + 1)
                keep_mod(bank[MODB][:, 0:2 * MOD_TILES].rearrange("p (m v) -> p m v", v=2),
                         bass.ts(b + MOD_PE_BLOCKS, MOD_TILES), MOD_TILES)

            def norm(n):
                dve.wait_ge(rms_ready, n + 1)
                chain.inc(dve.reciprocal(ss[:, :], ss[:, :]))
                chain.wait()

                def low(kt):
                    dve.wait_ge(h_hi_ready, KT * n + kt + 1)
                    dve.tensor_tensor(h_lo[:, kt, :], work_a[:, kt % 2, :], h_hi[:, kt, :].bitcast(F32), ALU.subtract)\
                        .then_inc(h_lo_ready, 1)
                for kt in range(KT):
                    if kt >= 2:
                        dve.wait_ge(h_ready, KT * n + kt - 1)
                    dve.tensor_tensor(work_b[:, kt % 2, :], x[:, kt, :], ss[:, :], ALU.mult).then_inc(xn_ready, 1)
                    if kt >= 1:
                        low(kt - 1)
                low(KT - 1)
                clear_ss()

            def clear_ss():
                chain.inc(dve.memset(ss[:, :], 0.0))

            def add_sq(n, d, c):
                dve.wait_ge(squared, KT * n + d + 1)
                if isinstance(d, int) and d == 0:
                    chain.wait()
                else:
                    dve.wait_ge(square_added, KT * n + d)
                dve.tensor_tensor(ss[:, :], ss[:, :], work_a[:, c, :], ALU.add).then_inc(square_added, 1)

            def ffn(f, after):
                U, (l, h) = FFN_AT[f], divmod(f, 2)
                blk = ffn.block

                def run(first, last, body):
                    turns = (last - first) // 2
                    per = (2 * KT - 1) + 4 if f < 2 else 0
                    start = chain.base + chain.n
                    with dve.Fori(0, turns) as t:
                        chain.base, chain.n = start + t * per, 0
                        for slot in range(2):
                            s = first + 2 * t + slot
                            body(s, slot)
                            if f < 2:
                                if slot == 0:
                                    keep_block(t + (blk[0] - 1))
                                sum_mod(t + blk[0], range(4 * slot, 4 * slot + 4))
                        assert chain.n == per, (chain.n, per)
                    chain.base, chain.n = start + turns * per, 0
                    if f < 2:
                        blk[0] += turns

                def in_step(shift):
                    def body(s, slot):
                        product(f, s - 2, s - 2 + shift[0], slot)
                        split_lo(U + s, slot, "in")
                        hidden_lo(f, s - 2 + shift[0], slot, s - 2 - shift[1])
                    return body

                def out_step(kind, origin, chunk):
                    def body(s, slot):
                        d = s - 2 - origin
                        update_x(U + s - 2, l, 2 * h, d, slot)
                        split_lo(U + s, slot, kind)
                        if chunk == 1 and after[0] is not None:
                            add_in_loop(after[0], d, slot)
                    return body

                def add_in_loop(n, d, c):
                    dve.wait_ge(squared, KT * n + d + 1)
                    dve.wait_ge(square_added, KT * n + d)
                    dve.tensor_tensor(ss[:, :], ss[:, :], work_a[:, c, :], ALU.add).then_inc(square_added, 1)

                run(2, A_IN, in_step((0, 0)))
                for s in range(A_IN, A_IN + 2):
                    product(f, s - 2, s - 2, s % 2)
                    split_lo(U + s, s % 2, "outA")
                    hidden_lo(f, s - 2, s % 2, s - 2)
                run(A_IN + 2, A_OUT, out_step("outA", A_IN, 0))
                for s in range(A_OUT, A_OUT + 2):
                    update_x(U + s - 2, l, 2 * h, s - 2 - A_IN, s % 2)
                    split_lo(U + s, s % 2, "in")
                run(A_OUT + 2, B_OUT, in_step((A_IN - A_OUT, A_OUT)))
                for s in range(B_OUT, B_OUT + 2):
                    product(f, s - 2, s - 2 - A_OUT + A_IN, s % 2)
                    split_lo(U + s, s % 2, "outB")
                    hidden_lo(f, s - 2 - A_OUT + A_IN, s % 2, s - 2 - A_OUT)
                chain.wait()
                run(B_OUT + 2, FFN_UNITS, out_step("outB", B_OUT, 1))
                for d in range(KT - 2, KT):
                    update_x(U + B_OUT + d, l, 2 * h, d, d % 2)
                    if d == KT - 2 and after[1] is not None:
                        split_lo(U + FFN_UNITS, 0, after[1])
                    if after[0] is not None:
                        add_in_loop(after[0], d, d % 2)
                if f == 1:
                    keep_block(MOD_BLOCKS - 1)
                if after[0] is not None:
                    norm(after[0])
                    split_lo(U + FFN_UNITS + 1, 1, after[1])
            ffn.block = [2]

            def do(ins):
                chain.inc(ins)
                chain.wait()

            def mix_updates(n, layer, unit, last_kind):
                for d in range(KT):
                    if d % 2 == 0 and d >= 2:
                        split_lo(unit + d // 2 + 1, (unit + d // 2 + 1) % 2, "mix" if d < 6 else last_kind)
                    if d % 2 == 0:
                        dve.wait_ge(out_ready, 4 * layer + d // 2 + 1)
                        update_x(None, layer, 1, d, 0)
                    else:
                        update_x(unit + d // 2, layer, 1, d, 1)
                    add_sq(n, d, d % 2)

            def even_dve():
                n_qk = TT * (NH + NKV)

                def keep(r):
                    fill_ready(dve, EU, r)
                    u, t = divmod(r, TT)
                    src = bank[r % 4]
                    if u == 0:
                        kt_ = 0 if t == 0 else t + 1
                        dve.tensor_copy(k_tok[:, kt_, :, 0, :], src[:, 0:P].rearrange("p (g d) -> p g d", g=NKV))
                        ins = dve.tensor_copy(v_tok[:, kt_, :], src[:, P:2 * P])
                    else:
                        ins = dve.tensor_copy(q_tok[:, t, (u - 1) * 2 * P:u * 2 * P], src[:, 0:2 * P])
                    ins.then_inc(tok_kept_dve, 1)

                def split(i):
                    split_lo(EU + i, (EU + i) % 2, "mix" if i not in (6, 7) else "one")

                def q_heads(t):
                    return q_tok[:, t, :].rearrange("p (h d) -> p h d", d=HD)

                def k_heads(t):
                    return k_tok[:, 0 if t == 0 else t + 1, :, 0, :]

                def scratch(n):
                    return rot[:, 0:n * HD].rearrange("p (h d) -> p h d", d=HD)

                def squares_of(src, n, at):
                    do(dve.tensor_tensor(scratch(n), src, src, ALU.mult))
                    return dve.tensor_reduce(stat[:, at:at + n], scratch(n), AX.X, ALU.add)

                def apply(src, n, at, gain, t):
                    do(dve.tensor_tensor(src, src, stat[:, at:at + n].unsqueeze(2).to_broadcast([P, n, HD]), ALU.mult))
                    ins = dve.tensor_tensor(src, src, qk_gain[:, gain, :].unsqueeze(1).to_broadcast([P, n, HD]), ALU.mult)
                    if t > 0:
                        do(ins)
                        turn, half = scratch(n), HD // 2
                        cos, sin = (rope[:, i, t - 1, :].unsqueeze(1).to_broadcast([P, n, HD]) for i in range(2))
                        chain.inc(dve.tensor_tensor(turn[:, :, 0:half], src[:, :, half:HD], sin[:, :, 0:half], ALU.mult))
                        do(dve.tensor_tensor(turn[:, :, half:HD], src[:, :, 0:half], sin[:, :, half:HD], ALU.mult))
                        do(dve.tensor_tensor(src, src, cos, ALU.mult))
                        ins = dve.tensor_tensor(src, src, turn, ALU.add)
                    return ins

                for r in range(5):
                    keep(r)
                split(2)
                for r in range(5, 10):
                    keep(r)
                split(3)
                for r in range(10, 15):
                    keep(r)
                split(4)
                dve.wait_ge(tok_kept_dve, 15)
                for t in range(TT):
                    do(squares_of(q_heads(t), NH, t * NH))
                    last = squares_of(k_heads(t), NKV, TT * NH + t * NKV)
                    if t < TT - 1:
                        do(last)
                last.then_inc(stat_ready, 1)
                split(5)
                dve.wait_ge(root_ready, 1)
                do(dve.reciprocal(stat[:, 0:n_qk], stat[:, 0:n_qk]))
                dve.wait_ge(tok_in, 16 * 7)
                for t in range(TT):
                    do(apply(k_heads(t), NKV, TT * NH + t * NKV, 1, t))
                dve.tensor_copy(k_tok[:, :, :, 1, :], k_tok[:, :, :, 0, :]).then_inc(qk_done, 1)
                for t in range(TT):
                    if t == 2:
                        split(6)
                    last = apply(q_heads(t), NH, t * NH, 0, t)
                    if t < TT - 1:
                        do(last)
                last.then_inc(qk_done, 1)
                dve.wait_ge(qk_done, 2)
                dve.wait_ge(tok_kept_act, 10)
                for t in range(TT):
                    src = v_gate[:, t, :].rearrange("p (g c) -> p g c", g=A_GROUPS)
                    r2 = rot[:, 0:A_WIDTH].rearrange("p (g c) -> p g c", g=A_GROUPS)
                    do(dve.tensor_tensor(r2, src, src, ALU.mult))
                    last = dve.tensor_reduce(stat[:, n_qk + t * A_GROUPS:n_qk + (t + 1) * A_GROUPS], r2, AX.X, ALU.add)
                    if t < TT - 1:
                        do(last)
                last.then_inc(stat_ready, 1)
                split(7)
                dve.wait_ge(root_ready, 2)
                gate_stat = stat[:, n_qk:n_qk + TT * A_GROUPS]
                do(dve.reciprocal(gate_stat, gate_stat))
                for t in range(TT):
                    src = v_gate[:, t, :].rearrange("p (g c) -> p g c", g=A_GROUPS)
                    scale = gate_stat[:, t * A_GROUPS:(t + 1) * A_GROUPS].unsqueeze(2).to_broadcast([P, A_GROUPS, A_DIM])
                    ins = dve.tensor_tensor(src, src, scale, ALU.mult)
                ins.then_inc(qk_done, 1)
                split(8)
                split(9)
                for n in range(1, 9, 2):
                    dve.wait_ge(turned, n + 1)
                    turned_out(dve.tensor_copy, n).then_inc(turn_kept_dve, 1)

                for g in range(A_GROUPS):
                    dve.wait_ge(spatial_ready, g + 1)
                    dve.wait_ge(u_gate_kept, g + 1)
                    if g >= 1:
                        dve.wait_ge(spatial_gated, g)
                    flat = bank2[g][:, :, :].rearrange("p a b -> p (a b)")[:, 0:T].rearrange("p (t q) -> p t q", q=P)
                    sg = rot[:, :].rearrange("p (t q) -> p t q", q=P)
                    do(dve.scalar_tensor_tensor(out=sg, in0=flat, scalar=rows_t[:, 64 + g:65 + g],
                                                in1=spatial_bias[:, g, :].unsqueeze(1).to_broadcast([P, TT, P]),
                                                op0=ALU.mult, op1=ALU.add))
                    dve.tensor_tensor(u_gate[:, g, :], u_gate[:, g, :], rot[:, :], ALU.mult).then_inc(spatial_gated, 1)
                for g in range(A_GROUPS):
                    dve.wait_ge(spatial_hi, g + 1)
                    dve.tensor_tensor(hid_lo[:, g, :], u_gate[:, g, :], hid_hi[:, g, :].bitcast(F32), ALU.subtract)\
                        .then_inc(mix_done, 1)

                for i in range(N_ATT + 3):
                    if i < N_ATT:
                        k0, k1 = att_keys(i)
                        n = (k1 - k0) * P
                        dve.wait_ge(scores_ready, i + 1)
                        src = bank2[i % 2][:, 0, 0:P] if n == P else bank2[i % 2][:, :, 0:n // 2]
                        do(dve.tensor_reduce(soft[:, 0, i % 4:i % 4 + 1], src, AX.X if n == P else AX.XY, ALU.max))
                        dve.tensor_scalar(soft[:, 1, i % 4:i % 4 + 1], soft[:, 0, i % 4:i % 4 + 1], -HD ** -0.5, None,
                                          ALU.mult).then_inc(max_ready, 1)
                    if 1 <= i <= N_ATT:
                        k0, k1 = att_keys(i - 1)
                        n, c = (k1 - k0) * P, (i - 1) % 4
                        dve.wait_ge(exp_done, i)
                        do(dve.reciprocal(soft[:, 2, c:c + 1], soft[:, 2, c:c + 1]))
                        dve.tensor_scalar(prob[:, (i - 1) % 2, 0:n], prob[:, (i - 1) % 2, 0:n], soft[:, 2, c:c + 1], None,
                                          ALU.mult).then_inc(prob_ready, 1)
                    if i >= 3 and (i - 3) % NH == NH - 1:
                        t = (i - 3) // NH
                        cols = slice(t * P, (t + 1) * P)
                        dve.wait_ge(att_hi, t + 1)
                        dve.tensor_tensor(hid_lo[:, 4:8, cols], bank[6 + t % 2][:, :].rearrange("p (k t) -> p k t", k=4),
                                          hid_hi[:, 4:8, cols].bitcast(F32), ALU.subtract).then_inc(mix_done, 1)
                mix_updates(2, 0, EU + 8, "in")
                norm(2)
                split_lo(EU + MIX_EVEN_UNITS + 1, 1, "in")

            def odd_dve():
                def split(i):
                    split_lo(OU + i, (OU + i) % 2, "mix")

                def keep(f):
                    odd_tile_ready(dve, f)
                    dst, scale = (k_f, DK ** -0.5) if f < 8 else (d_f, 1.0)
                    for hf, cols in halves():
                        ins = dve.tensor_scalar(dst[:, f % 4, cols], bank[4 + 2 * (f % 2) + hf][:, 0:HALF], scale, None, ALU.mult)
                    ins.then_inc(tile_kept_dve, 1)

                def keep_v(r):
                    fill_ready(dve, OU + 4, r)
                    u, t = divmod(r, TT)
                    dve.tensor_copy(v_t[:, t, 2 * P * u:2 * P * (u + 1)], bank[r % 4][:, 0:2 * P]).then_inc(tok_kept_dve, 1)

                gate_v = gates[:, :, :].rearrange("p t (d k h) -> p t d k h", d=2, k=2)

                def rows_view(tile):
                    return tile.rearrange("p (d r) -> p d r", d=2)

                def per_dir(tile, d):
                    return tile[:, 32 * d:32 * d + TT * CH].rearrange("p (t h) -> p t h", h=CH)

                dve.wait_ge(gate_w_hi, 1)
                dve.tensor_tensor(gate_lo[:, :, :], gate_raw[:, :, :], gate_hi[:, :, :].bitcast(F32), ALU.subtract)\
                    .then_inc(gate_dve, 1)
                chain.inc(dve.memset(log_f[:, :], 0.0))
                chain.inc(dve.memset(ab[:, :, :], 0.0))
                chain.inc(dve.memset(m_start[:, :], 0.0))
                split(2)
                split(3)
                dve.wait_ge(gate_pe, 1)
                dve.wait_ge(odd_in, 16 * 5)
                do(dve.tensor_tensor(gates[:, :, :], bank[0][:, 0:16 * TT].rearrange("p (t c) -> p t c", c=16),
                                     gate_bias[:, :].unsqueeze(1).to_broadcast([P, TT, 16]), ALU.add))
                for d in range(2):
                    f = gate_v[:, :, d, 1, :]
                    ins = dve.scalar_tensor_tensor(out=gate_abs[:, :, d, :], in0=f, scalar=-1.0, in1=f, op0=ALU.mult, op1=ALU.max)
                ins.then_inc(gate_dve_abs, 1)
                dve.wait_ge(gate_act, 2)
                for d in range(2):
                    ins = dve.scalar_tensor_tensor(out=per_dir(log_f, d), in0=gate_v[:, :, d, 1, :], scalar=0.0,
                                                   in1=gate_abs[:, :, d, :], op0=ALU.min, op1=ALU.subtract)
                ins.then_inc(gate_dve, 1)
                keep(4)
                keep(5)
                split(4)
                keep(6)
                keep(7)
                split(5)
                dve.wait_ge(gate_pe, 2)
                for d in range(2):
                    b = bank[3][:, 32 * d:32 * d + TT * CH].rearrange("p (t h) -> p t h", h=CH)
                    chain.inc(dve.tensor_tensor(per_dir(ab[:, 0, :], d), gate_v[:, :, d, 0, :], b, ALU.subtract))
                    chain.inc(dve.tensor_copy(per_dir(ab[:, 1, :], d), b))
                dve.tensor_copy(log_f[:, :], bank[3][:, GR:2 * GR]).then_inc(gate_dve, 1)
                for r in range(5):
                    keep_v(r)
                split(6)
                for r in range(5, 10):
                    keep_v(r)
                split(7)
                dve.wait_ge(gate_pe, 3)
                do(dve.tensor_copy(a_rows[:, :], bank[0][0:GR, 0:P]))
                chain.inc(dve.tensor_copy(b_rows[:, :], bank[0][0:GR, P:2 * P]))
                chain.inc(dve.tensor_tensor_scan(c_rows[0:32, :], a_rows[0:32, :], a_rows[0:32, :], -1e30, ALU.max, ALU.max))
                chain.inc(dve.tensor_tensor_scan(c_rows[32:GR, ::-1], a_rows[32:GR, ::-1], a_rows[32:GR, ::-1], -1e30,
                                                 ALU.max, ALU.max))
                chain.wait()
                chain.inc(dve.tensor_copy(a_max[0:32, :], c_rows[0:32, P - 1:P].to_broadcast([32, P])))
                dve.tensor_copy(a_max[32:GR, :], c_rows[32:GR, 0:1].to_broadcast([32, P])).then_inc(gate_dve, 1)
                split(8)
                dve.wait_ge(gate_pe, 4)
                a_top = bank[1]
                for d in range(2):
                    start = TT - 1 if d else 1
                    do(dve.tensor_copy(col_view(m_start, d, start), m_given[:, d, :]))
                    order = [start + (-i if d else i) for i in range(TT - 1)]
                    for t, nxt in [(0, None)] + list(zip(order[:-1], order[1:])):
                        top = gate_abs[:, 0, 0, :]
                        do(dve.tensor_tensor(top, col_view(m_start, d, t), col_view(a_top, d, t), ALU.max))
                        dst = m_end[:, d, :] if nxt is None else col_view(m_start, d, nxt)
                        do(dve.tensor_tensor(dst, top, col_view(log_f, d, t), ALU.add))
                dve.tensor_copy(gate_abs[:, 1, 0, :], gate_abs[:, 0, 0, :]).then_inc(gate_dve, 1)
                split(9)
                keep(12)
                keep(13)
                dve.wait_ge(gate_pe, 5)
                do(dve.tensor_tensor(m_rows[:, 0, :], c_rows[:, :], bank[2][0:GR, 0:P], ALU.max))
                dve.tensor_tensor(m_rows[:, 1, :], m_rows[:, 0, :], b_rows[:, :], ALU.add).then_inc(gate_dve, 1)
                split(10)
                keep(14)
                keep(15)
                for n in range(1, 2 * TT, 2):
                    if n == 2 * TT - 1:
                        split(11)
                    dve.wait_ge(uv_ready, n + 1)
                    dve.tensor_copy(uv[:, n // 2, 2:4, :], bank[n % 4][:, :].rearrange("p (g c) -> p g c", g=2))\
                        .then_inc(uv_kept_dve, 1)
                for g in range(D_GROUPS):
                    dve.wait_ge(four_hi, g + 1)
                    b = 4 + 2 * (g % 2)
                    for src, cols, n in ((bank[b][:, :], slice(T_CTX, T), T_LAT), (bank[b + 1][:, 0:P], slice(0, T_CTX), T_CTX)):
                        ins = dve.scalar_tensor_tensor(out=hid_lo[:, 4 + g, cols], in0=src, scalar=(n * D_DIM) ** -0.5,
                                                       in1=hid_hi[:, 4 + g, cols].bitcast(F32), op0=ALU.mult, op1=ALU.subtract)
                    ins.then_inc(four_lo, 1)
                for n in range(TT + 2):
                    dve.wait_ge(k_turned, n + 1)
                    src = bank[n % 4][:, :]
                    if n < TT:
                        dve.tensor_copy(k_t[:, n, :], src).then_inc(k_kept, 1)
                    else:
                        dve.tensor_copy(state[:, n - TT, :, 0:P], src.rearrange("p (h k) -> p h k", h=CH)).then_inc(k_kept, 1)
                dve.tensor_copy(state[:, :, :, P:2 * P], n_col[:, :, :].unsqueeze(3).to_broadcast([P, 2, CH, P]))\
                    .then_inc(state_kept, 1)

                def exponents(n):
                    t, d = GROUPS[n]
                    dve.wait_ge(bcast_ready, n + 1)
                    if n >= 2:
                        dve.wait_ge(a_ready, n - 1)
                        if n - 2 in STATE_GROUPS:
                            dve.wait_ge(v_ready, n - 1)
                    for h in range(CH):
                        r = row_of(t, d, h)
                        ins = dve.scalar_tensor_tensor(out=w_in_[:, n % 2, h, :], in0=bank[0][:, h * P:(h + 1) * P],
                                                       scalar=ab[:, 0, r:r + 1], in1=masks[:, d, :],
                                                       op0=ALU.subtract, op1=ALU.add)
                    ins.then_inc(x_ready, 1)

                def weigh(n):
                    t, d = GROUPS[n]
                    c = n % 2
                    last = P - 1 if d == 0 else 0
                    dve.wait_ge(exps_done, n + 1)
                    if n >= 2:
                        dve.wait_ge(nd_ready, n - 1)
                    dve.tensor_tensor(q_w[:, c, :, :], q_f[:, :, t * P:(t + 1) * P], w_pr[:, c, :, :], ALU.mult)
                    dve.wait_ge(qk_ready, n + 1)
                    dve.tensor_tensor(a_t[:, c, :], w_in_[:, c, :, :].rearrange("p h t -> p (h t)"), bank[4][:, :], ALU.mult)\
                        .then_inc(a_ready, 1)
                    if n in STATE_GROUPS:
                        if n >= 2:
                            dve.wait_ge(st_ready, n - 1)
                        for h in range(CH):
                            w_s = w_in_[:, c, h, last:last + 1]
                            dve.tensor_scalar(v_w[:, c, h, 0:P], v_t[:, t, h * P:(h + 1) * P], w_s, None, ALU.mult)
                            ins = dve.tensor_scalar(v_w[:, c, h, P:2 * P], ones[:, :], w_s, None, ALU.mult)
                        ins.then_inc(v_ready, 1)

                def finish(n):
                    t, d = GROUPS[n]
                    c = n % 2
                    dve.wait_ge(nd_ready, n + 1)
                    do(dve.scalar_tensor_tensor(out=den[:, :], in0=bank[3][:, :], scalar=-1.0, in1=e_m[:, c, :],
                                                op0=ALU.mult, op1=ALU.max))
                    do(dve.tensor_tensor(den[:, :], den[:, :], bank[3][:, :], ALU.max))
                    do(dve.reciprocal(den[:, :], den[:, :]))
                    hs = h_sum[:, :, t * P:(t + 1) * P]
                    den4, num = (x_.rearrange("p (h t) -> p h t", h=CH) for x_ in (den[:, :], bank[2][:, :]))
                    if SEEN[n]:
                        do(dve.tensor_tensor(den4, den4, num, ALU.mult))
                        dve.tensor_tensor(hs, hs, den4, ALU.add).then_inc(h_done, 1)
                    else:
                        dve.tensor_tensor(hs, den4, num, ALU.mult).then_inc(h_done, 1)
                    dve.wait_ge(h_done, n + 1)
                    if n not in STATE_GROUPS:
                        return
                    dve.wait_ge(st_ready, n + 1)
                    if t == 0:
                        chain.inc(dve.tensor_copy(c_end[d][:, :, :], bank[6][:, :].rearrange("p (h k) -> p h k", h=CH)))
                        chain.inc(dve.tensor_copy(n_end[:, d, :], bank[7][:, 0:CH]))
                        chain.wait()
                        dve.sem_inc(end_kept, 1)
                        dve.sem_inc(st_taken, 1)
                    else:
                        last = P - 1 if d == 0 else 0
                        for h in range(CH):
                            ins = dve.scalar_tensor_tensor(out=state[:, d, h, :], in0=state[:, d, h, :],
                                                           scalar=w_pr[:, c, h, last:last + 1],
                                                           in1=bank[6 + h // 2][:, h % 2 * 2 * P:(h % 2 + 1) * 2 * P],
                                                           op0=ALU.mult, op1=ALU.add)
                        ins.then_inc(st_taken, 1)

                exponents(0)
                for n in range(NG):
                    weigh(n)
                    if n + 1 < NG:
                        exponents(n + 1)
                    finish(n)
                dve.wait_ge(h_done, NG)
                for h in range(CH):
                    dve.tensor_tensor(h_sum[:, h, :], h_sum[:, h, :], o_f[:, h, :], ALU.mult).then_inc(h_final, 1)
                for h in range(CH):
                    dve.wait_ge(c_hi, h + 1)
                    dve.tensor_tensor(hid_lo[:, h, :], h_sum[:, h, :], hid_hi[:, h, :].bitcast(F32), ALU.subtract)\
                        .then_inc(c_lo, 1)
                mix_updates(5, 1, OU + 10, "in")
                norm(5)
                split_lo(OU + MIX_ODD_UNITS + 1, 1, "in")

            dve.memset(eps[:, :], EPS)
            dve.memset(ones[:, :], 1.0).then_inc(ones_set, 1)
            chain.inc(dve.memset(mod_mul[:, :], 1.0))
            clear_ss()
            dve.wait_ge(rows_turned, 1)
            for l in range(DEPTH):
                chain.inc(dve.tensor_copy(mod_add[:, l * 72:(l + 1) * 72], bank[5][:, l * P:l * P + 72]))
            dve.tensor_copy(rows_t[:, :], bank[5][:, 2 * P:2 * P + 72]).then_inc(rows_kept, 1)
            dve.wait_ge(rows_kept, 1)
            chain.wait()
            add_v = mod_add[:, :].rearrange("p (s k c) -> p s k c", s=DEPTH * N_SUB, k=3)
            mul_v = mod_mul[:, :].rearrange("p (l j k c) -> p l j k c", l=DEPTH, j=N_SUB, k=3)
            mul_s = mod_mul[:, :].rearrange("p (s k c) -> p s k c", s=DEPTH * N_SUB, k=3)
            chain.inc(dve.tensor_scalar(add_v[:, :, 1, :], add_v[:, :, 1, :], 1.0, None, ALU.add))
            for j in (0, 2):
                chain.inc(dve.memset(mul_v[:, :, j, 2, :], 0.5))
            chain.inc(dve.tensor_copy(mul_s[:, :, 1, :], rows_t[:, 2 * KT:8 * KT].rearrange("p (s c) -> p s c", c=KT)))
            for n in range(1, 2 * TT, 2):
                dve.wait_ge(x_turned, n + 1)
                dve.tensor_copy(x[:, 4:8, n // 2 * P:(n // 2 + 1) * P],
                                bank[n % 4][:, :].rearrange("p (k t) -> p k t", k=4)).then_inc(x_kept_dve, 1)
            for d in range(KT):
                add_sq(0, d, d % 2)
            split_lo(0, 0, "in")
            dve.wait_ge(mod_first_sum, 1)
            n_first = MOD_PE_BLOCKS * MOD_TILES
            keep_mod(bank[MODB][:, 0:2 * n_first].rearrange("p (m v) -> p m v", v=2), slice(0, n_first), n_first)
            norm(0)
            split_lo(1, 1, "in")
            sum_mod(0, range(KT))
            keep_block(0)
            sum_mod(1, range(KT))
            ffn(0, (1, "mix" if mixers else "in"))
            if mixers:
                even_dve()
            ffn(1, (norm_at[2], "in"))
            ffn(2, (norm_at[2] + 1, "mix" if mixers else "in"))
            if mixers:
                odd_dve()
            ffn(3, (None, None))
            for n in range(1, 2 * TT, 2):
                dve.wait_ge(y_turned, n + 1)
                dve.tensor_copy(y_rows[:, n // 2, 4 * P:8 * P], bank[n % 4 + 4][:, :]).then_inc(y_kept_dve, 1)


def constants():
    pos = np.arange(T_LAT)
    n_freq = HEAD_DIM // 4
    inv = np.float32(ROPE_THETA) ** (-np.arange(n_freq, dtype=np.float32) / np.float32(n_freq))
    ang = np.concatenate([(pos // GRID_W).astype(np.float32)[:, None] * inv,
                          (pos % GRID_W).astype(np.float32)[:, None] * inv], axis=-1)
    sin = np.sin(ang)
    rope = np.stack([np.concatenate([np.cos(ang)] * 2, axis=-1), np.concatenate([-sin, sin], axis=-1)])
    k = np.arange(P)
    ang_c = 2 * np.pi * (k[:, None] * k % P) / P
    n = np.arange(T_LAT)
    ang_t = 2 * np.pi * (n[:, None] * n % T_LAT) / T_LAT
    after = (k[:, None] > k[None, :]).astype(np.float32)
    return {"dft_c": np.stack([np.cos(ang_c), -np.sin(ang_c), np.sin(ang_c)]).astype(np.float32),
            "dft_t": np.stack([np.cos(ang_t), np.sin(ang_t)]).astype(np.float32),
            "masks": np.stack([after * np.float32(1e30), after.T * np.float32(1e30), 1 - after, 1 - after.T]).astype(np.float32),
            "identity": np.eye(P, dtype=np.float32), "rope": rope.astype(np.float32)}


_INS = ["x_prompt", "x_sample", "c", "cache_k", "cache_v", "state_C", "state_n", "state_m", "c_ctx", "norm_gain", "w_mod",
        "b_mod", "ffn_w_in", "ffn_w_out", "w_in_even", "w_out_even", "spatial_w", "spatial_b", "sgu_gain", "q_gain",
        "k_gain", "w_in_odd", "b_gate_odd", "w_out_odd"]
_OUTS = [("y_prompt", (1, T_CTX, D)), ("y_sample", (1, T_LAT, D)),
         ("new_cache_k", (1, 1, T_CTX, B_KV, HEAD_DIM)), ("new_cache_v", (1, 1, T_CTX, B_KV, HEAD_DIM)),
         ("new_state_C", (1, 1, 2, 4, P, P)), ("new_state_n", (1, 1, 2, 4, P)), ("new_state_m", (1, 1, 2, 4))]


def kernel(**inputs):
    import concourse.bacc as bacc
    from concourse.bass_utils import run_bass_kernel_spmd

    nc = bacc.Bacc("TRN2", target_bir_lowering=False, num_devices=1)
    arrays = {name: np.ascontiguousarray(inputs[name]) for name in _INS}
    arrays.update(constants())
    given = {name: nc.dram_tensor(name, v.shape, mybir.dt.from_np(v.dtype), kind="ExternalInput").ap()
             for name, v in arrays.items()}
    out = {name: nc.dram_tensor("out_" + name, shape, F32, kind="ExternalOutput").ap() for name, shape in _OUTS}
    trunk(nc, given, out)
    r = run_bass_kernel_spmd(nc, [arrays], core_ids=[0])
    return tuple(r.results[0]["out_" + name] for name, _ in _OUTS)
```

```python
import concourse.bass as bass
from concourse import mybir
from contextlib import ExitStack
import numpy as np

F32 = mybir.dt.float32
F32R = mybir.dt.float32r
ALU = mybir.AluOpType
ACT = mybir.ActivationFunctionType
AX = mybir.AxisListType

P = 128
D = 1024
KT = D // P
T_CTX = 128
T_LAT = 512
T = T_CTX + T_LAT
TT = T // P
HALF = T // 2
DEPTH = 2
C_HEADS, C_DK, C_DV = 4, 128, 128
C_WIDTH = C_HEADS * C_DV
D_GROUPS, D_DIM = 4, 128
A_GROUPS, A_DIM = 4, 128
A_WIDTH = A_GROUPS * A_DIM
B_HEADS, B_KV, HEAD_DIM = 8, 2, 64
B_WIDTH = B_HEADS * HEAD_DIM
GRID_W, ROPE_THETA = 64, 10000.0
N_SUB = 3
D_FF = 2816
FT = D_FF // P
CHUNK_TILES = (12, 10)
FFN_UNITS = FT + 2 * KT
MIX_EVEN_UNITS = 12
MIX_ODD_UNITS = 14
EPS = 1e-6
N_MOD = 3 * N_SUB * D
MOD_COLS = 512
MOD_TILES = MOD_COLS // P
MOD_PE_BLOCKS = 3
MOD_BLOCKS = DEPTH * N_MOD // MOD_COLS - MOD_PE_BLOCKS
MC = DEPTH * N_MOD // P

FFN_AT = (0, FFN_UNITS + MIX_EVEN_UNITS, 2 * FFN_UNITS + MIX_EVEN_UNITS,
          3 * FFN_UNITS + MIX_EVEN_UNITS + MIX_ODD_UNITS)
EVEN_AT = FFN_UNITS
ODD_AT = 3 * FFN_UNITS + MIX_EVEN_UNITS


def trunk(nc, a, out):
    with ExitStack() as ctx:
        sems = {}

        def sem(name):
            sems[name] = ctx.enter_context(nc.semaphore(name))
            return sems[name]

        arena = [-(-nc.sbuf_base // 64) * 64]

        def place(name, shape, dtype=F32, at=None):
            size = int(np.prod(shape[1:])) * 4
            if at is None:
                at, arena[0] = arena[0], arena[0] + -(-size // 32) * 32
                assert arena[0] <= nc.sbuf_usable_end, (name, arena[0])
            t = nc.alloc_sbuf_tensor_at(name, shape, dtype, offset=at)
            place.at[name] = at
            return t
        place.at = {}

        x = place("x", [P, KT, T])
        h_hi = place("h_hi", [P, KT, T], F32R)
        h_lo = place("h_lo", [P, KT, T], F32R)
        hid_hi = place("hid_hi", [P, CHUNK_TILES[0], T], F32R)
        hid_lo = place("hid_lo", [P, CHUNK_TILES[0], T], F32R)
        w_raw = place("w_raw", [P, 2 * 16 * P])
        w_hi = place("w_hi", [P, 2, 16, P], F32R)
        w_lo = place("w_lo", [P, 2, 16, P], F32R)
        mod_raw = place("mod_raw", [P, KT, MOD_COLS])
        mod_acc = place("mod_acc", [P, 2, MOD_COLS])
        mod = place("mod", [P, 2, MC])
        mod_add = place("mod_add", [P, MC])
        mod_mul = place("mod_mul", [P, MC])
        mod_tmp = place("mod_tmp", [P, 2, MOD_TILES])
        silu_c = place("silu_c", [P, KT, 2])
        rows_t = place("rows_t", [P, 72])
        ident = place("ident", [P, P])
        ones = place("ones", [P, P])
        eps = place("eps", [P, 1])
        table_call = place("table_call", [P, 1])
        rms = place("rms", [P, TT])
        work_a = place("work_a", [P, 2, T])
        work_b = place("work_b", [P, 2, T])
        ss = place("ss", [P, T])

        x_rows = place("x_rows", [P, TT, D], at=place.at["h_hi"])
        y_rows = place("y_rows", [P, TT, D], at=place.at["h_hi"])
        mod_first = [place(f"mod_first{r}", [P, KT, MOD_COLS], at=place.at["hid_hi"] + r * KT * MOD_COLS * 4)
                     for r in range(MOD_PE_BLOCKS)]
        small_rows = place("small_rows", [P, 3, P], at=place.at["w_hi"])

        bank2 = [ctx.enter_context(nc.psum_tensor(f"banks{2 * i}_{2 * i + 1}", [P, 2, 512], F32)) for i in range(4)]
        bank = [bank2[i // 2][:, i % 2, :] for i in range(8)]
        MODB = 4
        token_sums = bank[MODB][:, P:P + TT]
        rms_inverse = bank2[3][:, :, :].rearrange("p a b -> p (a b)")[:, 0:T]

        consts_in = sem("consts_in")
        rows_in = sem("rows_in")
        rows_turned = sem("rows_turned")
        rows_kept = sem("rows_kept")
        silu_ready = sem("silu_ready")
        x_in = sem("x_in")
        x_turned = sem("x_turned")
        x_kept_act = sem("x_kept_act")
        x_kept_dve = sem("x_kept_dve")
        mod_first_in = [sem(f"mod_first_in{r}") for r in range(MOD_PE_BLOCKS)]
        mod_first_sum = sem("mod_first_sum")
        mod_in = sem("mod_in")
        mod_summed = sem("mod_summed")
        mod_turned = sem("mod_turned")
        raw_in = sem("raw_in")
        hi_ready = sem("hi_ready")
        lo_ready = sem("lo_ready")
        w_used = sem("w_used")
        g_ready = sem("g_ready")
        silu_done = sem("silu_done")
        prod_done = sem("prod_done")
        hid_hi_done = sem("hid_hi_done")
        hid_lo_done = sem("hid_lo_done")
        out_ready = sem("out_ready")
        x_updated = sem("x_updated")
        squared = sem("squared")
        square_added = sem("square_added")
        sums_ready = sem("sums_ready")
        rms_ready = sem("rms_ready")
        inverse_ready = sem("inverse_ready")
        inverse_spread = sem("inverse_spread")
        scaled_ready = sem("scaled_ready")
        h_hi_ready = sem("h_hi_ready")
        h_lo_ready = sem("h_lo_ready")
        dve_chain = sem("dve_chain")
        y_turned = sem("y_turned")
        y_kept_act = sem("y_kept_act")
        y_kept_dve = sem("y_kept_dve")
        stored = sem("stored")

        HD, NH, NKV = HEAD_DIM, B_HEADS, B_KV
        KEY_TILES = TT + 1
        q_tok = place("q_tok", [P, TT, NH * HD], at=place.at["hid_hi"] + KT * T * 4)
        v_gate = place("v_gate", [P, TT, A_WIDTH], at=place.at["hid_lo"] + KT * T * 4)
        u_gate = place("u_gate", [P, A_GROUPS, T], at=place.at["work_a"])
        o = place.at["mod_raw"]
        k_tok = place("k_tok", [P, KEY_TILES, NKV, 2, HD], at=o)
        v_tok = place("v_tok", [P, KEY_TILES, NKV * HD], at=o + 6144)
        spatial_t = place("spatial_t", [P, A_GROUPS, P], at=o + 9216)
        spatial_bias = place("spatial_bias", [P, A_GROUPS, P], at=o + 11264)
        rope = place("rope", [P, 2, T_LAT // P, HD], at=o + 13312)
        qk_gain = place("qk_gain", [P, 2, HD], at=o + 15360)
        assert 15872 <= KT * MOD_COLS * 4
        spatial_raw = place("spatial_raw", [P, A_GROUPS, P], at=place.at["hid_hi"])
        q_feat = place("q_feat", [P, NH // 2, T], at=place.at["h_hi"])
        k_feat = place("k_feat", [P, NKV, KEY_TILES * P], at=place.at["h_hi"] + 10240)
        PROBS = 4
        prob = place("prob", [P, PROBS, T], at=place.at["h_lo"])
        prob_t = place("prob_t", [P, 2, T], at=place.at["h_lo"] + PROBS * T * 4)
        gate_squares = place("gate_squares", [P, TT * A_GROUPS, P], at=place.at["hid_hi"] + 4096)
        rot = place("rot", [P, T])
        stat = place("stat", [P, TT * (NH + NKV) + TT * A_GROUPS])
        soft = place("soft", [P, 3, 4])

        tok_in = sem("tok_in")
        tok_ready = sem("tok_ready")
        tok_kept_dve = sem("tok_kept_dve")
        tok_kept_act = sem("tok_kept_act")
        u_gate_ready = sem("u_gate_ready")
        u_gate_kept = sem("u_gate_kept")
        stat_ready = sem("stat_ready")
        gate_stat_ready = sem("gate_stat_ready")
        root_ready = sem("root_ready")
        qk_done = sem("qk_done")
        turned = sem("turned")
        turn_kept_act = sem("turn_kept_act")
        turn_kept_dve = sem("turn_kept_dve")
        spatial_ready = sem("spatial_ready")
        spatial_gated = sem("spatial_gated")
        spatial_hi = sem("spatial_hi")
        mix_done = sem("mix_done")
        scores_ready = sem("scores_ready")
        max_ready = sem("max_ready")
        exp_done = sem("exp_done")
        prob_ready = sem("prob_ready")
        prob_turned = sem("prob_turned")
        prob_kept = sem("prob_kept")
        att_ready = sem("att_ready")
        att_hi = sem("att_hi")
        cache_stored = sem("cache_stored")

        EU = EVEN_AT
        N_TOK_UNITS = 5
        N_ATT = TT * NH

        OUT_SPLITS = {14: 8, 18: 9}

        def att_keys(i):
            return (0, 1) if i // NH == 0 else (1, KEY_TILES)
        def turned_out(copy, n, *more):
            if n < 4:
                dst = k_feat[:, :, 2 * (n - 1) * P:2 * n * P].rearrange("p g (t k) -> p t g k", t=2)
                src = bank[n % 4][:, :].rearrange("p (t g k) -> p t g k", t=2, g=2)
            else:
                dst = q_feat[:, :, (n - 4) * P:(n - 3) * P]
                src = bank[n % 4][:, :].rearrange("p (j t) -> p j t", j=4)
            return copy(dst, src, *more)


        def fill_ready(eng, base, r):
            u, t = divmod(r, TT)
            if t == TT - 1:
                eng.wait_ge(w_used, base + u + 1)
            else:
                eng.wait_ge(tok_ready, (TT - 1) * (tok_units_before(base) + u) + t + 1)

        def tok_units_before(base):
            return 0 if base == EU else N_TOK_UNITS

        def u_tile_ready(eng, m):
            if m == 0:
                eng.wait_ge(u_gate_ready, 1)
            else:
                eng.wait_ge(w_used, EU + N_TOK_UNITS + m)


        OU = ODD_AT
        CH, DK = C_HEADS, C_DK
        GR = 2 * 32
        q_f = place("q_f", [P, CH, T], at=place.at["q_tok"])
        k_f = place("k_f", [P, CH, T], at=place.at["v_gate"])
        v_t = place("v_t", [P, TT, CH * C_DV], at=place.at["mod_raw"])
        o_f = place("o_f", [P, CH, T], at=place.at["mod_raw"] + 10240)
        d_f = place("d_f", [P, D_GROUPS, T], at=place.at["work_a"])
        hh, hl = place.at["hid_hi"], place.at["hid_lo"]
        state = place("state", [P, 2, CH, P + 1], at=hh)
        gate_bias = place("gate_bias", [P, 16], at=hh + 8192)
        m_start = place("m_start", [P, GR], at=hh + 8256)
        m_end = place("m_end", [P, 2, CH], at=hh + 8512)
        m_given = place("m_given", [P, 2, CH], at=hh + 8544)
        n_end = place("n_end", [P, 2, CH], at=hh + 8576)
        masks = place("masks", [P, 4, P], at=hl)
        gate_raw = place("gate_raw", [P, KT, 16], at=hl + 2048)
        gate_hi = place("gate_hi", [P, KT, 16], F32R, at=hl + 2560)
        gate_lo = place("gate_lo", [P, KT, 16], F32R, at=hl + 3072)
        gates = place("gates", [P, TT, 16], at=hl + 3584)
        gate_abs = place("gate_abs", [P, TT, 2, CH], at=hl + 3904)
        log_f = place("log_f", [P, GR], at=hl + 4096)
        ab = place("ab", [P, 2, GR], at=hl + 4352)
        a_rows = place("a_rows", [GR, P], at=hl + 4864)
        b_rows = place("b_rows", [GR, P], at=hl + 5376)
        c_rows = place("c_rows", [GR, P], at=hl + 5888)
        m_rows = place("m_rows", [GR, 2, P], at=hl + 6400)
        a_max = place("a_max", [GR, P], at=hl + 7424)
        n_col = place("n_col", [P, 2, CH], at=hl + 7936)
        dft_t = [place(f"dft_{n}", [P, T_LAT // P, T_LAT], at=place.at[w] + 4 * T * 4)
                 for n, w in (("cos", "hid_hi"), ("sin", "hid_lo"))]
        dft_c = place("dft_c", [P, 3, P], at=hh + 4 * T * 4 + 8192)
        uv = place("uv", [P, TT, D_GROUPS, 2 * P], at=place.at["h_hi"])
        a0 = place.at["h_hi"]
        k_t = place("k_t", [P, TT, CH * DK], at=a0)
        w_intra = place("w_intra", [P, 2, CH, P], at=a0 + 10240)
        w_prev = place("w_prev", [P, 2, CH, P], at=a0 + 14336)
        a0 = place.at["h_lo"]
        e_m = place("e_m", [P, GR], at=a0)
        a_t = place("a_t", [P, 2, CH * P], at=a0 + 4096)
        q_w = place("q_w", [P, 2, CH, P], at=a0 + 8192)
        v_w = place("v_w", [P, 2, CH, P + 1], at=a0 + 12288)
        c_end = [place("c_end0", [P, CH, P], at=place.at["h_hi"] + 18432),
                 place("c_end1", [P, CH, P], at=hl + 8192)]
        h_sum = place("h_sum", [P, CH, T], at=place.at["work_a"])
        den = place("den", [P, CH], at=place.at["rot"])
        h_part = place("h_part", [P, CH * P], at=place.at["rot"] + 512)

        odd_in = sem("odd_in")
        gate_w_in = sem("gate_w_in")
        gate_w_hi = sem("gate_w_hi")
        gate_pe = sem("gate_pe")
        gate_dve = sem("gate_dve")
        gate_act = sem("gate_act")
        tile_ready = sem("tile_ready")
        tile_kept_act = sem("tile_kept_act")
        tile_kept_dve = sem("tile_kept_dve")
        dft_in = sem("dft_in")
        uv_ready = sem("uv_ready")
        uv_kept_act = sem("uv_kept_act")
        uv_kept_dve = sem("uv_kept_dve")
        four_ready = sem("four_ready")
        four_hi = sem("four_hi")
        four_lo = sem("four_lo")
        k_turned = sem("k_turned")
        k_kept = sem("k_kept")
        state_kept = sem("state_kept")
        end_kept = sem("end_kept")
        bcast_ready = sem("bcast_ready")
        x_ready = sem("x_ready")
        exps_done = sem("exps_done")
        qk_ready = sem("qk_ready")
        m_turned = sem("m_turned")
        e_m_ready = sem("e_m_ready")
        den_ready = sem("den_ready")
        den_inverted = sem("den_inverted")
        inverse_kept = sem("inverse_kept")
        a_ready = sem("a_ready")
        v_ready = sem("v_ready")
        nd_ready = sem("nd_ready")
        st_ready = sem("st_ready")
        h_done = sem("h_done")
        st_taken = sem("st_taken")
        gate_dve_abs = sem("gate_dve_abs")
        h_final = sem("h_final")
        c_hi = sem("c_hi")
        c_lo = sem("c_lo")
        state_stored = sem("state_stored")

        GROUPS = [(0, 0), (0, 1)]
        for i in range(TT - 1):
            GROUPS += [(1 + i, 0), (TT - 1 - i, 1)]
        NG = len(GROUPS)
        SEEN = [sum(g[0] == t for g in GROUPS[:n]) for n, (t, _) in enumerate(GROUPS)]
        STATE_GROUPS = [n for n in range(NG) if n < NG - 2]

        def row_of(t, d, h=0):
            return d * 32 + t * CH + h

        def col_view(tile, d, t):
            return tile[:, row_of(t, d):row_of(t, d) + CH]

        def odd_bank(f):
            return 0 if f == 1 else 4 + 2 * (f % 2)

        def odd_tile_ready(eng, f):
            unit = (0, 2, 6, 8)[f // 4] + f % 4 // 2
            if f % 2 == 0:
                eng.wait_ge(tile_ready, f // 2 + 1)
            else:
                eng.wait_ge(w_used, OU + unit + 1)

        block = ctx.enter_context(nc.Block())

        class Count:

            def __init__(self, eng, s):
                self.eng, self.s, self.base, self.n = eng, s, 0, 0

            def inc(self, ins):
                self.n += 1
                return ins.then_inc(self.s, 1)

            def wait(self, back=0):
                self.eng.wait_ge(self.s, self.base + (self.n - back))

        A_IN, B_IN = CHUNK_TILES
        A_OUT = A_IN + KT
        assert FFN_UNITS == A_OUT + B_IN + KT
        B_OUT = A_OUT + B_IN

        A_TURNS, OUT_TURNS, B_TURNS = (A_IN - 2) // 2, (KT - 2) // 2, (B_IN - 2) // 2
        PER_FFN = A_TURNS + OUT_TURNS + B_TURNS
        L1_BLOCK = 1 + PER_FFN + 2
        assert L1_BLOCK == N_MOD // MOD_COLS - MOD_PE_BLOCKS
        assert L1_BLOCK + PER_FFN + A_TURNS + 1 == MOD_BLOCKS
        MOD_PHASES = ({0: 1, 1: 1 + A_TURNS, 2: 1 + A_TURNS + OUT_TURNS},
                      {p: L1_BLOCK + o for p, o in enumerate((0, A_TURNS, A_TURNS + OUT_TURNS))},
                      {0: L1_BLOCK + PER_FFN}, {})

        def halves():
            return [(0, slice(0, HALF)), (1, slice(HALF, T))]

        norm_at = (0, 2, 3, 5)

        def out_base(f):
            return 2 * KT * f + KT * ((f > 0) + (f > 2))

        PARTS = ((0, slice(0, T_CTX)), (1, slice(T_CTX, T)))
        PIECES = ((0, 0, slice(0, T_CTX), slice(0, T_CTX)),
                  (0, 1, slice(T_CTX, HALF), slice(T_CTX, HALF)),
                  (1, 1, slice(HALF, T), slice(0, HALF)))

        def scaled(kt):
            return (work_a, work_b)[kt // 2 % 2][:, kt % 2, :]

        def mod_col(v, layer, kind, kt):
            return mod[:, v, bass.ds((layer * 3 * N_SUB + kind) * KT + kt, 1)]

        def raw_view(kind, slot):
            if kind == "mix":
                return w_raw[:, :].rearrange("p (s n c) -> p s n c", s=2, c=P)[:, slot]
            if kind == "one":
                return w_raw[:, :].rearrange("p (s n c) -> p s n c", s=2, c=2 * P)[:, slot, :, 0:P]
            n = {"in": 16, "outA": CHUNK_TILES[0], "outB": CHUNK_TILES[1]}[kind]
            return w_raw[:, :].rearrange("p (n c) -> p n c", c=2 * P)[:, 0:n, slot * P:(slot + 1) * P]

        def split_view(w, kind, slot):
            if kind == "one":
                return w[:, slot].rearrange("p (k c) q -> p k c q", c=2)[:, :, 0, :]
            return w[:, slot, 0:{"in": 16, "mix": 16, "outA": CHUNK_TILES[0], "outB": CHUNK_TILES[1]}[kind], :]

        @block.sync
        def _(sp):
            w_in = a["ffn_w_in"].rearrange("l h (k p) n -> l h p k n", p=P)
            w_out = a["ffn_w_out"].rearrange("l h (k p) n -> l h p k n", p=P)
            w_mod = a["w_mod"].rearrange("l (k p) n -> l p k n", p=P)

            def load_pair(f, kind, pair, which):
                if not (isinstance(pair, int) and pair == 0):
                    sp.wait_ge(lo_ready, 2 * pair)
                l, h = divmod(f, 2)
                if kind == "in":
                    dst = w_raw[:, :].rearrange("p (k g c) -> p k g c", k=KT, g=2)
                    for g in range(2):
                        sp.dma_start(dst[:, :, g, :], w_in[l, h][:, :, bass.ts(which + g * (FT // 2), 2 * P)])\
                            .then_inc(raw_in, 16)
                else:
                    k0, n = (0, A_IN) if kind == "outA" else (A_IN, B_IN)
                    dst = w_raw[:, :].rearrange("p (k c) -> p k c", c=2 * P)
                    for i in range(2):
                        ks = slice(i * n // 2, (i + 1) * n // 2)
                        src = w_out[l, h][:, k0 + ks.start:k0 + ks.stop, bass.ts(which, 2 * P)]
                        sp.dma_start(dst[:, ks, :], src).then_inc(raw_in, 16)

            def load_mod(b, lay):
                if not (isinstance(b, int) and b == 0):
                    sp.wait_ge(mod_summed, b)
                cols = b + (MOD_PE_BLOCKS - lay * (N_MOD // MOD_COLS))
                sp.dma_start(mod_raw[:, :, :], w_mod[lay][:, :, bass.ts(cols, MOD_COLS)]).then_inc(mod_in, 16)

            def ffn(f):
                U = FFN_AT[f] // 2

                def run(in_phase, first, last, kind, origin):
                    with sp.Fori(0, (last - first) // 2) as t:
                        load_pair(f, kind, U + first // 2 + t, t + (first - origin[0]) // 2 + origin[1])
                        if in_phase in MOD_PHASES[f]:
                            load_mod(t + MOD_PHASES[f][in_phase] + 1, (f + 1) // 2)
                run(0, 2, A_IN, "in", (0, 0))
                load_pair(f, "outA", U + A_IN // 2, 0)
                run(1, A_IN + 2, A_OUT, "outA", (A_IN, 0))
                load_pair(f, "in", U + A_OUT // 2, A_IN // 2)
                run(2, A_OUT + 2, B_OUT, "in", (A_OUT, A_IN // 2))
                load_pair(f, "outB", U + B_OUT // 2, 0)
                if f == 0:
                    load_mod(L1_BLOCK - 1, 0)
                run(3, B_OUT + 2, FFN_UNITS, "outB", (B_OUT, 0))

            def load_mix(unit, w, kts, cols):
                if unit % 2 == 0:
                    sp.wait_ge(lo_ready, unit)
                dst = w_raw[:, unit % 2 * 16 * P:(unit % 2 + 1) * 16 * P].rearrange("p (k c) -> p k c", c=2 * P)
                sp.dma_start(dst[:, 0:kts, 0:cols.stop - cols.start], w[:, :, cols]).then_inc(raw_in, 16)

            def even_sp():
                w = a["w_in_even"][0].rearrange("(k p) n -> p k n", p=P)
                wo = a["w_out_even"][0].rearrange("(k p) n -> p k n", p=P)
                AV, Q, K = A_WIDTH, 2 * A_WIDTH, 2 * A_WIDTH + B_WIDTH
                starts = [(K, 256), (Q, 256), (Q + 256, 256), (AV, 256), (AV + 256, 256), (0, 256), (256, P), (384, P)]
                sp.wait_ge(mod_summed, L1_BLOCK)
                sp.dma_start(k_tok[:, 1, :, 0, :], a["cache_k"][0, 0]).then_inc(tok_in, 16)
                sp.dma_start(v_tok[:, 1, :], a["cache_v"][0, 0].rearrange("t h d -> t (h d)")).then_inc(tok_in, 16)
                sp.dma_start(rope[:, :, :, :], a["rope"].rearrange("s (t p) d -> p s t d", p=P)).then_inc(tok_in, 16)
                for i, g in enumerate(("q_gain", "k_gain")):
                    sp.dma_start(qk_gain[:, i, :], a[g][0].partition_broadcast(P)).then_inc(tok_in, 16)
                sp.dma_start(spatial_bias[:, :, :].rearrange("p g q -> p (g q)"),
                             a["spatial_b"][0].rearrange("g q -> (g q)").partition_broadcast(P)).then_inc(tok_in, 16)
                for i, (c0, n) in enumerate(starts):
                    if i == 2:
                        sp.wait_ge(w_used, EU)
                        sp.dma_start(spatial_raw[:, :, :], a["spatial_w"][0].rearrange("g p q -> p g q"))\
                            .then_inc(tok_in, 16)
                    load_mix(EU + i, w, KT, slice(c0, c0 + n))
                for i in range(4):
                    load_mix(EU + 8 + i, wo, KT, slice(256 * i, 256 * (i + 1)))
                sp.wait_ge(qk_done, 1)
                sp.dma_start(out["new_cache_k"][0, 0], k_tok[:, 0, :, 0, :]).then_inc(cache_stored, 16)
                sp.dma_start(out["new_cache_v"][0, 0].rearrange("t h d -> t (h d)"), v_tok[:, 0, :]).then_inc(cache_stored, 16)
                sp.wait_ge(cache_stored, 32)

            def odd_sp():
                w = a["w_in_odd"][0].rearrange("(k p) n -> p k n", p=P)
                wo = a["w_out_odd"][0].rearrange("(k p) n -> p k n", p=P)
                K, V, O = CH * DK, 2 * CH * DK, 2 * CH * DK + C_WIDTH
                G = O + C_WIDTH
                DD = G + 16
                for i, c0 in enumerate((0, 256, K, K + 256, V, V + 256, O, O + 256, DD, DD + 256)):
                    load_mix(OU + i, w, KT, slice(c0, c0 + 256))
                    if i == 1:
                        sp.wait_ge(w_used, OU)
                        sp.dma_start(gate_raw[:, :, :], w[:, :, G:G + 16]).then_inc(gate_w_in, 16)
                        sp.dma_start(gate_bias[:, :], a["b_gate_odd"][0].rearrange("d k h -> (d k h)")
                                     .partition_broadcast(P)).then_inc(odd_in, 16)
                        sp.dma_start(m_given[:, :, :].rearrange("p d h -> p (d h)"),
                                     a["state_m"][0, 0].rearrange("d h -> (d h)").partition_broadcast(P)).then_inc(odd_in, 16)
                        sp.dma_start(masks[:, :, :], a["masks"].rearrange("m s t -> s m t")).then_inc(odd_in, 16)
                        with nc.allow_non_contiguous_dma(reason="1024 values of state n, one per partition"):
                            sp.dma_start(n_col[:, :, :], a["state_n"][0, 0].rearrange("d h k -> k d h")).then_inc(odd_in, 16)
                        sp.dma_start(state[:, :, :, 0:P], a["state_C"][0, 0].rearrange("d h e k -> e d h k"))\
                            .then_inc(odd_in, 16)
                    if i == 5:
                        sp.dma_start(dft_c[:, :, :], a["dft_c"].rearrange("s p n -> p s n")).then_inc(dft_in, 16)
                        for s in range(2):
                            sp.dma_start(dft_t[s][:, :, :], a["dft_t"][s].rearrange("(t p) n -> p t n", p=P)).then_inc(dft_in, 16)
                for i in range(4):
                    load_mix(OU + 10 + i, wo, KT, slice(256 * i, 256 * (i + 1)))
                for d in range(2):
                    sp.wait_ge(end_kept, d + 1)
                    sp.dma_start(out["new_state_C"][0, 0, d].rearrange("h e k -> e h k"), c_end[d][:, :, :])\
                        .then_inc(state_stored, 16)
                with nc.allow_non_contiguous_dma(reason="1024 values of state n, one per partition"):
                    sp.dma_start(out["new_state_n"][0, 0].rearrange("d h k -> k d h"), n_end[:, :, :]).then_inc(state_stored, 16)
                sp.dma_start(out["new_state_m"][0, 0].rearrange("(o d) h -> o (d h)", o=1),
                             m_end[0:1, :, :].rearrange("p d h -> p (d h)")).then_inc(state_stored, 16)
                sp.wait_ge(state_stored, 16 * 4)

            sp.dma_start(ident[:, :], a["identity"]).then_inc(consts_in, 16)
            b_rows = a["b_mod"].rearrange("l (r p) -> l r p", p=P)
            for l in range(DEPTH):
                sp.dma_start(small_rows[0:3 * N_SUB * KT, l, :], b_rows[l]).then_inc(rows_in, 16)
            sp.dma_start(small_rows[0:KT, 2, :], a["c_ctx"].rearrange("(r p) -> r p", p=P)).then_inc(rows_in, 16)
            sp.dma_start(small_rows[KT:2 * KT, 2, :], a["c"].rearrange("b (r p) -> (b r) p", p=P)).then_inc(rows_in, 16)
            sp.dma_start(small_rows[2 * KT:8 * KT, 2, :], a["norm_gain"].rearrange("l s (r p) -> (l s r) p", p=P))\
                .then_inc(rows_in, 16)
            sp.dma_start(small_rows[64:68, 2, :], a["sgu_gain"].rearrange("e g p -> (e g) p")).then_inc(rows_in, 16)
            sp.dma_start(small_rows[68:72, 2, :], a["identity"][0:4, :]).then_inc(rows_in, 16)
            sp.dma_start(x_rows[:, 0, :], a["x_prompt"][0]).then_inc(x_in, 16)
            sp.dma_start(x_rows[:, 1:TT, :], a["x_sample"][0].rearrange("(t p) d -> p t d", p=P)).then_inc(x_in, 16)
            for r in range(MOD_PE_BLOCKS):
                sp.dma_start(mod_first[r][:, :, :], w_mod[0][:, :, r * MOD_COLS:(r + 1) * MOD_COLS])\
                    .then_inc(mod_first_in[r], 16)
            load_mod(0, 0)
            load_pair(0, "in", 0, 0)
            load_mod(1, 0)
            ffn(0)
            even_sp()
            load_pair(1, "in", FFN_AT[1] // 2, 0)
            load_mod(L1_BLOCK, 1)
            ffn(1)
            load_pair(2, "in", FFN_AT[2] // 2, 0)
            ffn(2)
            odd_sp()
            load_pair(3, "in", FFN_AT[3] // 2, 0)
            ffn(3)
            for t in range(TT):
                sp.wait_ge(y_kept_act, t + 1)
                sp.wait_ge(y_kept_dve, t + 1)
                dst = out["y_prompt"][0] if t == 0 else out["y_sample"][0][(t - 1) * P:t * P, :]
                sp.dma_start(dst, y_rows[:, t, :]).then_inc(stored, 16)
            sp.wait_ge(stored, 16 * TT)

        @block.tensor
        def _(pe):
            def split_product(outs, w3, v3, first, last):
                for i, (w, v) in enumerate(((0, 0), (0, 1), (1, 0))):
                    for o, cols in outs:
                        ins = pe.matmul(o, w3[w], v3[v][cols], start=first and i == 0, stop=last and i == 2)
                return ins

            def in_unit(f, s, slot, i, fresh=False):
                n = 22 * f + i
                pe.wait_ge(lo_ready, FFN_AT[f] + s + 1)
                if isinstance(i, int) and i == A_IN:
                    pe.wait_ge(x_updated, out_base(f) + KT)
                elif not (isinstance(i, int) and i == 0):
                    pe.wait_ge(silu_done, n)
                order = [(g, kt) for kt in range(KT) for g in range(2)] if fresh else \
                    [(g, kt) for g in range(2) for kt in range(KT)]
                for g, kt in order:
                    if (g, kt) == (1, 0) and not (isinstance(i, int) and i in (0, A_IN)):
                        pe.wait_ge(prod_done, n)
                    if fresh and g == 0:
                        pe.wait_ge(h_lo_ready, 8 * norm_at[f] + kt + 1)
                    t = 2 * kt + g
                    ins = split_product(
                        [(bank[2 * g + hf][:, 0:HALF], (slice(None), kt, cols)) for hf, cols in halves()],
                        (w_hi[:, slot, t, :], w_lo[:, slot, t, :]), (h_hi, h_lo), kt == 0, kt == KT - 1)
                    if kt == KT - 1:
                        ins.then_inc(g_ready if g == 0 else w_used, 1)

            def out_unit(f, s, slot, kd, chunk):
                pe.wait_ge(lo_ready, FFN_AT[f] + s + 1)
                first = isinstance(kd, int) and kd == 0
                if first:
                    pe.wait_ge(silu_done, 22 * f + (A_IN, FT)[chunk])
                elif isinstance(kd, int) and kd == 1:
                    pe.wait_ge(prod_done, 22 * f + (A_IN, FT)[chunk])
                else:
                    pe.wait_ge(x_updated, out_base(f) + 8 * chunk + kd - 1)
                n = CHUNK_TILES[chunk]
                for k in range(n):
                    if first:
                        pe.wait_ge(hid_lo_done, 22 * f + (0, A_IN)[chunk] + k + 1)
                    ins = split_product(
                        [(bank[2 * slot + hf][:, 0:HALF], (slice(None), k, cols)) for hf, cols in halves()],
                        (w_hi[:, slot, k, :], w_lo[:, slot, k, :]), (hid_hi, hid_lo), k == 0, k == n - 1)
                ins.then_inc(w_used, 1)

            def turn_mod(b):
                pe.wait_ge(mod_summed, b + 1)
                for m in range(MOD_TILES):
                    for v in range(2):
                        ins = pe.matmul(bank[MODB][:, 2 * m + v:2 * m + v + 1], mod_acc[:, v, m * P:(m + 1) * P],
                                        ones[:, 0:1], start=True, stop=True)
                ins.then_inc(mod_turned, 1)

            def sum_squares(n):
                pe.wait_ge(square_added, KT * (n + 1))
                for t in range(TT):
                    ins = pe.matmul(token_sums[:, t:t + 1], ss[:, t * P:(t + 1) * P], ones[:, 0:1], start=True, stop=True)
                ins.then_inc(sums_ready, 1)

            def spread_inverse(n):
                pe.wait_ge(inverse_ready, n + 1)
                for t in range(TT):
                    ins = pe.matmul(rms_inverse[:, t * P:(t + 1) * P], rms[:, t:t + 1].to_broadcast([P, P]), ident[:, :],
                                    start=True, stop=True)
                ins.then_inc(inverse_spread, 1)

            def ffn(f):
                def run(phase, first, last, body):
                    with pe.Fori(0, (last - first) // 2) as t:
                        if phase in MOD_PHASES[f]:
                            turn_mod(t + MOD_PHASES[f][phase])
                        for slot in range(2):
                            body(first + 2 * t + slot, slot)
                for s in range(2):
                    in_unit(f, s, s, s, fresh=s == 0)
                    if f == 1 and s == 0:
                        turn_mod(L1_BLOCK - 1)
                run(0, 2, A_IN, lambda s, slot: in_unit(f, s, slot, s))
                for s in range(A_IN, A_IN + 2):
                    if f == 2 and s == A_IN:
                        turn_mod(MOD_BLOCKS - 1)
                    out_unit(f, s, s % 2, s - A_IN, 0)
                run(1, A_IN + 2, A_OUT, lambda s, slot: out_unit(f, s, slot, s - A_IN, 0))
                for s in range(A_OUT, A_OUT + 2):
                    in_unit(f, s, s % 2, s - A_OUT + A_IN)
                run(2, A_OUT + 2, B_OUT, lambda s, slot: in_unit(f, s, slot, s - (A_OUT - A_IN)))
                for s in range(B_OUT, B_OUT + 2):
                    if f == 0 and s == B_OUT:
                        turn_mod(L1_BLOCK - 2)
                    out_unit(f, s, s % 2, s - B_OUT, 1)
                run(3, B_OUT + 2, FFN_UNITS, lambda s, slot: out_unit(f, s, slot, s - B_OUT, 1))

            def first_out_pair(unit, early, late, banks_free, late_ready):
                slot = unit % 2
                pe.wait_ge(lo_ready, unit + 1)
                for ks in (early, late):
                    for i in range(2):
                        if ks is early and i == 1:
                            banks_free()
                        for k in ks:
                            if ks is late and i == 0:
                                late_ready(k)
                            ins = split_product(
                                [(bank[2 * i + hf][:, 0:HALF], (slice(None), k, cols)) for hf, cols in halves()],
                                (w_hi[:, slot, 2 * k + i, :], w_lo[:, slot, 2 * k + i, :]), (hid_hi, hid_lo),
                                k == early[0], k == late[-1])
                        if ks is late:
                            ins.then_inc(out_ready if i == 0 else w_used, 1)

            def out_pair(unit, ready_x, first):
                slot = unit % 2
                pe.wait_ge(lo_ready, unit + 1)
                for i in range(2):
                    if ready_x + i >= first + 2:
                        pe.wait_ge(x_updated, ready_x + i - 1)
                    for k in range(KT):
                        ins = split_product(
                            [(bank[2 * i + hf][:, 0:HALF], (slice(None), k, cols)) for hf, cols in halves()],
                            (w_hi[:, slot, 2 * k + i, :], w_lo[:, slot, 2 * k + i, :]), (hid_hi, hid_lo), k == 0, k == KT - 1)
                    ins.then_inc(out_ready if i == 0 else w_used, 1)

            def token_unit(unit, fill0, fresh, taken):
                slot = unit % 2
                pe.wait_ge(lo_ready, unit + 1)
                wh, wl = (w[:, slot].rearrange("p (k c) q -> p k (c q)", c=2) for w in (w_hi, w_lo))
                order = [(t, kt) for t in range(TT) for kt in range(KT)]
                if fresh is not None:
                    order = [(t, kt) for kt in range(KT) for t in range(4)] + order[4 * KT:]
                for t, kt in order:
                    if kt == 0:
                        taken(fill0 + t)
                    if fresh is not None and t == 0:
                        pe.wait_ge(h_lo_ready, KT * fresh + kt + 1)
                    cols = slice(t * P, (t + 1) * P)
                    dst = bank[(fill0 + t) % 4][:, 0:2 * P]
                    pe.matmul(dst, h_hi[:, kt, cols], wh[:, kt, :], start=kt == 0, stop=False)
                    pe.matmul(dst, h_hi[:, kt, cols], wl[:, kt, :], start=False, stop=False)
                    ins = pe.matmul(dst, h_lo[:, kt, cols], wh[:, kt, :], start=False, stop=kt == KT - 1)
                    if kt == KT - 1:
                        ins.then_inc(tok_ready if t < TT - 1 else w_used, 1)

            def feature_tile(unit, i, banks, last_sem):
                slot = unit % 2
                if i == 0:
                    pe.wait_ge(lo_ready, unit + 1)
                for kt in range(KT):
                    ins = split_product(
                        [(bank[banks + hf][:, 0:HALF], (slice(None), kt, cols)) for hf, cols in halves()],
                        (w_hi[:, slot, 2 * kt + i, :], w_lo[:, slot, 2 * kt + i, :]), (h_hi, h_lo), kt == 0, kt == KT - 1)
                ins.then_inc(last_sem, 1)

            def even_pe():
                def taken(r):
                    if r - 4 >= 15:
                        pe.wait_ge(tok_kept_act, r - 4 - 15 + 1)
                    elif r >= 4:
                        pe.wait_ge(tok_kept_dve, r - 4 + 1)
                for u in range(N_TOK_UNITS):
                    token_unit(EU + u, TT * u, 1 if u == 0 else None, taken)
                for m, (u, i) in enumerate(((5, 0), (5, 1), (6, 0), (7, 0))):
                    if m >= 2:
                        pe.wait_ge(u_gate_kept, m - 1)
                    feature_tile(EU + u, i, 4 + 2 * (m % 2), u_gate_ready if m == 0 else w_used)

                def turn(n, blocks):
                    if n >= 4:
                        pe.wait_ge(turn_kept_act if n % 2 == 0 else turn_kept_dve, (n - 4) // 2 + 1)
                    for j, src in enumerate(blocks):
                        ins = pe.transpose(bank[n % 4][:, j * P:(j + 1) * P], src, ident[:, :])
                    ins.then_inc(turned, 1)
                pe.wait_ge(tok_in, 16 * 7)
                pe.wait_ge(tok_kept_act, 10)
                turn(0, [spatial_raw[:, g, :] for g in range(A_GROUPS)])
                pe.wait_ge(qk_done, 1)
                for n in range(3):
                    turn(1 + n, [k_tok[:, 2 * n + j // 2, j % 2, :, :].rearrange("p a d -> p (a d)") for j in range(4)])
                pe.wait_ge(qk_done, 2)
                for t in range(TT):
                    turn(4 + t, [q_tok[:, t, j * P:(j + 1) * P] for j in range(NH // 2)])

                pe.wait_ge(qk_done, 3)
                pe.wait_ge(turn_kept_act, 5)
                pe.wait_ge(turn_kept_dve, 4)
                pe.wait_ge(u_gate_kept, 4)
                for g in range(A_GROUPS):
                    for t in range(TT):
                        ins = pe.matmul(bank[2 * g + t // 4][:, t % 4 * P:(t % 4 + 1) * P],
                                        v_gate[:, t, g * P:(g + 1) * P], spatial_t[:, g, :], start=True, stop=True)
                    ins.then_inc(spatial_ready, 1)

                def scores(i):
                    t, h = divmod(i, NH)
                    k0, k1 = att_keys(i)
                    if i < 2:
                        pe.wait_ge(spatial_gated, i + 1)
                    else:
                        pe.wait_ge(exp_done, i - 1)
                    rows = slice(h % 2 * HD, (h % 2 + 1) * HD)
                    q = q_feat[rows, h // 2, t * P:(t + 1) * P]
                    n = (k1 - k0) * P
                    parts = [slice(0, n)] if n <= 512 else [slice(0, n // 2), slice(n // 2, n)]
                    for j, c in enumerate(parts):
                        ins = pe.matmul(bank[2 * (i % 2) + j][:, 0:c.stop - c.start], q,
                                        k_feat[rows, h // (NH // NKV), k0 * P + c.start:k0 * P + c.stop],
                                        start=True, stop=True)
                    ins.then_inc(scores_ready, 1)

                def turn_probs(i):
                    k0, k1 = att_keys(i)
                    pe.wait_ge(prob_ready, i + 1)
                    if i == 0:
                        pe.wait_ge(spatial_gated, 3)
                    else:
                        pe.wait_ge(prob_kept, i)
                    for j in range(k1 - k0):
                        ins = pe.transpose(bank[4 + j // 4][:, j % 4 * P:(j % 4 + 1) * P],
                                           prob[:, i % PROBS, j * P:(j + 1) * P], ident[:, :])
                    ins.then_inc(prob_turned, 1)

                def values(i):
                    t, h = divmod(i, NH)
                    k0, k1 = att_keys(i)
                    pe.wait_ge(prob_kept, i + 1)
                    if h == 0:
                        if t == 0:
                            pe.wait_ge(spatial_gated, 4)
                        elif t >= 2:
                            pe.wait_ge(mix_done, A_GROUPS + t - 1)
                    g = h // (NH // NKV)
                    for j in range(k1 - k0):
                        ins = pe.matmul(bank[6 + t % 2][h % 2 * HD:(h % 2 + 1) * HD, h // 2 * P:(h // 2 + 1) * P],
                                        v_tok[:, k0 + j, g * HD:(g + 1) * HD], prob_t[:, i % 2, j * P:(j + 1) * P],
                                        start=j == 0, stop=j == k1 - k0 - 1)
                    if h == NH - 1:
                        ins.then_inc(att_ready, 1)

                for i in range(N_ATT + 3):
                    if i < N_ATT:
                        scores(i)
                    if i >= 3:
                        values(i - 3)
                    if 2 <= i <= N_ATT + 1:
                        turn_probs(i - 2)

                pe.wait_ge(mix_done, A_GROUPS)
                first_out_pair(EU + 8, range(A_GROUPS), range(A_GROUPS, KT), lambda: None,
                               lambda k: pe.wait_ge(mix_done, A_GROUPS + TT))
                for i in range(1, 4):
                    out_pair(EU + 8 + i, out_base(1) - KT + 2 * i, out_base(1) - KT)

            def odd_pe():
                def first_pair(unit):
                    pe.wait_ge(lo_ready, unit + 1)
                    for kt in range(KT):
                        pe.wait_ge(h_lo_ready, KT * 4 + kt + 1)
                        for i in range(2):
                            ins = split_product(
                                [(bank[odd_bank(i) + hf][:, 0:HALF], (slice(None), kt, cols)) for hf, cols in halves()],
                                (w_hi[:, unit % 2, 2 * kt + i, :], w_lo[:, unit % 2, 2 * kt + i, :]), (h_hi, h_lo),
                                kt == 0, kt == KT - 1)
                            if kt == KT - 1:
                                ins.then_inc(tile_ready if i == 0 else w_used, 1)

                def feature_pair(unit, f0):
                    for i in range(2):
                        f = f0 + i
                        if f >= 2:
                            kind, n = (f - 2) // 4, (f - 2) % 4
                            pe.wait_ge(tile_kept_act if kind in (0, 2) else tile_kept_dve, (kind // 2) * 4 + n + 1)
                        feature_tile(unit, i, odd_bank(f), tile_ready if i == 0 else w_used)

                def taken(r):
                    if r < 4:
                        pe.wait_ge(gate_dve, 1 if r < 3 else 3)
                    else:
                        pe.wait_ge(tok_kept_dve, 15 + r - 4 + 1)

                first_pair(OU)
                feature_pair(OU + 1, 2)
                pe.wait_ge(gate_dve, 1)
                for t in range(TT):
                    cols = slice(t * P, (t + 1) * P)
                    for kt in range(KT):
                        for i, (hx, gx) in enumerate(((h_hi, gate_hi), (h_hi, gate_lo), (h_lo, gate_hi))):
                            ins = pe.matmul(bank[0][:, 16 * t:16 * t + 16], hx[:, kt, cols], gx[:, kt, :],
                                            start=kt == 0 and i == 0, stop=kt == KT - 1 and i == 2)
                ins.then_inc(gate_pe, 1)
                feature_pair(OU + 2, 4)
                feature_pair(OU + 3, 6)
                pe.wait_ge(gate_dve, 2)
                for d in range(2):
                    pe.matmul(bank[3][:, 32 * d:32 * (d + 1)], masks[:, 2 + d, :], log_f[:, 32 * d:32 * (d + 1)],
                              start=True, stop=True)
                pe.matmul(bank[3][:, GR:2 * GR], ones[:, :], log_f[:, :], start=True, stop=True).then_inc(gate_pe, 1)
                for u in range(2):
                    token_unit(OU + 4 + u, TT * u, None, taken)
                pe.wait_ge(tok_kept_dve, 25)
                for i in range(2):
                    ins = pe.transpose(bank[0][0:GR, i * P:(i + 1) * P], ab[:, i, :], ident[:, :])
                ins.then_inc(gate_pe, 1)
                feature_pair(OU + 6, 8)
                pe.wait_ge(gate_dve, 4)
                pe.matmul(bank[1][:, 0:GR], a_max[:, :], ident[0:GR, 0:GR], start=True, stop=True).then_inc(gate_pe, 1)
                feature_pair(OU + 7, 10)
                pe.wait_ge(gate_dve, 5)
                pe.transpose(bank[2][0:GR, 0:P], m_start[:, :], ident[:, :]).then_inc(gate_pe, 1)
                feature_pair(OU + 8, 12)
                feature_pair(OU + 9, 14)

                pe.wait_ge(dft_in, 48)
                pe.wait_ge(gate_dve, 6)
                pe.wait_ge(tile_kept_dve, 8)
                for n in range(2 * TT):
                    t, g0 = n // 2, n % 2 * 2
                    if n >= 4:
                        pe.wait_ge(uv_kept_act if n % 2 == 0 else uv_kept_dve, (n - 4) // 2 + 1)
                    for j in range(2):
                        ins = pe.matmul(bank[n % 4][:, 2 * P * j:2 * P * (j + 1)], d_f[:, g0 + j, t * P:(t + 1) * P],
                                        dft_c[:, 0:2, :].rearrange("p s n -> p (s n)"), start=True, stop=True)
                    ins.then_inc(uv_ready, 1)
                pe.wait_ge(uv_kept_act, TT)
                pe.wait_ge(uv_kept_dve, TT)
                for g in range(D_GROUPS):
                    for t in range(1, TT):
                        for s in range(2):
                            pe.matmul(bank[4 + g][:, :], uv[:, t, g, s * P:(s + 1) * P], dft_t[s][:, t - 1, :],
                                      start=t == 1 and s == 0, stop=t == TT - 1 and s == 1)
                    for s in range(2):
                        ins = pe.matmul(bank[3][:, g * P:(g + 1) * P], uv[:, 0, g, s * P:(s + 1) * P], dft_c[:, 2 * s, :],
                                        start=s == 0, stop=s == 1)
                ins.then_inc(four_ready, 1)

                for n in range(TT + 2):
                    if n == 3:
                        pe.wait_ge(four_lo, 1)
                    elif n >= 4:
                        pe.wait_ge(k_kept, n - 3)
                    for h in range(CH):
                        src = k_f[:, h, n * P:(n + 1) * P] if n < TT else state[:, n - TT, h, 0:P]
                        if n == TT and h == 0:
                            pe.wait_ge(odd_in, 16 * 5)
                        ins = pe.transpose(bank[n % 4][:, h * P:(h + 1) * P], src, ident[:, :])
                    ins.then_inc(k_turned, 1)

                def bcast(n):
                    t, d = GROUPS[n]
                    if n >= 2:
                        pe.wait_ge(exps_done, n - 1)
                    for h in range(CH):
                        r = row_of(t, d, h)
                        ins = pe.matmul(bank[n % 2][:, h * P:(h + 1) * P], ident[0:GR, r:r + 1].to_broadcast([GR, P]),
                                        m_rows[:, 0, :], start=True, stop=True)
                    ins.then_inc(bcast_ready, 1)

                def keys_queries(n):
                    t, d = GROUPS[n]
                    if n >= 1:
                        pe.wait_ge(a_ready, n)
                    for h in range(CH):
                        cols = slice(t * P, (t + 1) * P)
                        ins = pe.matmul(bank[4][:, h * P:(h + 1) * P], k_f[:, h, cols], q_f[:, h, cols],
                                        start=True, stop=True)
                    ins.then_inc(qk_ready, 1)

                def denominators(n):
                    t, d = GROUPS[n]
                    given = t > 0
                    pe.wait_ge(a_ready, n + 1)
                    if given:
                        if n >= 4:
                            pe.wait_ge(st_taken, n - 1)
                        else:
                            pe.wait_ge(state_kept, 1)
                    for h in range(CH):
                        ins = pe.matmul(bank[5][:, h:h + 1], a_t[:, n % 2, h * P:(h + 1) * P], ones[:, 0:1],
                                        start=True, stop=not given)
                        if given:
                            ins = pe.matmul(bank[5][:, h:h + 1], q_w[:, n % 2, h, :], state[:, d, h, P:P + 1],
                                            start=False, stop=True)
                    ins.then_inc(den_ready, 1)

                def numerators(n):
                    t, d = GROUPS[n]
                    if n >= 1:
                        pe.wait_ge(h_done, n)
                    for h in range(CH):
                        hp = slice(h * P, (h + 1) * P)
                        pe.matmul(bank[2][:, hp], v_t[:, t, hp], a_t[:, n % 2, hp], start=True, stop=t == 0)
                        if t > 0:
                            pe.matmul(bank[2][:, hp], state[:, d, h, 0:P], q_w[:, n % 2, h, :], start=False, stop=True)

                def spread(n):
                    pe.wait_ge(den_inverted, n + 1)
                    for h in range(CH):
                        ins = pe.matmul(bank[3][:, h * P:(h + 1) * P], den[:, h:h + 1].to_broadcast([P, P]), ident[:, :],
                                        start=True, stop=True)
                    ins.then_inc(nd_ready, 1)

                def states(n):
                    if n not in STATE_GROUPS:
                        return
                    t, d = GROUPS[n]
                    c = n % 2
                    pe.wait_ge(v_ready, n + 1)
                    if n >= 1:
                        pe.wait_ge(st_taken, n)
                    for h in range(CH):
                        k_h = k_t[:, t, h * P:(h + 1) * P]
                        if t > 0:
                            ins = pe.matmul(bank[6 + h // 2][:, h % 2 * 2 * P:h % 2 * 2 * P + P + 1], k_h, v_w[:, c, h, :],
                                            start=True, stop=True)
                        else:
                            pe.matmul(bank[6][:, h * P:(h + 1) * P], v_w[:, c, h, 0:P], k_h, start=True, stop=True)
                            ins = pe.matmul(bank[7][:, h:h + 1], k_h, v_w[:, c, h, P:P + 1], start=True, stop=True)
                    ins.then_inc(st_ready, 1)

                pe.wait_ge(k_kept, TT + 2)
                pe.wait_ge(four_lo, 1 + D_GROUPS)
                pe.transpose(bank[5][:, GR:2 * GR], m_rows[:, 1, :], ident[0:GR, 0:GR]).then_inc(m_turned, 1)
                bcast(0)
                keys_queries(0)
                bcast(1)
                pe.wait_ge(e_m_ready, 1)
                for n in range(NG):
                    if n + 1 < NG:
                        keys_queries(n + 1)
                    denominators(n)
                    numerators(n)
                    if n + 2 < NG:
                        bcast(n + 2)
                    spread(n)
                    states(n)
                pe.wait_ge(four_lo, 1 + D_GROUPS)
                first_out_pair(OU + 10, range(CH, KT), range(CH), lambda: pe.wait_ge(h_done, NG),
                               lambda k: pe.wait_ge(c_lo, k + 1))
                for i in range(1, 4):
                    out_pair(OU + 10 + i, out_base(3) - KT + 2 * i, out_base(3) - KT)

            pe.wait_ge(consts_in, 16)
            pe.wait_ge(rows_in, 16 * 7)
            for r in range(3):
                ins = pe.transpose(bank[5][:, r * P:r * P + 72], small_rows[0:72, r, :], ident[0:72, 0:72])
            ins.then_inc(rows_turned, 1)
            pe.wait_ge(x_in, 32)
            for n in range(2 * TT):
                t, half = divmod(n, 2)
                if n >= 4:
                    pe.wait_ge(x_kept_act if n % 2 == 0 else x_kept_dve, (n - 4) // 2 + 1)
                for q in range(4):
                    kt = 4 * half + q
                    ins = pe.transpose(bank[n % 4][:, q * P:(q + 1) * P], x_rows[:, t, kt * P:(kt + 1) * P], ident[:, :])
                ins.then_inc(x_turned, 1)
            pe.wait_ge(silu_ready, 1)
            for r in range(MOD_PE_BLOCKS):
                pe.wait_ge(mod_first_in[r], 16)
                for m in range(MOD_TILES):
                    o = 2 * (MOD_TILES * r + m)
                    for kt in range(KT):
                        ins = pe.matmul(bank[5][:, o:o + 2], mod_first[r][:, kt, m * P:(m + 1) * P],
                                        silu_c[:, kt, :], start=kt == 0, stop=kt == KT - 1)
                if r == 1:
                    sum_squares(0)
            ins.then_inc(mod_first_sum, 1)
            spread_inverse(0)
            turn_mod(0)
            ffn(0)
            sum_squares(1)
            spread_inverse(1)
            even_pe()
            sum_squares(2)
            spread_inverse(2)
            ffn(1)
            sum_squares(norm_at[2])
            spread_inverse(norm_at[2])
            ffn(2)
            sum_squares(norm_at[2] + 1)
            spread_inverse(norm_at[2] + 1)
            odd_pe()
            sum_squares(5)
            spread_inverse(5)
            ffn(3)
            pe.wait_ge(x_updated, out_base(3) + 16)
            for n in range(2 * TT):
                t, half = divmod(n, 2)
                if n >= 4:
                    pe.wait_ge(y_kept_act if n % 2 == 0 else y_kept_dve, (n - 4) // 2 + 1)
                for q in range(4):
                    kt = 4 * half + q
                    ins = pe.transpose(bank[n % 4 + 4][:, q * P:(q + 1) * P], x[:, kt, t * P:(t + 1) * P], ident[:, :])
                ins.then_inc(y_turned, 1)

        @block.scalar
        def _(act):
            def split_hi(u, slot, pair, kind):
                act.wait_ge(raw_in, 32 * (pair + 1))
                if not (isinstance(u, int) and u < 2):
                    act.wait_ge(w_used, u - 1)
                act.activation(split_view(w_hi, kind, slot), raw_view(kind, slot), ACT.Copy).then_inc(hi_ready, 1)

            def silu(f, i, c):
                act.wait_ge(g_ready, 22 * f + i + 1)
                for hf, cols in halves():
                    ins = act.activation(work_a[:, c, cols], bank[hf][:, 0:HALF], ACT.Silu)
                ins.then_inc(silu_done, 1)

            def hidden_hi(f, i, c, k):
                act.wait_ge(prod_done, 22 * f + i + 1)
                act.activation(hid_hi[:, k, :], work_b[:, c, :], ACT.Copy).then_inc(hid_hi_done, 1)

            def square(n, d, c):
                if not (isinstance(d, int) and d < 2):
                    act.wait_ge(square_added, KT * n + d - 1)
                act.activation(work_a[:, c, :], x[:, d, :], ACT.Square).then_inc(squared, 1)

            def norm(n, unit, kind):
                l, j = divmod(n, N_SUB)
                act.activation(table_call[:, :], eps[:, :], ACT.Sqrt)
                act.wait_ge(sums_ready, n + 1)
                act.activation(rms[:, :], token_sums, ACT.Sqrt, scale=1.0 / D, bias=eps[:, 0:1]).then_inc(rms_ready, 1)
                split_hi(unit, 1, unit // 2, kind)
                for kt in range(KT):
                    act.wait_ge(scaled_ready, KT * n + kt + 1)
                    for v, cols in PARTS:
                        ins = act.activation(h_hi[:, kt, cols], scaled(kt)[:, cols], ACT.Identity, bias=mod_col(v, l, 3 * j, kt))
                    ins.then_inc(h_hi_ready, 1)

            def ffn(f, after):
                U = FFN_AT[f]

                def run(first, last, body):
                    with act.Fori(0, (last - first) // 2) as t:
                        for slot in range(2):
                            body(first + 2 * t + slot, slot, U // 2 + first // 2 + t)

                def in_step(shift):
                    def body(s, slot, pair):
                        split_hi(U + s, slot, pair, "in")
                        hidden_hi(f, s - 2 + shift[0], slot, s - 2 - shift[1])
                        silu(f, s - 1 + shift[0], 1 - slot)
                    return body

                def out_step(kind, origin, final):
                    def body(s, slot, pair):
                        split_hi(U + s, slot, pair, kind)
                        if final:
                            d = s - 2 - origin
                            act.wait_ge(x_updated, out_base(f) + 8 + d + 1)
                            square_in_loop(d, slot)
                    return body

                def square_in_loop(d, c):
                    if after[0] is not None:
                        act.wait_ge(square_added, KT * after[0] + d - 1)
                        act.activation(work_a[:, c, :], x[:, d, :], ACT.Square).then_inc(squared, 1)

                silu(f, 0, 0)
                run(2, A_IN, in_step((0, 0)))
                split_hi(U + A_IN, 0, (U + A_IN) // 2, "outA")
                hidden_hi(f, A_IN - 2, 0, A_IN - 2)
                silu(f, A_IN - 1, 1)
                split_hi(U + A_IN + 1, 1, (U + A_IN) // 2, "outA")
                hidden_hi(f, A_IN - 1, 1, A_IN - 1)
                run(A_IN + 2, A_OUT, out_step("outA", A_IN, False))
                split_hi(U + A_OUT, 0, (U + A_OUT) // 2, "in")
                split_hi(U + A_OUT + 1, 1, (U + A_OUT) // 2, "in")
                silu(f, A_IN, 0)
                run(A_OUT + 2, B_OUT, in_step((A_IN - A_OUT, A_OUT)))
                split_hi(U + B_OUT, 0, (U + B_OUT) // 2, "outB")
                hidden_hi(f, FT - 2, 0, B_IN - 2)
                silu(f, FT - 1, 1)
                split_hi(U + B_OUT + 1, 1, (U + B_OUT) // 2, "outB")
                hidden_hi(f, FT - 1, 1, B_IN - 1)
                run(B_OUT + 2, FFN_UNITS, out_step("outB", B_OUT, True))
                for d in range(KT - 2, KT):
                    if d == KT - 2 and after[1] is not None:
                        split_hi(U + FFN_UNITS, 0, (U + FFN_UNITS) // 2, after[1])
                    act.wait_ge(x_updated, out_base(f) + 8 + d + 1)
                    square_in_loop(d, d % 2)
                if after[0] is not None:
                    norm(after[0], U + FFN_UNITS + 1, after[1])

            def mix_squares(n, base, unit, last_kind):
                for d in range(KT):
                    if d % 2 == 0 and d >= 2:
                        split_hi(unit + d // 2 + 1, (unit + d // 2 + 1) % 2, (unit + d // 2 + 1) // 2,
                                 "mix" if d < 6 else last_kind)
                    act.wait_ge(x_updated, base + d + 1)
                    square(n, d, d % 2)

            def even_act():
                def keep_v(r):
                    fill_ready(act, EU, r)
                    u, t = divmod(r - 15, TT)
                    act.activation(v_gate[:, t, 2 * P * u:2 * P * (u + 1)], bank[r % 4][:, 0:2 * P], ACT.Gelu_apprx_tanh)\
                        .then_inc(tok_kept_act, 1)

                def keep_u(m):
                    u_tile_ready(act, m)
                    for hf, cols in halves():
                        ins = act.activation(u_gate[:, m, cols], bank[4 + 2 * (m % 2) + hf][:, 0:HALF], ACT.Gelu_apprx_tanh)
                    ins.then_inc(u_gate_kept, 1)

                def roots(n, cols, scale):
                    act.wait_ge(stat_ready, n)
                    act.activation(stat[:, cols], stat[:, cols], ACT.Sqrt, scale=scale, bias=eps[:, 0:1]).then_inc(root_ready, 1)

                def split(i):
                    split_hi(EU + i, (EU + i) % 2, (EU + i) // 2, "mix" if i not in (6, 7) else "one")
                n_qk = TT * (NH + NKV)
                for i in (2, 3, 4):
                    split(i)
                for r in range(15, 20):
                    keep_v(r)
                roots(1, slice(0, n_qk), 1.0 / HD)
                split(5)
                for r in range(20, 25):
                    keep_v(r)
                act.wait_ge(tok_kept_act, 2 * TT)
                for t in range(TT):
                    for g in range(A_GROUPS):
                        at = n_qk + t * A_GROUPS + g
                        ins = act.activation(gate_squares[:, t * A_GROUPS + g, :], v_gate[:, t, g * P:(g + 1) * P],
                                             ACT.Square, accum_out=stat[:, at:at + 1])
                    if t == 1:
                        split(6)
                ins.then_inc(gate_stat_ready, 1)
                keep_u(0)
                keep_u(1)
                split(7)
                act.wait_ge(gate_stat_ready, 1)
                gate_stat = stat[:, n_qk:n_qk + TT * A_GROUPS]
                act.activation(gate_stat, gate_stat, ACT.Sqrt, scale=1.0 / A_DIM, bias=eps[:, 0:1]).then_inc(root_ready, 1)
                keep_u(2)
                keep_u(3)
                act.wait_ge(turned, 1)
                act.activation(spatial_t[:, :, :], bank[0][:, :].rearrange("p (g q) -> p g q", g=A_GROUPS), ACT.Copy)\
                    .then_inc(turn_kept_act, 1)
                for n in range(2, 9, 2):
                    act.wait_ge(turned, n + 1)
                    turned_out(act.activation, n, ACT.Copy).then_inc(turn_kept_act, 1)
                for g in range(A_GROUPS):
                    act.wait_ge(spatial_gated, g + 1)
                    act.activation(hid_hi[:, g, :], u_gate[:, g, :], ACT.Copy).then_inc(spatial_hi, 1)

                for i in range(N_ATT + 3):
                    if i in OUT_SPLITS:
                        split(OUT_SPLITS[i])
                    if 2 <= i <= N_ATT + 1:
                        k0, k1 = att_keys(i - 2)
                        n = (k1 - k0) * P
                        act.wait_ge(prob_turned, i - 1)
                        act.activation(prob_t[:, (i - 2) % 2, 0:n], bank2[2][:, :, :].rearrange("p a b -> p (a b)")[:, 0:n],
                                       ACT.Copy).then_inc(prob_kept, 1)
                    if i < N_ATT:
                        k0, k1 = att_keys(i)
                        n = (k1 - k0) * P
                        act.wait_ge(max_ready, i + 1)
                        if i >= PROBS:
                            act.wait_ge(prob_turned, i - PROBS + 1)
                        src = bank2[i % 2][:, 0, 0:P] if n == P else bank2[i % 2][:, :, 0:n // 2]
                        dst = prob[:, i % PROBS, 0:n] if n == P else prob[:, i % PROBS, :].rearrange("p (a b) -> p a b", a=2)
                        act.activation(dst, src, ACT.Exp, scale=HD ** -0.5, bias=soft[:, 1, i % 4:i % 4 + 1],
                                       accum_out=soft[:, 2, i % 4:i % 4 + 1]).then_inc(exp_done, 1)
                    if i >= 3 and (i - 3) % NH == NH - 1:
                        t = (i - 3) // NH
                        act.wait_ge(att_ready, t + 1)
                        act.activation(hid_hi[:, 4:8, t * P:(t + 1) * P],
                                       bank[6 + t % 2][:, :].rearrange("p (k t) -> p k t", k=4), ACT.Copy).then_inc(att_hi, 1)
                mix_squares(2, out_base(1) - KT, EU + 8, "in")
                norm(2, EU + MIX_EVEN_UNITS + 1, "in")

            def odd_act():
                def keep(f):
                    odd_tile_ready(act, f)
                    dst, func = (q_f, ACT.Copy) if f < 4 else (o_f, ACT.Sigmoid)
                    for hf, cols in halves():
                        ins = act.activation(dst[:, f % 4, cols], bank[odd_bank(f) + hf][:, 0:HALF], func)
                    ins.then_inc(tile_kept_act, 1)

                def split(i):
                    split_hi(OU + i, (OU + i) % 2, (OU + i) // 2, "mix")
                act.wait_ge(gate_w_in, 16)
                act.activation(gate_hi[:, :, :], gate_raw[:, :, :], ACT.Copy).then_inc(gate_w_hi, 1)
                keep(0)
                keep(1)
                split(2)
                keep(2)
                keep(3)
                split(3)
                act.wait_ge(gate_dve_abs, 1)
                act.activation(gate_abs[:, :, :, :], gate_abs[:, :, :, :], ACT.Exp, scale=-1.0).then_inc(gate_act, 1)
                act.wait_ge(gate_act, 1)
                act.activation(gate_abs[:, :, :, :], gate_abs[:, :, :, :], ACT.Ln, bias=ones[:, 0:1]).then_inc(gate_act, 1)
                for i in range(4, 8):
                    split(i)
                keep(8)
                keep(9)
                split(8)
                keep(10)
                keep(11)
                split(9)
                split(10)
                for n in range(0, 2 * TT, 2):
                    if n == 2 * TT - 2:
                        split(11)
                    act.wait_ge(uv_ready, n + 1)
                    act.activation(uv[:, n // 2, 0:2, :], bank[n % 4][:, :].rearrange("p (g c) -> p g c", g=2), ACT.Copy)\
                        .then_inc(uv_kept_act, 1)
                act.wait_ge(four_ready, 1)
                act.activation(hid_hi[:, 4:8, 0:T_CTX], bank[3][:, :].rearrange("p (g t) -> p g t", g=D_GROUPS), ACT.Copy,
                               scale=(T_CTX * D_DIM) ** -0.5).then_inc(four_hi, 1)
                for g in range(D_GROUPS):
                    act.activation(hid_hi[:, 4 + g, T_CTX:T], bank[4 + g][:, :], ACT.Copy, scale=(T_LAT * D_DIM) ** -0.5)\
                        .then_inc(four_hi, 1)
                act.wait_ge(m_turned, 1)
                act.activation(e_m[:, :], bank[5][:, GR:2 * GR], ACT.Exp, scale=-1.0).then_inc(e_m_ready, 1)
                def keep_inverse(n):
                    act.wait_ge(nd_ready, n + 1)
                    act.activation(h_part[:, :], bank[3][:, :], ACT.Copy).then_inc(inverse_kept, 1)

                def weights(n):
                    t, d = GROUPS[n]
                    c = n % 2
                    act.wait_ge(x_ready, n + 1)
                    if n >= 2:
                        act.wait_ge(a_ready, n - 1)
                        if n - 2 in STATE_GROUPS:
                            act.wait_ge(st_taken, n - 1)
                    act.activation(w_intra[:, c, :, :], w_intra[:, c, :, :], ACT.Exp, scale=-1.0)
                    for h in range(CH):
                        r = row_of(t, d, h)
                        ins = act.activation(w_prev[:, c, h, :], bank[c][:, h * P:(h + 1) * P], ACT.Exp, scale=-1.0,
                                             bias=m_start[:, r:r + 1])
                    ins.then_inc(exps_done, 1)

                weights(0)
                weights(1)
                for n in range(NG):
                    keep_inverse(n)
                    if n + 2 < NG:
                        weights(n + 2)
                act.wait_ge(state_stored, 16 * 4)
                for h in range(CH):
                    act.wait_ge(h_final, h + 1)
                    act.activation(hid_hi[:, h, :], h_sum[:, h, :], ACT.Copy).then_inc(c_hi, 1)
                mix_squares(5, out_base(3) - KT, OU + 10, "in")
                norm(5, OU + MIX_ODD_UNITS + 1, "in")

            act.wait_ge(rows_kept, 1)
            act.activation(silu_c[:, :, :].rearrange("p k v -> p v k"),
                           rows_t[:, 0:2 * KT].rearrange("p (v k) -> p v k", v=2), ACT.Silu).then_inc(silu_ready, 1)
            for n in range(0, 2 * TT, 2):
                act.wait_ge(x_turned, n + 1)
                act.activation(x[:, 0:4, n // 2 * P:(n // 2 + 1) * P],
                               bank[n % 4][:, :].rearrange("p (k t) -> p k t", k=4), ACT.Copy).then_inc(x_kept_act, 1)
            act.wait_ge(x_kept_dve, TT)
            act.wait_ge(x_kept_act, TT)
            for d in range(KT):
                square(0, d, d % 2)
            split_hi(0, 0, 0, "in")
            norm(0, 1, "in")
            ffn(0, (1, "mix"))
            even_act()
            ffn(1, (norm_at[2], "in"))
            ffn(2, (norm_at[2] + 1, "mix"))
            odd_act()
            ffn(3, (None, None))
            for n in range(0, 2 * TT, 2):
                act.wait_ge(y_turned, n + 1)
                act.activation(y_rows[:, n // 2, 0:4 * P], bank[n % 4 + 4][:, :], ACT.Copy).then_inc(y_kept_act, 1)

        @block.vector
        def _(dve):
            chain = Count(dve, dve_chain)

            def split_lo(u, slot, kind):
                dve.wait_ge(hi_ready, u + 1)
                dve.tensor_tensor(split_view(w_lo, kind, slot), raw_view(kind, slot),
                                  split_view(w_hi, kind, slot).bitcast(F32), ALU.subtract).then_inc(lo_ready, 1)

            def product(f, s, i, c):
                dve.wait_ge(silu_done, 22 * f + i + 1)
                dve.wait_ge(w_used, FFN_AT[f] + s + 1)
                for hf, cols in halves():
                    ins = dve.tensor_tensor(work_b[:, c, cols], work_a[:, c, cols], bank[2 + hf][:, 0:HALF], ALU.mult)
                ins.then_inc(prod_done, 1)

            def hidden_lo(f, i, c, k):
                dve.wait_ge(hid_hi_done, 22 * f + i + 1)
                dve.wait_ge(prod_done, 22 * f + i + 1)
                dve.tensor_tensor(hid_lo[:, k, :], work_b[:, c, :], hid_hi[:, k, :].bitcast(F32), ALU.subtract)\
                    .then_inc(hid_lo_done, 1)

            def update_x(unit, layer, j, d, c):
                if unit is not None:
                    dve.wait_ge(w_used, unit + 1)
                for hf, v, cols, in_bank in PIECES:
                    xs = x[:, d, cols]
                    ins = dve.scalar_tensor_tensor(out=xs, in0=bank[2 * c + hf][:, in_bank],
                                                   scalar=mod_col(v, layer, 3 * j + 2, d), in1=xs,
                                                   op0=ALU.mult, op1=ALU.add)
                ins.then_inc(x_updated, 1)

            def sum_mod(b, kts):
                if kts[0] == 0:
                    dve.wait_ge(mod_in, 16 * (b + 1))
                for kt in kts:
                    for v in range(2):
                        sc = silu_c[:, kt, v:v + 1]
                        if kt == 0:
                            chain.inc(dve.tensor_scalar(mod_acc[:, v, :], mod_raw[:, kt, :], sc, None, ALU.mult))
                        else:
                            chain.wait(back=1)
                            ins = dve.scalar_tensor_tensor(out=mod_acc[:, v, :], in0=mod_raw[:, kt, :], scalar=sc,
                                                           in1=mod_acc[:, v, :], op0=ALU.mult, op1=ALU.add)
                            if kt == KT - 1 and v == 1:
                                ins.then_inc(mod_summed, 1)
                            else:
                                chain.inc(ins)

            def keep_mod(sums, cols, n):

                def partial(v):
                    return mod_tmp[:, v, 0:n] if n <= MOD_TILES else work_b[:, v, 0:n]
                for v in range(2):
                    chain.inc(dve.tensor_tensor(partial(v), sums[:, :, v], mod_add[:, cols], ALU.add))
                chain.wait()
                for v in range(2):
                    chain.inc(dve.tensor_tensor(mod[:, v, cols], partial(v), mod_mul[:, cols], ALU.mult))
                chain.wait()

            def keep_block(b):
                dve.wait_ge(mod_turned, b + 1)
                keep_mod(bank[MODB][:, 0:2 * MOD_TILES].rearrange("p (m v) -> p m v", v=2),
                         bass.ts(b + MOD_PE_BLOCKS, MOD_TILES), MOD_TILES)

            def invert(n):
                dve.wait_ge(rms_ready, n + 1)
                dve.reciprocal(rms[:, :], rms[:, :]).then_inc(inverse_ready, 1)

            def norm(n, unit, kind):
                l, j = divmod(n, N_SUB)
                if n > 0:
                    invert(n)
                dve.wait_ge(inverse_spread, n + 1)

                def low(kt):
                    dve.wait_ge(h_hi_ready, KT * n + kt + 1)
                    for v, cols in PARTS:
                        ins = dve.scalar_tensor_tensor(out=h_lo[:, kt, cols], in0=scaled(kt)[:, cols],
                                                       scalar=mod_col(v, l, 3 * j, kt),
                                                       in1=h_hi[:, kt, cols].bitcast(F32), op0=ALU.add, op1=ALU.subtract)
                    ins.then_inc(h_lo_ready, 1)
                for kt in range(KT):
                    if kt >= 4:
                        dve.wait_ge(h_lo_ready, KT * n + kt - 3)
                    for v, cols in PARTS:
                        ins = dve.scalar_tensor_tensor(out=scaled(kt)[:, cols], in0=x[:, kt, cols],
                                                       scalar=mod_col(v, l, 3 * j + 1, kt), in1=rms_inverse[:, cols],
                                                       op0=ALU.mult, op1=ALU.mult)
                    ins.then_inc(scaled_ready, 1)
                    if kt >= 1:
                        low(kt - 1)
                    if kt == KT - 2:
                        split_lo(unit, 1, kind)
                low(KT - 1)
                clear_ss()

            def clear_ss():
                chain.inc(dve.memset(ss[:, :], 0.0))

            def add_sq(n, d, c):
                dve.wait_ge(squared, KT * n + d + 1)
                if isinstance(d, int) and d == 0:
                    chain.wait()
                else:
                    dve.wait_ge(square_added, KT * n + d)
                dve.tensor_tensor(ss[:, :], ss[:, :], work_a[:, c, :], ALU.add).then_inc(square_added, 1)

            def ffn(f, after):
                U, (l, h) = FFN_AT[f], divmod(f, 2)

                def run(phase, first, last, body):
                    turns = (last - first) // 2
                    per = 4 + 2 * KT - 1 if phase in MOD_PHASES[f] else 0
                    start = chain.base + chain.n
                    with dve.Fori(0, turns) as t:
                        chain.base, chain.n = start + t * per, 0
                        for slot in range(2):
                            s = first + 2 * t + slot
                            body(s, slot)
                            if phase in MOD_PHASES[f]:
                                b = t + MOD_PHASES[f][phase]
                                if slot == 0:
                                    sum_mod(b, range(KT // 2, KT))
                                else:
                                    keep_block(b)
                                    sum_mod(b + 1, range(KT // 2))
                        assert chain.n == per, (chain.n, per)
                    chain.base, chain.n = start + turns * per, 0

                def in_step(shift):
                    def body(s, slot):
                        product(f, s - 2, s - 2 + shift[0], slot)
                        split_lo(U + s, slot, "in")
                        hidden_lo(f, s - 2 + shift[0], slot, s - 2 - shift[1])
                    return body

                def out_step(kind, origin, chunk):
                    def body(s, slot):
                        d = s - 2 - origin
                        update_x(U + s - 2, l, 2 * h, d, slot)
                        split_lo(U + s, slot, kind)
                        if chunk == 1 and after[0] is not None:
                            add_in_loop(after[0], d, slot)
                    return body

                def add_in_loop(n, d, c):
                    dve.wait_ge(squared, KT * n + d + 1)
                    dve.wait_ge(square_added, KT * n + d)
                    dve.tensor_tensor(ss[:, :], ss[:, :], work_a[:, c, :], ALU.add).then_inc(square_added, 1)

                if f == 1:
                    keep_block(L1_BLOCK - 1)
                    sum_mod(L1_BLOCK, range(KT // 2))
                run(0, 2, A_IN, in_step((0, 0)))
                for s in range(A_IN, A_IN + 2):
                    product(f, s - 2, s - 2, s % 2)
                    split_lo(U + s, s % 2, "outA")
                    hidden_lo(f, s - 2, s % 2, s - 2)
                    if f == 2 and s == A_IN:
                        sum_mod(MOD_BLOCKS - 1, range(KT // 2, KT))
                    elif f == 2:
                        keep_block(MOD_BLOCKS - 1)
                run(1, A_IN + 2, A_OUT, out_step("outA", A_IN, 0))
                for s in range(A_OUT, A_OUT + 2):
                    update_x(U + s - 2, l, 2 * h, s - 2 - A_IN, s % 2)
                    split_lo(U + s, s % 2, "in")
                run(2, A_OUT + 2, B_OUT, in_step((A_IN - A_OUT, A_OUT)))
                for s in range(B_OUT, B_OUT + 2):
                    product(f, s - 2, s - 2 - A_OUT + A_IN, s % 2)
                    split_lo(U + s, s % 2, "outB")
                    hidden_lo(f, s - 2 - A_OUT + A_IN, s % 2, s - 2 - A_OUT)
                    if f == 0 and s == B_OUT:
                        sum_mod(L1_BLOCK - 2, range(KT // 2, KT))
                    elif f == 0:
                        keep_block(L1_BLOCK - 2)
                        sum_mod(L1_BLOCK - 1, range(KT))
                chain.wait()
                run(3, B_OUT + 2, FFN_UNITS, out_step("outB", B_OUT, 1))
                for d in range(KT - 2, KT):
                    update_x(U + B_OUT + d, l, 2 * h, d, d % 2)
                    if d == KT - 2 and after[1] is not None:
                        split_lo(U + FFN_UNITS, 0, after[1])
                    if after[0] is not None:
                        add_in_loop(after[0], d, d % 2)
                if after[0] is not None:
                    norm(after[0], U + FFN_UNITS + 1, after[1])

            def do(ins):
                chain.inc(ins)
                chain.wait()

            def mix_updates(n, layer, unit, last_kind):
                for d in range(KT):
                    if d % 2 == 0 and d >= 2:
                        split_lo(unit + d // 2 + 1, (unit + d // 2 + 1) % 2, "mix" if d < 6 else last_kind)
                    if d % 2 == 0:
                        dve.wait_ge(out_ready, 4 * layer + d // 2 + 1)
                        update_x(None, layer, 1, d, 0)
                    else:
                        update_x(unit + d // 2, layer, 1, d, 1)
                    add_sq(n, d, d % 2)

            def even_dve():
                n_qk = TT * (NH + NKV)

                def keep(r):
                    fill_ready(dve, EU, r)
                    u, t = divmod(r, TT)
                    src = bank[r % 4]
                    if u == 0:
                        kt_ = 0 if t == 0 else t + 1
                        dve.tensor_copy(k_tok[:, kt_, :, 0, :], src[:, 0:P].rearrange("p (g d) -> p g d", g=NKV))
                        ins = dve.tensor_copy(v_tok[:, kt_, :], src[:, P:2 * P])
                    else:
                        ins = dve.tensor_copy(q_tok[:, t, (u - 1) * 2 * P:u * 2 * P], src[:, 0:2 * P])
                    ins.then_inc(tok_kept_dve, 1)

                def split(i):
                    split_lo(EU + i, (EU + i) % 2, "mix" if i not in (6, 7) else "one")

                def q_heads(t):
                    return q_tok[:, t, :].rearrange("p (h d) -> p h d", d=HD)

                def k_heads(t):
                    return k_tok[:, 0 if t == 0 else t + 1, :, 0, :]

                def scratch(n):
                    return rot[:, 0:n * HD].rearrange("p (h d) -> p h d", d=HD)

                def squares_of(src, n, at):
                    do(dve.tensor_tensor(scratch(n), src, src, ALU.mult))
                    return dve.tensor_reduce(stat[:, at:at + n], scratch(n), AX.X, ALU.add)

                def apply(src, n, at, gain, t):
                    do(dve.tensor_tensor(src, src, stat[:, at:at + n].unsqueeze(2).to_broadcast([P, n, HD]), ALU.mult))
                    ins = dve.tensor_tensor(src, src, qk_gain[:, gain, :].unsqueeze(1).to_broadcast([P, n, HD]), ALU.mult)
                    if t > 0:
                        do(ins)
                        turn, half = scratch(n), HD // 2
                        cos, sin = (rope[:, i, t - 1, :].unsqueeze(1).to_broadcast([P, n, HD]) for i in range(2))
                        chain.inc(dve.tensor_tensor(turn[:, :, 0:half], src[:, :, half:HD], sin[:, :, 0:half], ALU.mult))
                        do(dve.tensor_tensor(turn[:, :, half:HD], src[:, :, 0:half], sin[:, :, half:HD], ALU.mult))
                        do(dve.tensor_tensor(src, src, cos, ALU.mult))
                        ins = dve.tensor_tensor(src, src, turn, ALU.add)
                    return ins

                for r in range(5):
                    keep(r)
                split(2)
                for r in range(5, 10):
                    keep(r)
                split(3)
                for r in range(10, 15):
                    keep(r)
                split(4)
                dve.wait_ge(tok_kept_dve, 15)
                for t in range(TT):
                    do(squares_of(q_heads(t), NH, t * NH))
                    last = squares_of(k_heads(t), NKV, TT * NH + t * NKV)
                    if t < TT - 1:
                        do(last)
                last.then_inc(stat_ready, 1)
                split(5)
                dve.wait_ge(root_ready, 1)
                do(dve.reciprocal(stat[:, 0:n_qk], stat[:, 0:n_qk]))
                dve.wait_ge(tok_in, 16 * 7)
                for t in range(TT):
                    do(apply(k_heads(t), NKV, TT * NH + t * NKV, 1, t))
                dve.tensor_copy(k_tok[:, :, :, 1, :], k_tok[:, :, :, 0, :]).then_inc(qk_done, 1)
                for t in range(TT):
                    if t == 2:
                        split(6)
                    last = apply(q_heads(t), NH, t * NH, 0, t)
                    if t < TT - 1:
                        do(last)
                last.then_inc(qk_done, 1)
                split(7)
                dve.wait_ge(root_ready, 2)
                gate_stat = stat[:, n_qk:n_qk + TT * A_GROUPS]
                do(dve.reciprocal(gate_stat, gate_stat))
                for t in range(TT):
                    src = v_gate[:, t, :].rearrange("p (g c) -> p g c", g=A_GROUPS)
                    scale = gate_stat[:, t * A_GROUPS:(t + 1) * A_GROUPS].unsqueeze(2).to_broadcast([P, A_GROUPS, A_DIM])
                    ins = dve.tensor_tensor(src, src, scale, ALU.mult)
                ins.then_inc(qk_done, 1)
                for n in range(1, 9, 2):
                    dve.wait_ge(turned, n + 1)
                    turned_out(dve.tensor_copy, n).then_inc(turn_kept_dve, 1)

                for g in range(A_GROUPS):
                    dve.wait_ge(spatial_ready, g + 1)
                    dve.wait_ge(u_gate_kept, g + 1)
                    if g >= 1:
                        dve.wait_ge(spatial_gated, g)
                    flat = bank2[g][:, :, :].rearrange("p a b -> p (a b)")[:, 0:T].rearrange("p (t q) -> p t q", q=P)
                    sg = rot[:, :].rearrange("p (t q) -> p t q", q=P)
                    do(dve.scalar_tensor_tensor(out=sg, in0=flat, scalar=rows_t[:, 64 + g:65 + g],
                                                in1=spatial_bias[:, g, :].unsqueeze(1).to_broadcast([P, TT, P]),
                                                op0=ALU.mult, op1=ALU.add))
                    dve.tensor_tensor(u_gate[:, g, :], u_gate[:, g, :], rot[:, :], ALU.mult).then_inc(spatial_gated, 1)
                for i in range(N_ATT + 4):
                    if 1 <= i <= A_GROUPS:
                        dve.wait_ge(spatial_hi, i)
                        dve.tensor_tensor(hid_lo[:, i - 1, :], u_gate[:, i - 1, :], hid_hi[:, i - 1, :].bitcast(F32),
                                          ALU.subtract).then_inc(mix_done, 1)
                    if i - 1 in OUT_SPLITS:
                        split(OUT_SPLITS[i - 1])
                    if i < N_ATT:
                        k0, k1 = att_keys(i)
                        n = (k1 - k0) * P
                        dve.wait_ge(scores_ready, i + 1)
                        src = bank2[i % 2][:, 0, 0:P] if n == P else bank2[i % 2][:, :, 0:n // 2]
                        do(dve.tensor_reduce(soft[:, 0, i % 4:i % 4 + 1], src, AX.X if n == P else AX.XY, ALU.max))
                        dve.tensor_scalar(soft[:, 1, i % 4:i % 4 + 1], soft[:, 0, i % 4:i % 4 + 1], -HD ** -0.5, None,
                                          ALU.mult).then_inc(max_ready, 1)
                    if 1 <= i <= N_ATT:
                        k0, k1 = att_keys(i - 1)
                        n, c = (k1 - k0) * P, (i - 1) % 4
                        dve.wait_ge(exp_done, i)
                        do(dve.reciprocal(soft[:, 2, c:c + 1], soft[:, 2, c:c + 1]))
                        dve.tensor_scalar(prob[:, (i - 1) % PROBS, 0:n], prob[:, (i - 1) % PROBS, 0:n], soft[:, 2, c:c + 1], None,
                                          ALU.mult).then_inc(prob_ready, 1)
                    if i >= 4 and (i - 4) % NH == NH - 1:
                        t = (i - 4) // NH
                        cols = slice(t * P, (t + 1) * P)
                        dve.wait_ge(att_hi, t + 1)
                        dve.tensor_tensor(hid_lo[:, 4:8, cols], bank[6 + t % 2][:, :].rearrange("p (k t) -> p k t", k=4),
                                          hid_hi[:, 4:8, cols].bitcast(F32), ALU.subtract).then_inc(mix_done, 1)
                mix_updates(2, 0, EU + 8, "in")
                norm(2, EU + MIX_EVEN_UNITS + 1, "in")

            def odd_dve():
                def split(i):
                    split_lo(OU + i, (OU + i) % 2, "mix")

                def keep(f):
                    odd_tile_ready(dve, f)
                    dst, scale = (k_f, DK ** -0.5) if f < 8 else (d_f, 1.0)
                    for hf, cols in halves():
                        ins = dve.tensor_scalar(dst[:, f % 4, cols], bank[odd_bank(f) + hf][:, 0:HALF], scale, None, ALU.mult)
                    ins.then_inc(tile_kept_dve, 1)

                def keep_v(r):
                    fill_ready(dve, OU + 4, r)
                    u, t = divmod(r, TT)
                    dve.tensor_copy(v_t[:, t, 2 * P * u:2 * P * (u + 1)], bank[r % 4][:, 0:2 * P]).then_inc(tok_kept_dve, 1)

                gate_v = gates[:, :, :].rearrange("p t (d k h) -> p t d k h", d=2, k=2)

                def per_dir(tile, d):
                    return tile[:, 32 * d:32 * d + TT * CH].rearrange("p (t h) -> p t h", h=CH)

                dve.wait_ge(gate_w_hi, 1)
                dve.tensor_tensor(gate_lo[:, :, :], gate_raw[:, :, :], gate_hi[:, :, :].bitcast(F32), ALU.subtract)\
                    .then_inc(gate_dve, 1)
                chain.inc(dve.memset(log_f[:, :], 0.0))
                chain.inc(dve.memset(ab[:, :, :], 0.0))
                chain.inc(dve.memset(m_start[:, :], 0.0))
                split(2)
                split(3)
                dve.wait_ge(gate_pe, 1)
                dve.wait_ge(odd_in, 16 * 5)
                do(dve.tensor_tensor(gates[:, :, :], bank[0][:, 0:16 * TT].rearrange("p (t c) -> p t c", c=16),
                                     gate_bias[:, :].unsqueeze(1).to_broadcast([P, TT, 16]), ALU.add))
                for d in range(2):
                    f = gate_v[:, :, d, 1, :]
                    ins = dve.scalar_tensor_tensor(out=gate_abs[:, :, d, :], in0=f, scalar=-1.0, in1=f, op0=ALU.mult, op1=ALU.max)
                ins.then_inc(gate_dve_abs, 1)
                dve.wait_ge(gate_act, 2)
                for d in range(2):
                    ins = dve.scalar_tensor_tensor(out=per_dir(log_f, d), in0=gate_v[:, :, d, 1, :], scalar=0.0,
                                                   in1=gate_abs[:, :, d, :], op0=ALU.min, op1=ALU.subtract)
                ins.then_inc(gate_dve, 1)
                keep(4)
                keep(5)
                split(4)
                keep(6)
                keep(7)
                split(5)
                dve.wait_ge(gate_pe, 2)
                for d in range(2):
                    b = bank[3][:, 32 * d:32 * d + TT * CH].rearrange("p (t h) -> p t h", h=CH)
                    chain.inc(dve.tensor_tensor(per_dir(ab[:, 0, :], d), gate_v[:, :, d, 0, :], b, ALU.subtract))
                    chain.inc(dve.tensor_copy(per_dir(ab[:, 1, :], d), b))
                dve.tensor_copy(log_f[:, :], bank[3][:, GR:2 * GR]).then_inc(gate_dve, 1)
                for r in range(5):
                    keep_v(r)
                split(6)
                for r in range(5, 10):
                    keep_v(r)
                split(7)
                dve.wait_ge(gate_pe, 3)
                do(dve.tensor_copy(a_rows[:, :], bank[0][0:GR, 0:P]))
                chain.inc(dve.tensor_copy(b_rows[:, :], bank[0][0:GR, P:2 * P]))
                chain.inc(dve.tensor_tensor_scan(c_rows[0:32, :], a_rows[0:32, :], a_rows[0:32, :], -1e30, ALU.max, ALU.max))
                chain.inc(dve.tensor_tensor_scan(c_rows[32:GR, ::-1], a_rows[32:GR, ::-1], a_rows[32:GR, ::-1], -1e30,
                                                 ALU.max, ALU.max))
                chain.wait()
                chain.inc(dve.tensor_copy(a_max[0:32, :], c_rows[0:32, P - 1:P].to_broadcast([32, P])))
                dve.tensor_copy(a_max[32:GR, :], c_rows[32:GR, 0:1].to_broadcast([32, P])).then_inc(gate_dve, 1)
                split(8)
                dve.wait_ge(gate_pe, 4)
                a_top = bank[1]
                for d in range(2):
                    start = TT - 1 if d else 1
                    do(dve.tensor_copy(col_view(m_start, d, start), m_given[:, d, :]))
                    order = [start + (-i if d else i) for i in range(TT - 1)]
                    for t, nxt in [(0, None)] + list(zip(order[:-1], order[1:])):
                        top = gate_abs[:, 0, 0, :]
                        do(dve.tensor_tensor(top, col_view(m_start, d, t), col_view(a_top, d, t), ALU.max))
                        dst = m_end[:, d, :] if nxt is None else col_view(m_start, d, nxt)
                        do(dve.tensor_tensor(dst, top, col_view(log_f, d, t), ALU.add))
                dve.tensor_copy(gate_abs[:, 1, 0, :], gate_abs[:, 0, 0, :]).then_inc(gate_dve, 1)
                split(9)
                keep(12)
                keep(13)
                dve.wait_ge(gate_pe, 5)
                do(dve.tensor_tensor(m_rows[:, 0, :], c_rows[:, :], bank[2][0:GR, 0:P], ALU.max))
                dve.tensor_tensor(m_rows[:, 1, :], m_rows[:, 0, :], b_rows[:, :], ALU.add).then_inc(gate_dve, 1)
                split(10)
                keep(14)
                keep(15)
                for n in range(1, 2 * TT, 2):
                    if n == 2 * TT - 1:
                        split(11)
                    dve.wait_ge(uv_ready, n + 1)
                    dve.tensor_copy(uv[:, n // 2, 2:4, :], bank[n % 4][:, :].rearrange("p (g c) -> p g c", g=2))\
                        .then_inc(uv_kept_dve, 1)
                pieces = [(bank[3][:, :].rearrange("p (g t) -> p g t", g=D_GROUPS), slice(4, 8), slice(0, T_CTX), T_CTX)]
                pieces += [(bank[4 + g][:, :], 4 + g, slice(T_CTX, T), T_LAT) for g in range(D_GROUPS)]
                for n, (src, tiles, cols, length) in enumerate(pieces):
                    dve.wait_ge(four_hi, n + 1)
                    dve.scalar_tensor_tensor(out=hid_lo[:, tiles, cols], in0=src, scalar=(length * D_DIM) ** -0.5,
                                             in1=hid_hi[:, tiles, cols].bitcast(F32), op0=ALU.mult, op1=ALU.subtract)\
                        .then_inc(four_lo, 1)
                for n in range(TT + 2):
                    dve.wait_ge(k_turned, n + 1)
                    src = bank[n % 4][:, :]
                    if n < TT:
                        dve.tensor_copy(k_t[:, n, :], src).then_inc(k_kept, 1)
                    else:
                        dve.tensor_copy(state[:, n - TT, :, 0:P], src.rearrange("p (h k) -> p h k", h=CH)).then_inc(k_kept, 1)
                dve.tensor_copy(state[:, :, :, P:P + 1], n_col[:, :, :].unsqueeze(3))\
                    .then_inc(state_kept, 1)

                def exponents(n):
                    t, d = GROUPS[n]
                    dve.wait_ge(bcast_ready, n + 1)
                    if n >= 2:
                        dve.wait_ge(a_ready, n - 1)
                        if n - 2 in STATE_GROUPS:
                            dve.wait_ge(v_ready, n - 1)
                    for h in range(CH):
                        r = row_of(t, d, h)
                        ins = dve.scalar_tensor_tensor(out=w_intra[:, n % 2, h, :], in0=bank[n % 2][:, h * P:(h + 1) * P],
                                                       scalar=ab[:, 0, r:r + 1], in1=masks[:, d, :],
                                                       op0=ALU.subtract, op1=ALU.add)
                    ins.then_inc(x_ready, 1)

                def weigh(n):
                    t, d = GROUPS[n]
                    c = n % 2
                    last = P - 1 if d == 0 else 0
                    dve.wait_ge(exps_done, n + 1)
                    if n >= 2:
                        dve.wait_ge(nd_ready, n - 1)
                    dve.tensor_tensor(q_w[:, c, :, :], q_f[:, :, t * P:(t + 1) * P], w_prev[:, c, :, :], ALU.mult)
                    dve.wait_ge(qk_ready, n + 1)
                    dve.tensor_tensor(a_t[:, c, :], w_intra[:, c, :, :].rearrange("p h t -> p (h t)"), bank[4][:, :], ALU.mult)\
                        .then_inc(a_ready, 1)
                    if n in STATE_GROUPS:
                        if n >= 2:
                            dve.wait_ge(st_ready, n - 1)
                        for h in range(CH):
                            w_s = w_intra[:, c, h, last:last + 1]
                            dve.tensor_scalar(v_w[:, c, h, 0:P], v_t[:, t, h * P:(h + 1) * P], w_s, None, ALU.mult)
                        dve.tensor_copy(v_w[:, c, :, P:P + 1], w_intra[:, c, :, last:last + 1]).then_inc(v_ready, 1)

                def invert_den(n):
                    t, d = GROUPS[n]
                    dve.wait_ge(den_ready, n + 1)
                    if n == 0:
                        dve.wait_ge(e_m_ready, 1)
                    raw = bank[5][:, 0:CH]
                    do(dve.scalar_tensor_tensor(out=den[:, :], in0=raw, scalar=-1.0, in1=col_view(e_m, d, t),
                                                op0=ALU.mult, op1=ALU.max))
                    do(dve.tensor_tensor(den[:, :], den[:, :], raw, ALU.max))
                    dve.reciprocal(den[:, :], den[:, :]).then_inc(den_inverted, 1)

                def finish(n):
                    t, d = GROUPS[n]
                    c = n % 2
                    dve.wait_ge(inverse_kept, n + 1)
                    hs = h_sum[:, :, t * P:(t + 1) * P]
                    part, num = (view.rearrange("p (h t) -> p h t", h=CH) for view in (h_part[:, :], bank[2][:, :]))
                    if SEEN[n]:
                        do(dve.tensor_tensor(part, part, num, ALU.mult))
                        dve.tensor_tensor(hs, hs, part, ALU.add).then_inc(h_done, 1)
                    else:
                        dve.tensor_tensor(hs, part, num, ALU.mult).then_inc(h_done, 1)
                    dve.wait_ge(h_done, n + 1)
                    if n not in STATE_GROUPS:
                        return
                    dve.wait_ge(st_ready, n + 1)
                    if t == 0:
                        chain.inc(dve.tensor_copy(c_end[d][:, :, :], bank[6][:, :].rearrange("p (h k) -> p h k", h=CH)))
                        chain.inc(dve.tensor_copy(n_end[:, d, :], bank[7][:, 0:CH]))
                        chain.wait()
                        dve.sem_inc(end_kept, 1)
                        dve.sem_inc(st_taken, 1)
                    else:
                        last = P - 1 if d == 0 else 0
                        for h in range(CH):
                            ins = dve.scalar_tensor_tensor(out=state[:, d, h, :], in0=state[:, d, h, :],
                                                           scalar=w_prev[:, c, h, last:last + 1],
                                                           in1=bank[6 + h // 2][:, h % 2 * 2 * P:h % 2 * 2 * P + P + 1],
                                                           op0=ALU.mult, op1=ALU.add)
                        ins.then_inc(st_taken, 1)

                exponents(0)
                exponents(1)
                weigh(0)
                for n in range(NG):
                    if n + 1 < NG:
                        weigh(n + 1)
                    invert_den(n)
                    if n + 2 < NG:
                        exponents(n + 2)
                    finish(n)
                dve.wait_ge(h_done, NG)
                for step in range(CH + 1):
                    if step < CH:
                        dve.tensor_tensor(h_sum[:, step, :], h_sum[:, step, :], o_f[:, step, :], ALU.mult).then_inc(h_final, 1)
                    if step >= 1:
                        h = step - 1
                        dve.wait_ge(c_hi, h + 1)
                        dve.tensor_tensor(hid_lo[:, h, :], h_sum[:, h, :], hid_hi[:, h, :].bitcast(F32), ALU.subtract)\
                            .then_inc(c_lo, 1)
                mix_updates(5, 1, OU + 10, "in")
                norm(5, OU + MIX_ODD_UNITS + 1, "in")

            dve.memset(eps[:, :], EPS)
            dve.memset(ones[:, :], 1.0)
            chain.inc(dve.memset(mod_mul[:, :], 1.0))
            clear_ss()
            dve.wait_ge(rows_turned, 1)
            for l in range(DEPTH):
                chain.inc(dve.tensor_copy(mod_add[:, l * 72:(l + 1) * 72], bank[5][:, l * P:l * P + 72]))
            dve.tensor_copy(rows_t[:, :], bank[5][:, 2 * P:2 * P + 72]).then_inc(rows_kept, 1)
            dve.wait_ge(rows_kept, 1)
            chain.wait()
            add_v = mod_add[:, :].rearrange("p (s k c) -> p s k c", s=DEPTH * N_SUB, k=3)
            mul_v = mod_mul[:, :].rearrange("p (l j k c) -> p l j k c", l=DEPTH, j=N_SUB, k=3)
            mul_s = mod_mul[:, :].rearrange("p (s k c) -> p s k c", s=DEPTH * N_SUB, k=3)
            chain.inc(dve.tensor_scalar(add_v[:, :, 1, :], add_v[:, :, 1, :], 1.0, None, ALU.add))
            for j in (0, 2):
                chain.inc(dve.memset(mul_v[:, :, j, 2, :], 0.5))
            chain.inc(dve.tensor_copy(mul_s[:, :, 1, :], rows_t[:, 2 * KT:8 * KT].rearrange("p (s c) -> p s c", c=KT)))
            for n in range(1, 2 * TT, 2):
                dve.wait_ge(x_turned, n + 1)
                dve.tensor_copy(x[:, 4:8, n // 2 * P:(n // 2 + 1) * P],
                                bank[n % 4][:, :].rearrange("p (k t) -> p k t", k=4)).then_inc(x_kept_dve, 1)
            for d in range(KT):
                add_sq(0, d, d % 2)
            split_lo(0, 0, "in")
            invert(0)
            sum_mod(0, range(KT))
            dve.wait_ge(mod_first_sum, 1)
            n_first = MOD_PE_BLOCKS * MOD_TILES
            keep_mod(bank[5][:, 0:2 * n_first].rearrange("p (m v) -> p m v", v=2), slice(0, n_first), n_first)
            keep_block(0)
            norm(0, 1, "in")
            sum_mod(1, range(KT // 2))
            ffn(0, (1, "mix"))
            even_dve()
            ffn(1, (norm_at[2], "in"))
            ffn(2, (norm_at[2] + 1, "mix"))
            odd_dve()
            ffn(3, (None, None))
            for n in range(1, 2 * TT, 2):
                dve.wait_ge(y_turned, n + 1)
                dve.tensor_copy(y_rows[:, n // 2, 4 * P:8 * P], bank[n % 4 + 4][:, :]).then_inc(y_kept_dve, 1)


def constants():
    pos = np.arange(T_LAT)
    n_freq = HEAD_DIM // 4
    inv = np.float32(ROPE_THETA) ** (-np.arange(n_freq, dtype=np.float32) / np.float32(n_freq))
    ang = np.concatenate([(pos // GRID_W).astype(np.float32)[:, None] * inv,
                          (pos % GRID_W).astype(np.float32)[:, None] * inv], axis=-1)
    sin = np.sin(ang)
    rope = np.stack([np.concatenate([np.cos(ang)] * 2, axis=-1), np.concatenate([-sin, sin], axis=-1)])
    k = np.arange(P)
    ang_c = 2 * np.pi * (k[:, None] * k % P) / P
    n = np.arange(T_LAT)
    ang_t = 2 * np.pi * (n[:, None] * n % T_LAT) / T_LAT
    after = (k[:, None] > k[None, :]).astype(np.float32)
    return {"dft_c": np.stack([np.cos(ang_c), -np.sin(ang_c), np.sin(ang_c)]).astype(np.float32),
            "dft_t": np.stack([np.cos(ang_t), np.sin(ang_t)]).astype(np.float32),
            "masks": np.stack([after * np.float32(1e30), after.T * np.float32(1e30), 1 - after, 1 - after.T]).astype(np.float32),
            "identity": np.eye(P, dtype=np.float32), "rope": rope.astype(np.float32)}


_INS = ["x_prompt", "x_sample", "c", "cache_k", "cache_v", "state_C", "state_n", "state_m", "c_ctx", "norm_gain", "w_mod",
        "b_mod", "ffn_w_in", "ffn_w_out", "w_in_even", "w_out_even", "spatial_w", "spatial_b", "sgu_gain", "q_gain",
        "k_gain", "w_in_odd", "b_gate_odd", "w_out_odd"]
_OUTS = [("y_prompt", (1, T_CTX, D)), ("y_sample", (1, T_LAT, D)),
         ("new_cache_k", (1, 1, T_CTX, B_KV, HEAD_DIM)), ("new_cache_v", (1, 1, T_CTX, B_KV, HEAD_DIM)),
         ("new_state_C", (1, 1, 2, 4, P, P)), ("new_state_n", (1, 1, 2, 4, P)), ("new_state_m", (1, 1, 2, 4))]


def kernel(**inputs):
    import concourse.bacc as bacc
    from concourse.bass_utils import run_bass_kernel_spmd

    nc = bacc.Bacc("TRN2", target_bir_lowering=False, num_devices=1)
    arrays = {name: np.ascontiguousarray(inputs[name]) for name in _INS}
    arrays.update(constants())
    given = {name: nc.dram_tensor(name, v.shape, mybir.dt.from_np(v.dtype), kind="ExternalInput").ap()
             for name, v in arrays.items()}
    out = {name: nc.dram_tensor("out_" + name, shape, F32, kind="ExternalOutput").ap() for name, shape in _OUTS}
    trunk(nc, given, out)
    r = run_bass_kernel_spmd(nc, [arrays], core_ids=[0])
    return tuple(r.results[0]["out_" + name] for name, _ in _OUTS)
```
